# Optimizing a Trainium2 kernel written in Bass

```python
import jax, jax.numpy as jnp
from jax import lax
import numpy as np

D_MODEL = 1024
BATCH = 1
SEQ = 256
DEPTH = 1
DEC_BATCH = 8
DEC_SEQ = 16
PAST_LEN = 512

CHUNK = 64
EPS = 1e-6
DN_HEADS = 4
DN_HEAD_DIM = 128
DN_WIDTH = DN_HEADS * DN_HEAD_DIM
DN_CONV = 4
SC_WIDTH = 256
SC_CONV = 3
MEM_LEN = 256
MEM_HEADS = 4
MEM_HEAD_DIM = 64
MEM_WIDTH = MEM_HEADS * MEM_HEAD_DIM
MIX_WIDTH = DN_WIDTH + SC_WIDTH + MEM_WIDTH
N_BRANCH = 3
IN_WIDTH = 4 * DN_WIDTH + 2 * DN_HEADS + 3 * SC_WIDTH + MEM_WIDTH + N_BRANCH * D_MODEL
N_EXPERTS = 32
TOP_K = 4
D_FF = D_MODEL
SWIGLU_ALPHA = 1.702
SWIGLU_LIMIT = 7.0

kernel_name = 'hybrid_deltanet_shortconv_mem_moe_stream_step'

def rmsnorm(x, w):
    xf = x.astype(jnp.float32)
    y = xf * lax.rsqrt(jnp.mean(xf * xf, axis=-1, keepdims=True) + EPS)
    return (y * w.astype(jnp.float32)).astype(x.dtype)

def l2norm(x):
    xf = x.astype(jnp.float32)
    return xf * lax.rsqrt(jnp.sum(xf * xf, axis=-1, keepdims=True) + EPS)

def causal_conv(x, buf, w):
    width, t = w.shape[0], x.shape[1]
    xp = jnp.concatenate([buf.astype(x.dtype), x], axis=1)
    y = w[0] * xp[:, 0:t]
    for j in range(1, width):
        y = y + w[j] * xp[:, j:j + t]
    return y.astype(x.dtype), xp[:, t:]

def gated_delta_chunked(q, k, v, g, beta, s0):
    b, t, h, dk = q.shape
    dv = v.shape[-1]
    L = CHUNK if t % CHUNK == 0 else t
    n = t // L

    def blocks(a):
        a = a.astype(jnp.float32).reshape((b, n, L, h) + a.shape[3:])
        return jnp.moveaxis(a, (1, 3), (0, 2))

    qc, kc, vc = blocks(q), blocks(k), blocks(v)
    gc, bc = blocks(g), blocks(beta)
    cum = jnp.cumsum(gc, axis=-1)
    causal = jnp.tril(jnp.ones((L, L), dtype=bool))
    strict = jnp.tril(jnp.ones((L, L), dtype=bool), -1)
    diff = cum[..., :, None] - cum[..., None, :]
    decay = jnp.where(causal, jnp.exp(jnp.where(causal, diff, 0.0)), 0.0)
    kk = jnp.einsum('nbhik,nbhjk->nbhij', kc, kc)
    a_mat = jnp.where(strict, decay * kk, 0.0) * bc[..., :, None]
    t_mat = a_mat + jnp.eye(L, dtype=jnp.float32)
    rhs = jnp.concatenate([bc[..., None] * vc, (bc * jnp.exp(cum))[..., None] * kc], axis=-1)
    sol = lax.linalg.triangular_solve(t_mat, rhs, left_side=True, lower=True, unit_diagonal=True)
    w_v, w_k = sol[..., :dv], sol[..., dv:]
    qk = jnp.einsum('nbhik,nbhjk->nbhij', qc, kc) * decay
    q_dec = jnp.exp(cum)[..., None] * qc
    k_dec = jnp.exp(cum[..., -1:] - cum)[..., None] * kc
    c_dec = jnp.exp(cum[..., -1])

    def step(s, xs):
        w_v_c, w_k_c, qk_c, q_c, k_c, d_c = xs
        u = w_v_c - jnp.einsum('bhlk,bhkv->bhlv', w_k_c, s)
        o = jnp.einsum('bhlk,bhkv->bhlv', q_c, s) + jnp.einsum('bhij,bhjv->bhiv', qk_c, u)
        s = d_c[..., None, None] * s + jnp.einsum('bhlk,bhlv->bhkv', k_c, u)
        return s, o

    s_final, o = lax.scan(step, s0.astype(jnp.float32), (w_v, w_k, qk, q_dec, k_dec, c_dec))
    o = jnp.moveaxis(o, (0, 2), (1, 3)).reshape(b, t, h, dv)
    return o, s_final

def split_in(proj):
    sizes = [DN_WIDTH, DN_WIDTH, DN_WIDTH, DN_HEADS, DN_HEADS, DN_WIDTH,
             SC_WIDTH, SC_WIDTH, SC_WIDTH, MEM_WIDTH, D_MODEL, D_MODEL, D_MODEL]
    offs = [int(o) for o in np.cumsum(sizes)[:-1]]
    return jnp.split(proj, offs, axis=-1)

def memory_kv(mem, mem_norm_w, w_mem_kv):
    b, m, _ = mem.shape
    kv = rmsnorm(mem, mem_norm_w) @ w_mem_kv
    mk, mv = jnp.split(kv, 2, axis=-1)
    return (mk.reshape(b, m, MEM_HEADS, MEM_HEAD_DIM), mv.reshape(b, m, MEM_HEADS, MEM_HEAD_DIM))

def mem_attend(q, mk, mv):
    s = jnp.einsum('bthd,bmhd->bhtm', q.astype(jnp.float32), mk.astype(jnp.float32)) * (MEM_HEAD_DIM ** -0.5)
    p = jax.nn.softmax(s, axis=-1)
    return jnp.einsum('bhtm,bmhd->bthd', p, mv.astype(jnp.float32)).astype(q.dtype)

def moe(x, w_router, b_router, w_gate, b_gate, w_up, b_up, w_down, b_down):
    bsz, t, d = x.shape
    n_tok = bsz * t
    xf = x.reshape(n_tok, d)
    logits = xf.astype(jnp.float32) @ w_router.astype(jnp.float32) + b_router.astype(jnp.float32)
    top_val, top_idx = lax.top_k(logits, TOP_K)
    gate = jax.nn.softmax(top_val, axis=-1)
    nk = n_tok * TOP_K
    flat_e = top_idx.reshape(nk)
    flat_tok = jnp.repeat(jnp.arange(n_tok, dtype=jnp.int32), TOP_K)
    order = jnp.argsort(flat_e)
    se, stok, sgate = flat_e[order], flat_tok[order], gate.reshape(nk)[order]
    blk = max(8, min(128, nk // N_EXPERTS))
    n_blocks = -(-nk // blk) + N_EXPERTS
    counts = jnp.bincount(flat_e, length=N_EXPERTS)
    pcounts = (counts + blk - 1) // blk * blk
    starts = jnp.cumsum(counts) - counts
    pends = jnp.cumsum(pcounts)
    pstarts = pends - pcounts
    dest = pstarts[se] + jnp.arange(nk, dtype=jnp.int32) - starts[se]
    rows = jnp.full((n_blocks * blk,), n_tok, dtype=jnp.int32).at[dest].set(stok)
    xpad = jnp.concatenate([xf, jnp.zeros((1, d), xf.dtype)], axis=0)
    xb = xpad[rows].reshape(n_blocks, blk, d)
    block_e = jnp.minimum(jnp.searchsorted(pends, jnp.arange(n_blocks, dtype=jnp.int32) * blk, side='right'), N_EXPERTS - 1)

    def expert_block(args):
        xblk, e = args
        gl = jnp.minimum(xblk @ w_gate[e] + b_gate[e], SWIGLU_LIMIT)
        ul = jnp.clip(xblk @ w_up[e] + b_up[e], -SWIGLU_LIMIT, SWIGLU_LIMIT)
        return ((ul + 1.0) * (gl * jax.nn.sigmoid(SWIGLU_ALPHA * gl))) @ w_down[e] + b_down[e]

    yb = lax.map(expert_block, (xb, block_e)).reshape(n_blocks * blk, d)
    pair = yb[dest] * sgate[:, None].astype(yb.dtype)
    out = jax.ops.segment_sum(pair, stok, num_segments=n_tok)
    return out.reshape(bsz, t, d).astype(x.dtype)

def trunk_layer(x, dn_conv_buf, dn_state, sc_conv_buf, mem_k, mem_v, p):
    b, t, _ = x.shape
    xn = rmsnorm(x, p['norm1_w'])
    proj = xn @ p['w_in']
    (q, k, v, a_logit, b_logit, dn_gate, sc_b, sc_c, sc_h, mq, g_dn, g_sc, g_mem) = split_in(proj)
    qkv, new_dn_conv = causal_conv(jnp.concatenate([q, k, v], axis=-1), dn_conv_buf, p['dn_conv_w'])
    q, k, v = jnp.split(jax.nn.silu(qkv), 3, axis=-1)
    q = l2norm(q.reshape(b, t, DN_HEADS, DN_HEAD_DIM)) * (DN_HEAD_DIM ** -0.5)
    k = l2norm(k.reshape(b, t, DN_HEADS, DN_HEAD_DIM))
    v = v.reshape(b, t, DN_HEADS, DN_HEAD_DIM)
    beta = jax.nn.sigmoid(b_logit.astype(jnp.float32))
    g = -jnp.exp(p['dn_A_log'].astype(jnp.float32)) * jax.nn.softplus(a_logit.astype(jnp.float32) + p['dn_dt_bias'].astype(jnp.float32))
    o, new_dn_state = gated_delta_chunked(q, k, v, g, beta, dn_state)
    o = o * lax.rsqrt(jnp.mean(o * o, axis=-1, keepdims=True) + EPS) * p['dn_norm_w'].astype(jnp.float32)
    o = o * jax.nn.silu(dn_gate.reshape(b, t, DN_HEADS, DN_HEAD_DIM).astype(jnp.float32))
    y_dn = o.reshape(b, t, DN_WIDTH).astype(x.dtype)
    conv_out, new_sc_conv = causal_conv(sc_c * sc_h, sc_conv_buf, p['sc_conv_w'])
    y_sc = sc_b * conv_out
    y_mem = mem_attend(mq.reshape(b, t, MEM_HEADS, MEM_HEAD_DIM), mem_k, mem_v).reshape(b, t, MEM_WIDTH)
    w_br = p['w_br']
    merged = (jax.nn.sigmoid(g_dn) * (y_dn @ w_br[:DN_WIDTH])
              + jax.nn.sigmoid(g_sc) * (y_sc @ w_br[DN_WIDTH:DN_WIDTH + SC_WIDTH])
              + jax.nn.sigmoid(g_mem) * (y_mem @ w_br[DN_WIDTH + SC_WIDTH:]))
    h = x + (merged @ p['w_o']).astype(x.dtype)
    h = h + moe(rmsnorm(h, p['norm2_w']), p['w_router'], p['b_router'], p['w_gate'], p['b_gate'],
                p['w_up'], p['b_up'], p['w_down'], p['b_down'])
    return h, new_dn_conv, new_dn_state.astype(x.dtype), new_sc_conv

def setup_inputs(seed: int = 0) -> dict:
    key = jax.random.key(seed)
    ks = jax.random.split(key, 32)
    f32 = jnp.float32

    def nrm(kk, shape, scale):
        return jax.random.normal(kk, shape, f32) * scale

    def gain(kk, shape):
        return 1.0 + 0.02 * jax.random.normal(kk, shape, f32)

    return {
        'x_prompt': nrm(ks[0], (BATCH, SEQ, D_MODEL), 1.0),
        'x_sample': nrm(ks[1], (DEC_BATCH, DEC_SEQ, D_MODEL), 1.0),
        'mem_prompt': nrm(ks[2], (BATCH, MEM_LEN, D_MODEL), 1.0),
        'state_dn': nrm(ks[3], (DEPTH, DEC_BATCH, DN_HEADS, DN_HEAD_DIM, DN_HEAD_DIM), 0.1),
        'state_dn_conv': nrm(ks[4], (DEPTH, DEC_BATCH, DN_CONV - 1, 3 * DN_WIDTH), 1.0),
        'state_sc_conv': nrm(ks[5], (DEPTH, DEC_BATCH, SC_CONV - 1, SC_WIDTH), 1.0),
        'cache_mem_k': nrm(ks[6], (DEPTH, DEC_BATCH, MEM_LEN, MEM_HEADS, MEM_HEAD_DIM), 1.0),
        'cache_mem_v': nrm(ks[7], (DEPTH, DEC_BATCH, MEM_LEN, MEM_HEADS, MEM_HEAD_DIM), 1.0),
        'w_in': nrm(ks[8], (DEPTH, D_MODEL, IN_WIDTH), D_MODEL ** -0.5),
        'dn_conv_w': nrm(ks[9], (DEPTH, DN_CONV, 3 * DN_WIDTH), DN_CONV ** -0.5),
        'dn_A_log': jnp.log(jax.random.uniform(ks[10], (DEPTH, DN_HEADS), f32, 1.0, 16.0)),
        'dn_dt_bias': jax.random.uniform(ks[11], (DEPTH, DN_HEADS), f32, -6.0, -3.0),
        'dn_norm_w': gain(ks[12], (DEPTH, DN_HEAD_DIM)),
        'sc_conv_w': nrm(ks[13], (DEPTH, SC_CONV, SC_WIDTH), SC_CONV ** -0.5),
        'mem_norm_w': gain(ks[14], (DEPTH, D_MODEL)),
        'w_mem_kv': nrm(ks[15], (DEPTH, D_MODEL, 2 * MEM_WIDTH), D_MODEL ** -0.5),
        'w_br': nrm(ks[16], (DEPTH, MIX_WIDTH, D_MODEL), MIX_WIDTH ** -0.5),
        'w_o': nrm(ks[17], (DEPTH, D_MODEL, D_MODEL), D_MODEL ** -0.5),
        'norm1_w': gain(ks[18], (DEPTH, D_MODEL)),
        'norm2_w': gain(ks[19], (DEPTH, D_MODEL)),
        'w_router': nrm(ks[20], (DEPTH, D_MODEL, N_EXPERTS), D_MODEL ** -0.5),
        'b_router': nrm(ks[21], (DEPTH, N_EXPERTS), 0.01),
        'w_gate': nrm(ks[22], (DEPTH, N_EXPERTS, D_MODEL, D_FF), D_MODEL ** -0.5),
        'b_gate': nrm(ks[23], (DEPTH, N_EXPERTS, D_FF), 0.01),
        'w_up': nrm(ks[24], (DEPTH, N_EXPERTS, D_MODEL, D_FF), D_MODEL ** -0.5),
        'b_up': nrm(ks[25], (DEPTH, N_EXPERTS, D_FF), 0.01),
        'w_down': nrm(ks[26], (DEPTH, N_EXPERTS, D_FF, D_MODEL), D_FF ** -0.5),
        'b_down': nrm(ks[27], (DEPTH, N_EXPERTS, D_MODEL), 0.01),
        'final_norm_w': gain(ks[28], (D_MODEL,)),
    }

def reference(x_prompt, x_sample, mem_prompt, state_dn, state_dn_conv, state_sc_conv, cache_mem_k, cache_mem_v,
              w_in, dn_conv_w, dn_A_log, dn_dt_bias, dn_norm_w, sc_conv_w, mem_norm_w, w_mem_kv, w_br, w_o,
              norm1_w, norm2_w, w_router, b_router, w_gate, b_gate, w_up, b_up, w_down, b_down, final_norm_w):
    hp, hs = x_prompt, x_sample
    bp = x_prompt.shape[0]
    p_dn, p_dnc, p_scc, p_mk, p_mv = [], [], [], [], []
    s_dn, s_dnc, s_scc = [], [], []
    for l in range(DEPTH):
        p = {'w_in': w_in[l], 'dn_conv_w': dn_conv_w[l], 'dn_A_log': dn_A_log[l], 'dn_dt_bias': dn_dt_bias[l],
             'dn_norm_w': dn_norm_w[l], 'sc_conv_w': sc_conv_w[l], 'w_br': w_br[l], 'w_o': w_o[l],
             'norm1_w': norm1_w[l], 'norm2_w': norm2_w[l], 'w_router': w_router[l], 'b_router': b_router[l],
             'w_gate': w_gate[l], 'b_gate': b_gate[l], 'w_up': w_up[l], 'b_up': b_up[l],
             'w_down': w_down[l], 'b_down': b_down[l]}
        mk, mv = memory_kv(mem_prompt, mem_norm_w[l], w_mem_kv[l])
        hp, dnc, dns, scc = trunk_layer(
            hp, jnp.zeros((bp, DN_CONV - 1, 3 * DN_WIDTH), hp.dtype),
            jnp.zeros((bp, DN_HEADS, DN_HEAD_DIM, DN_HEAD_DIM), jnp.float32),
            jnp.zeros((bp, SC_CONV - 1, SC_WIDTH), hp.dtype), mk, mv, p)
        p_dn.append(dns); p_dnc.append(dnc); p_scc.append(scc); p_mk.append(mk); p_mv.append(mv)
        hs, dnc2, dns2, scc2 = trunk_layer(hs, state_dn_conv[l], state_dn[l], state_sc_conv[l],
                                           cache_mem_k[l], cache_mem_v[l], p)
        s_dn.append(dns2); s_dnc.append(dnc2); s_scc.append(scc2)
    y_prompt = rmsnorm(hp, final_norm_w)
    y_sample = rmsnorm(hs, final_norm_w)
    return (y_prompt, y_sample, jnp.stack(p_dn), jnp.stack(p_dnc), jnp.stack(p_scc), jnp.stack(p_mk), jnp.stack(p_mv),
            jnp.stack(s_dn), jnp.stack(s_dnc), jnp.stack(s_scc))


_drawn_inputs = setup_inputs


def setup_inputs(seed=0):
    import zlib

    import numpy as np

    out = dict(_drawn_inputs(seed))
    spreads = {}
    factors = {'mem_norm_w': 2.884, 'b_gate': 8.0, 'b_up': 8.0, 'b_down': 8.0, 'final_norm_w': 2.736}
    for name, (base, spread) in spreads.items():
        noise = np.random.default_rng([zlib.crc32(name.encode()), seed]).standard_normal(out[name].shape)
        drawn = base * np.exp(spread * noise) if base else spread * noise
        out[name] = __import__('jax').numpy.asarray(drawn.astype(out[name].dtype))
    for name, factor in factors.items():
        out[name] = (out[name] * factor).astype(out[name].dtype)
    return out
```

```python
from contextlib import ExitStack

import concourse.bass as bass
import numpy as np
from concourse import mybir

P = 128
F32 = mybir.dt.float32
BF16 = mybir.dt.bfloat16
I32 = mybir.dt.int32
ALU = mybir.AluOpType
ACT = mybir.ActivationFunctionType
AX = mybir.AxisListType

EPS = 1e-6
HEADS = 4
CAP = 64
LIMIT = 7.0
ALPHA = 1.702
LEVELS = (1, 2, 4, 8, 16, 32)

CONST_COLS = {}
_at = 0
for _name, _n in (
    ("ident", P), ("ones", P), ("upto_prompt", P), ("upto_sample", P), ("block_prompt", P), ("block_sample", P),
    ("before", P), *((f"level{s}", P) for s in LEVELS), ("seq", 8), ("slots", CAP), ("rounds", 24), ("offsets", 5),
):
    CONST_COLS[_name] = (_at, _n)
    _at += _n
CONST_WIDTH = _at


def constant_table():
    i = np.arange(P)[:, None]
    j = np.arange(P)[None, :]
    table = np.zeros((P, CONST_WIDTH), np.float32)

    def put(name, value):
        a, n = CONST_COLS[name]
        table[:, a:a + n] = value

    put("ident", i == j)
    put("ones", 1.0)
    for name, block in (("prompt", 64), ("sample", 16)):
        put(f"upto_{name}", (i // block == j // block) & (i <= j))
        put(f"block_{name}", i // block == j // block)
    put("before", i < j)
    for s in LEVELS:
        put(f"level{s}", (i // (2 * s) == j // (2 * s)) & (i // s % 2 == 1) & (j // s % 2 == 0))
    put("seq", i // 16 == np.arange(8)[None, :])
    put("slots", np.arange(CAP)[None, :])
    put("rounds", np.arange(24)[None, :])
    put("offsets", CAP * np.arange(1, 6)[None, :])
    return table


def build(nc, A):
    D = A["x_prompt"].shape[2]
    KT8 = D // P
    E = A["w_router"].shape[2]
    TILES = 3
    TOK = TILES * P
    NSEQ = A["x_sample"].shape[0]
    LS = A["x_sample"].shape[1]
    MAX_OVER = TOK * 4 // CAP
    NQKV = 12
    LP = 3 + 256
    WP = LP + NSEQ * (3 + LS)
    SP2 = 2 + 256
    WS = SP2 + NSEQ * (2 + LS)
    TRUNK_PIECES = 17
    LAST_TRUNK = [max(n for n in range(TRUNK_PIECES) if n % 4 == s) for s in range(4)]

    ctx = ExitStack()
    with ctx:
        def sb(name, shape, dt=F32):
            return ctx.enter_context(nc.sbuf_tensor("sb_" + name, shape, dt))

        def sem(name):
            return ctx.enter_context(nc.semaphore("s_" + name))

        ring = sb("ring", [P, 6, 4096])
        h = sb("h", [P, TILES, D])
        xn = sb("xn", [P, 3072])
        r1 = sb("r1", [P, NQKV * WP])
        rq = sb("rq", [P, 4608])
        dg = sb("dg", [P, HEADS, TOK])
        sbb = sb("sbb", [P, 2, TOK])
        sp = sb("sp", [P, 2, WS])
        mq = sb("mq", [P, 2, TOK])
        qm = sb("qm", [P, 2048])
        kvp = sb("kvp", [P, 2, 512])
        wk = sb("wk", [P, 2048])
        cw = sb("cw", [P, 12 * 28 + 2 * 19])
        co = sb("co", [P, 12 * 27 + 2 * 18])
        scor = sb("scor", [18, 256])
        cst = sb("cst", [P, CONST_WIDTH])
        st = sb("st", [P, HEADS, P])
        wab = sb("wab", [P, KT8, 8])
        norms = sb("norms", [P, 3 * KT8 + 1])
        hb = sb("hb", [P, 8])
        small = sb("small", [P, 256])
        over = sb("over", [1, 1 + MAX_OVER], I32)

        ps = ctx.enter_context(nc.psum_tensor("ps", [P, 8 * 512], F32))

        def bank(b, n=1):
            return ps[:, b * 512:(b + n) * 512]

        def const(name):
            a, n = CONST_COLS[name]
            return cst[:, a:a + n]

        ident = const("ident")
        ones = const("ones")

        def piece(slot):
            return ring[:, slot, :].rearrange("p (t n) -> p t n", t=KT8)

        rd = ring[:, 4:6, :].rearrange("p a n -> p (a n)")
        mem = rd[:, 0:2048].rearrange("p (a n) -> p a n", a=2)
        xs_mem = rd[:, 2048:4096].rearrange("p (a n) -> p a n", a=2)
        mT = rd[:, 4096:6144].rearrange("p (t n) -> p t n", t=KT8)
        xs = rq[:, 0:3072].rearrange("p (a n) -> p a n", a=3)
        cwr = rq[0:28, 3072:4608]
        scr = dg[0:19, 0, 0:256]
        xnT = xn[:, :].rearrange("p (t n) -> p t n", t=KT8)
        xp = r1[:, :].rearrange("p (c n) -> p c n", c=NQKV)
        qkv = rq[:, :].rearrange("p (c n) -> p c n", c=NQKV)
        cwv = cw[:, 0:336].rearrange("p (c n) -> p c n", n=28)
        scwv = cw[:, 336:374].rearrange("p (c n) -> p c n", n=19)
        cov = co[:, 0:324].rearrange("p (c n) -> p c n", n=27)
        scov = co[:, 324:360].rearrange("p (c n) -> p c n", n=18)
        conv_acc = wk[:, 0:WP]
        cT = wk[:, 512:1280].rearrange("p (c n) -> p c n", c=2)
        hT = wk[:, 1280:2048].rearrange("p (c n) -> p c n", c=2)
        sq4 = r1[:, 0:1536].rearrange("p (c n) -> p c n", c=4)
        nr4 = r1[:, 1536:3072].rearrange("p (c n) -> p c n", c=4)
        cor = qm[0:27, 0:1536]
        kc = rd[:, 0:4096].rearrange("p (s m n) -> p s m n", s=NSEQ, m=2)
        vc = rd[:, 4096:8192].rearrange("p (s m n) -> p s m n", s=NSEQ, m=2)
        kT = r1[:, 0:4608].rearrange("p (b s m) -> p b s m", b=2, s=9)
        qmv = qm[:, :].rearrange("p (s b n) -> p s b n", s=NSEQ, b=2)
        prob = wk[:, 0:1024].rearrange("p (h m) -> p h m", h=4)
        probT = wk[:, 1024:2048].rearrange("p (c n) -> p c n", c=8)
        states = rd[:, 0:4096].rearrange("p (s h v) -> p s h v", s=NSEQ, h=HEADS)

        def t4(region, k):
            return region[:, k * 512:(k + 1) * 512].rearrange("p (h n) -> p h n", h=HEADS)

        gb, dTm, dec, eB, Am, Dm, Fm, Ym, Em = (t4(r1, k) for k in range(9))
        qkT, qd, bk, kd, bv, nwk, um, uT = (t4(rd, 8 + k) for k in range(8))
        oS, osq = t4(wk, 0), t4(wk, 1)
        umask = wk[:, 1024:2048].rearrange("p (s v) -> p s v", s=NSEQ)
        mg = rq[:, 0:3072].rearrange("p (t n) -> p t n", t=KT8)
        sig = wk[:, 0:1536].rearrange("p (a n) -> p a n", a=4)
        x2 = xn[:, :].rearrange("p (a n) -> p a n", a=3)
        x2T = r1[:, 0:3072].rearrange("p (t n) -> p t n", t=KT8)
        w2b = r1[:, 3072:4096]
        split = rq[:, :].bitcast(BF16).rearrange("p (k a n) -> p k a n", k=3, a=3)
        wr = qm[:, 0:256].rearrange("p (t e) -> p t e", t=KT8)
        br = qm[:, 256:256 + E]
        lg = qm[:, 288:384].rearrange("p (a e) -> p a e", a=3)
        rt = [qm[:, 384 + 96 * k:480 + 96 * k].rearrange("p (a e) -> p a e", a=3) for k in range(6)]
        pos = sb("pos", [P, 3, E + 1])
        gate = sb("gate", [P, 3, E + 1])
        shift = sb("shift", [P, MAX_OVER])
        bg = mq[:, 0, 0:256 + 8]
        bu = mq[:, 1, 0:256 + 8]
        gT = dg[0:E, 3, :]
        bd = dg[0:E, :, :].rearrange("p a n -> p (a n)")[:, 0:D]
        onehot = sbb[:, 0, 0:96].bitcast(BF16).rearrange("p (a c) -> p a c", a=3)
        onehot_g = sbb[:, 1, 0:192].rearrange("p (a c) -> p a c", a=3)
        brow = wk[:, 0:512].rearrange("p (b r n) -> p b r n", b=2, r=2)
        xg, hg, hu, sg, hTt, yT = (r1[:, k * 512:(k + 1) * 512] for k in range(6))
        pgT = r1[0:CAP, 3072:3072 + TOK]
        y = r1[0:CAP, 3584:4608]
        fw = xn[:, 0:1024]
        outb = xn[:, 1024:3072].rearrange("p (a n) -> p a n", a=2)
        hacc = h

        names = """cst x_in mem_in rows_in vec_in wab_in kc_in vc_in st_in rout_in bdn_in
            ss rt5 rs5 xs xtr xT cwtr cwT wabstep pj pjev pads conv silu sc_in sc_done
            sq nsum nadd nsqrt norm co cotr cor kv_out corout
            ktr kT qm sc soft pexp pn ptr pT pv ym
            gates gcum gex gbr cumb dexp dmul kk kkev tok tokev lv Fready Yready Gready wkt nwk u uev utr uready oT oev osum onorm snew st_upd um yd st_all
            ab abx abl abg
            gp gz gsig mrg wo hadd ss2 rt2 x2 x2tr x2T lgm lgx sel posm posx brt bT gtr gT bdm  overx
            P xg xgev pgt pgtev mgate hg sgm mup hh dn ytev ytr yev acc accrd used
            fw_in fss frt fo fout out tabs""".split()
        S = {n: sem(n) for n in dict.fromkeys(names)}
        loaded = [sem(f"loaded{k}") for k in range(6)]
        vlink, plink, mlink, olink = sem("vlink"), sem("plink"), sem("mlink"), sem("olink")

        block = ctx.enter_context(nc.Block())

        win = A["w_in"][0].rearrange("(p t) n -> p t n", t=KT8)
        wbr = A["w_br"][0].rearrange("(k p) n -> p k n", p=P)
        wo = A["w_o"][0].rearrange("(k p) n -> p k n", p=P)
        gcol = 3080
        trunk = [A["w_mem_kv"][0].rearrange("(p t) n -> p t n", t=KT8)]
        trunk += [win[:, :, c:c + 512] for c in (0, 512, 1024, 1544, 2056, 2568)]
        for half in range(2):
            trunk += [win[:, :, gcol + 1024 * b + 512 * half:gcol + 1024 * b + 512 * half + 512] for b in range(3)]
            trunk += [wbr[:, :, 512 * half:512 * half + 512]]
        trunk += [wo[:, :, 512 * k:512 * k + 512] for k in range(2)]
        assert len(trunk) == TRUNK_PIECES
        wg = A["w_gate"][0].rearrange("e (p t) n -> e p t n", t=KT8)
        wu = A["w_up"][0].rearrange("e (p t) n -> e p t n", t=KT8)
        wd = A["w_down"][0].rearrange("e (f p) n -> e p f n", p=P)

        x_s = A["x_sample"].rearrange("s l d -> (s l) d")
        outs = [A[f"out_{k}"] for k in range(10)]
        yp = outs[0][0].rearrange("(a p) d -> a p d", p=P)
        ys = outs[1].rearrange("s l d -> (s l) d")

        @block.sync
        def _(sp_):
            dma = sp_.dma_start

            def through(n):
                if n < 7:
                    sp_.wait_ge(S["pj"], 2 + 4 * n + (1 if n >= 4 else 0))
                elif n < 15:
                    sp_.wait_ge(S["gz"], 12 if n < 11 else 24)
                else:
                    sp_.wait_ge(S["wo"], 3 * (n - 14))

            def trunk_piece(n):
                if n >= 4:
                    through(n - 4)
                dma(piece(n % 4), trunk[n]).then_inc(loaded[n % 4], 16)

            dma(h[:, 0:2, :], A["x_prompt"][0].rearrange("(a p) d -> p a d", p=P)).then_inc(S["x_in"], 16)
            dma(h[:, 2, :], x_s).then_inc(S["x_in"], 16)
            dma(cst[:, :], A["consts"]).then_inc(S["cst"], 16)
            dma(mem, A["mem_prompt"][0].rearrange("(a p) d -> p a d", p=P)).then_inc(S["mem_in"], 16)
            trunk_piece(0)
            dma(cwr[0:24, :], A["state_dn_conv"][0].rearrange("s r c -> (s r) c")).then_inc(S["rows_in"], 16)
            dma(cwr[24:28, :], A["dn_conv_w"][0]).then_inc(S["rows_in"], 16)
            dma(scr[0:16, :], A["state_sc_conv"][0].rearrange("s r c -> (s r) c")).then_inc(S["rows_in"], 16)
            dma(scr[16:19, :], A["sc_conv_w"][0]).then_inc(S["rows_in"], 16)
            for k, name in enumerate(("norm1_w", "norm2_w", "mem_norm_w")):
                dma(norms[:, k * KT8:(k + 1) * KT8], A[name][0].rearrange("(p t) -> p t", t=KT8)).then_inc(S["vec_in"], 16)
            dma(norms[:, 24:25], A["dn_norm_w"][0].rearrange("(p o) -> p o", o=1)).then_inc(S["vec_in"], 16)
            dma(hb[:, 0:4], A["dn_A_log"].partition_broadcast(P).rearrange("p o h -> p (o h)")).then_inc(S["vec_in"], 16)
            dma(hb[:, 4:8], A["dn_dt_bias"].partition_broadcast(P).rearrange("p o h -> p (o h)")).then_inc(S["vec_in"], 16)
            trunk_piece(1)
            trunk_piece(2)
            trunk_piece(3)
            dma(wab[:, :, :], win[:, :, 1536:1544]).then_inc(S["wab_in"], 16)
            trunk_piece(4)
            sp_.wait_ge(S["pjev"], 2)
            for k in range(2):
                dma(outs[5 + k][0, 0].rearrange("(a p) h d -> p a (h d)", p=P),
                    kvp[:, :, 256 * k:256 * k + 256]).then_inc(S["kv_out"], 16)
            dma(kc, A["cache_mem_k"][0].rearrange("s (m p) h d -> p s m (h d)", p=P)).then_inc(S["kc_in"], 16)
            dma(vc, A["cache_mem_v"][0].rearrange("s (m p) h d -> p s m (h d)", p=P)).then_inc(S["vc_in"], 16)
            for n in range(5, 10):
                trunk_piece(n)
            sp_.wait_ge(S["cor"], 4)
            dma(outs[3][0, 0], cor[0:3, :]).then_inc(S["corout"], 16)
            dma(outs[8][0].rearrange("s r c -> (s r) c"), cor[3:27, :]).then_inc(S["corout"], 16)
            dma(outs[4][0, 0], scor[0:2, :]).then_inc(S["out"], 16)
            dma(outs[9][0].rearrange("s r c -> (s r) c"), scor[2:18, :]).then_inc(S["out"], 16)
            sp_.wait_ge(S["ktr"], 9)
            dma(states, A["state_dn"][0].rearrange("s h k v -> k s h v")).then_inc(S["st_in"], 16)
            sp_.wait_ge(S["st_all"], 1)
            dma(outs[2][0, 0].rearrange("h k v -> k h v"), st[:, :, :]).then_inc(S["out"], 16)
            sp_.wait_ge(S["st_all"], 2)
            dma(outs[7][0].rearrange("s h k v -> k s h v"), states).then_inc(S["out"], 16)
            for n in range(10, TRUNK_PIECES):
                trunk_piece(n)
            sp_.wait_ge(S["ym"], 3)
            dma(wr, A["w_router"][0].rearrange("(p t) e -> p t e", t=KT8)).then_inc(S["rout_in"], 16)
            dma(br, A["b_router"].partition_broadcast(P).rearrange("p o e -> p (o e)")).then_inc(S["rout_in"], 16)
            sp_.wait_ge(S["mrg"], 24)
            dma(w2b, A["norm2_w"].partition_broadcast(P).rearrange("p o d -> p (o d)")).then_inc(S["rout_in"], 16)
            dma(bd, A["b_down"][0]).then_inc(S["bdn_in"], 16)
            for k, name in enumerate(("b_gate", "b_up")):
                dma(brow[:, k, :, :], A[name][0].rearrange("(r e) (f p) -> (e f) r p", r=2, p=P)).then_inc(S["bdn_in"], 16)

            def expert_pieces(item, expert, first):
                for s in range(6):
                    w = (wg, wu, wd)[s // 2]
                    if not first:
                        sp_.wait_ge(S["used"], 6 * item + (s - 5))
                    elif s < 4:
                        through(LAST_TRUNK[s])
                    elif s == 4:
                        sp_.wait_ge(S["out"], 64)
                    src = w[bass.ds(expert, 1), :, 4 * (s % 2):4 * (s % 2) + 4, :] if not isinstance(expert, int) \
                        else w[expert:expert + 1, :, 4 * (s % 2):4 * (s % 2) + 4, :]
                    dma(ring[:, s, :], src.rearrange("e p t n -> p (e t) n")).then_inc(loaded[s], 16)

            expert_pieces(0, 0, True)
            sp_.wait_ge(S["accrd"], 1)
            dma(fw, A["final_norm_w"].partition_broadcast(P)).then_inc(S["fw_in"], 16)
            with sp_.Fori(1, E) as e:
                expert_pieces(e, e, False)
            sp_.wait_ge(S["overx"], 1)
            n_over = sp_.value_load(over[0:1, 0:1], min_val=0, max_val=MAX_OVER)
            with sp_.If(n_over > 0):
                with sp_.Fori(0, MAX_OVER) as i:
                    with sp_.If(n_over > i):
                        expert = sp_.value_load(over[0:1, bass.ds(i + 1, 1)], min_val=0, max_val=E - 1)
                        expert_pieces(i + E, expert, False)
            for t in range(TILES):
                sp_.wait_ge(S["fo"], t + 1)
                dma(yp[t] if t < 2 else ys, outb[:, t % 2, :]).then_inc(S["fout"], 16)
            sp_.wait_ge(S["fout"], 48)
            sp_.wait_ge(S["out"], 64)
            sp_.wait_ge(S["kv_out"], 32)
            sp_.wait_ge(S["corout"], 32)

        upto = [const("upto_prompt"), const("upto_prompt"), const("upto_sample")]
        blockones = [const("block_prompt"), const("block_prompt"), const("block_sample")]
        tile_levels = [LEVELS, LEVELS, LEVELS[:4]]
        LEVEL_STEPS = [sum(len(tile_levels[u]) - 1 for u in range(t)) for t in range(TILES + 1)]

        @block.tensor
        def _(pe):
            mm = nc.tensor.matmul

            def tr(out, in_, n=P):
                return nc.tensor.transpose(out, in_, ident[0:n, 0:n])

            pe.wait_ge(S["cst"], 16)
            for t in range(5):
                pe.wait_ge(S["xs"], t + 1)
                if t >= 4:
                    pe.wait_ge(S["xT"], t - 3)
                src = xs[:, t, :] if t < 3 else xs_mem[:, t - 3, :]
                for k in range(KT8):
                    last = tr(bank((2 * t + k // 4) % 8)[:, (k % 4) * P:(k % 4 + 1) * P], src[:, k::KT8])
                last.then_inc(S["xtr"], 1)
            pe.wait_ge(S["rows_in"], 64)
            pe.wait_ge(S["xT"], 2)
            for c in range(12):
                tr(bank(2)[:, c * 28:(c + 1) * 28], cwr[:, c * P:(c + 1) * P], 28)
            for c in range(2):
                last = tr(bank(2)[:, 336 + c * 19:336 + (c + 1) * 19], scr[:, c * P:(c + 1) * P], 19)
            last.then_inc(S["cwtr"], 1)

            def step_start(q):
                if q >= 8:
                    pe.wait_ge(S["pjev"], q - 7)

            pe.wait_ge(S["xT"], 5)
            pe.wait_ge(S["cwT"], 1)
            pe.wait_ge(loaded[0], 16)
            for q in range(2):
                for t in range(KT8):
                    last = mm(bank(q), mT[:, t, q * P:(q + 1) * P], piece(0)[:, t, :], start=(t == 0), stop=(t == KT8 - 1))
                last.then_inc(S["pj"], 1)

            q = 2
            for n in range(1, 7):
                pe.wait_ge(loaded[n % 4], 16 * (n // 4 + 1))
                if n == 4:
                    pe.wait_ge(S["wab_in"], 16)
                    step_start(q)
                    for a in range(TILES):
                        for t in range(KT8):
                            last = mm(bank(q % 8)[:, a * 8:(a + 1) * 8], xnT[:, t, a * P:(a + 1) * P], wab[:, t, :],
                                      start=(t == 0), stop=(t == KT8 - 1))
                    last.then_inc(S["pj"], 1)
                    q += 1
                for c in range(4):
                    step_start(q)
                    for t in range(KT8):
                        last = mm(bank(q % 8)[:, 0:TOK], piece(n % 4)[:, t, c * P:(c + 1) * P], xnT[:, t, :],
                                  start=(t == 0), stop=(t == KT8 - 1))
                    last.then_inc(S["pj"], 1)
                    q += 1
            assert q == 27

            pe.wait_ge(S["pjev"], 27)
            for g in range(2):
                pe.wait_ge(S["sq"], g + 1)
                if g:
                    pe.wait_ge(S["nadd"], g)
                for c in range(4):
                    last = mm(bank(c)[:, 0:TOK], ones, sq4[:, c, :], start=True, stop=True)
                last.then_inc(S["nsum"], 1)
            pe.wait_ge(S["co"], 2)
            for c in range(12):
                last = tr(bank(4 + c // 4)[0:27, (c % 4) * P:(c % 4 + 1) * P], cov[:, c, :])
                if c % 4 == 3:
                    last.then_inc(S["cotr"], 1)
            for c in range(2):
                last = tr(bank(7)[0:18, c * P:(c + 1) * P], scov[:, c, :])
            last.then_inc(S["cotr"], 1)

            pe.wait_ge(S["kc_in"], 16)
            pe.wait_ge(S["nadd"], 2)
            pe.wait_ge(S["cor"], 4)
            for s in range(9):
                if s >= 8:
                    pe.wait_ge(S["kT"], s - 7)
                for b in range(2):
                    for m in range(2):
                        src = kc[:, s, m, b * P:(b + 1) * P] if s < 8 else kvp[:, m, b * P:(b + 1) * P]
                        last = tr(bank(s % 8)[:, (2 * b + m) * P:(2 * b + m + 1) * P], src)
                last.then_inc(S["ktr"], 1)
            pe.wait_ge(S["kT"], 9)
            pe.wait_ge(S["qm"], 1)
            pe.wait_ge(S["vc_in"], 16)
            for t in range(TILES):
                if t >= 1:
                    pe.wait_ge(S["ym"], t)
                for hh in range(4):
                    o = bank(2 * t + hh % 2)[:, (hh // 2) * 256:(hh // 2) * 256 + 256]
                    rows = slice(64 * (hh % 2), 64 * (hh % 2) + 64)
                    if t < 2:
                        last = mm(o, mq[rows, hh // 2, t * P:(t + 1) * P], kT[rows, hh // 2, 8, :], start=True, stop=True)
                    else:
                        for s in range(NSEQ):
                            last = mm(o, qmv[rows, s, hh // 2, :], kT[rows, hh // 2, s, :], start=(s == 0), stop=(s == NSEQ - 1))
                last.then_inc(S["sc"], 1)
                pe.wait_ge(S["pn"], t + 1)
                for hh in range(4):
                    for m in range(2):
                        k = 2 * hh + m
                        last = tr(bank(6 + k // 4)[:, (k % 4) * P:(k % 4 + 1) * P],
                                  prob[:, 2 * (hh % 2) + hh // 2, m * P:(m + 1) * P])
                last.then_inc(S["ptr"], 1)
                pe.wait_ge(S["pT"], t + 1)
                for hh in range(4):
                    rows = slice(64 * (hh % 2), 64 * (hh % 2) + 64)
                    o = bank(2 * t)[rows, (hh // 2) * P:(hh // 2 + 1) * P]
                    if t < 2:
                        for m in range(2):
                            last = mm(o, kvp[:, m, 256 + 64 * hh:320 + 64 * hh], probT[:, 2 * hh + m, :],
                                      start=(m == 0), stop=(m == 1))
                    else:
                        for s in range(NSEQ):
                            for m in range(2):
                                last = mm(o[:, s * LS:(s + 1) * LS], vc[:, s, m, 64 * hh:64 * hh + 64],
                                          probT[:, 2 * hh + m, s * LS:(s + 1) * LS], start=(m == 0), stop=(m == 1))
                last.then_inc(S["pv"], 1)

            pe.wait_ge(S["norm"], 2)
            pe.wait_ge(S["gates"], 1)
            pe.wait_ge(S["ym"], 3)
            for t in range(TILES):
                cols = slice(t * P, (t + 1) * P)
                if t >= 1:
                    pe.wait_ge(S["yd"], t)
                mm(bank(0)[:, 0:4], upto[t], small[:, 12 * t:12 * t + 4], start=True, stop=True)
                mm(bank(0)[:, 4:8], blockones[t], small[:, 12 * t:12 * t + 4], start=True, stop=True).then_inc(S["gcum"], 1)
                pe.wait_ge(S["gbr"], t + 1)
                for hh in range(HEADS):
                    last = mm(bank(1)[:, hh * P:(hh + 1) * P], gb[:, hh, :], upto[t], start=True, stop=True)
                last.then_inc(S["cumb"], 1)
                for hh in range(HEADS):
                    mm(bank(2)[:, hh * P:(hh + 1) * P], qkv[:, 4 + hh, cols], qkv[:, 4 + hh, cols], start=True, stop=True)
                    last = mm(bank(3)[:, hh * P:(hh + 1) * P], qkv[:, 4 + hh, cols], qkv[:, hh, cols], start=True, stop=True)
                last.then_inc(S["kk"], 1)
                for hh in range(HEADS):
                    tr(bank(4)[:, hh * P:(hh + 1) * P], qkv[:, 4 + hh, cols])
                    last = tr(bank(5)[:, hh * P:(hh + 1) * P], qkv[:, 8 + hh, cols])
                last.then_inc(S["tok"], 1)
                pe.wait_ge(S["lv"], LEVEL_STEPS[t] + 2 * t + 1)
                for hh in range(HEADS):
                    last = tr(bank(6)[:, hh * P:(hh + 1) * P], Dm[:, hh, :])
                last.then_inc(S["Fready"], 1)
                for n in range(1, len(tile_levels[t])):
                    k = LEVEL_STEPS[t] + n
                    pe.wait_ge(S["lv"], k + 2 * t + 1)
                    for hh in range(HEADS):
                        last = mm(bank(7)[:, hh * P:(hh + 1) * P], Em[:, hh, :], Fm[:, hh, :], start=True, stop=True)
                    last.then_inc(S["Yready"], 1)
                    pe.wait_ge(S["uready"], k)
                    for hh in range(HEADS):
                        mm(bank(6)[:, hh * P:(hh + 1) * P], Dm[:, hh, :], Ym[:, hh, :], start=True, stop=True)
                        last = mm(bank(2)[:, hh * P:(hh + 1) * P], Ym[:, hh, :], Dm[:, hh, :], start=True, stop=True)
                    last.then_inc(S["Gready"], 1)
                pe.wait_ge(S["lv"], LEVEL_STEPS[t + 1] + 2 * t + 2)
                pe.wait_ge(S["tokev"], t + 1)
                for hh in range(HEADS):
                    last = mm(bank(4)[:, hh * P:(hh + 1) * P], bk[:, hh, :], Fm[:, hh, :], start=True, stop=True)
                last.then_inc(S["wkt"], 1)
                pe.wait_ge(S["nwk"], t + 1)
                if t < 2:
                    for b in range(2):
                        g = 2 * t + b
                        rows = slice(64 * b, 64 * b + 64)
                        if g >= 1:
                            pe.wait_ge(S["st_upd"], g)
                        for hh in range(HEADS):
                            o = bank(5)[rows, hh * P:(hh + 1) * P]
                            last = mm(o, Fm[:, hh, rows], bv[:, hh, :], start=True, stop=(g == 0))
                            if g >= 1:
                                last = mm(o, nwk[:, hh, rows], st[:, hh, :], start=False, stop=True)
                        last.then_inc(S["u"], 1)
                        for hh in range(HEADS):
                            if g >= 1:
                                mm(bank(0)[:, hh * P + 64 * b:hh * P + 64 * b + 64], st[:, hh, :], qd[:, hh, rows],
                                   start=True, stop=False)
                            if hh == 0:
                                pe.wait_ge(S["uev"], g + 1)
                            mm(bank(0)[:, hh * P + 64 * b:hh * P + 64 * b + 64], um[rows, hh, :], qkT[rows, hh, rows],
                               start=(g == 0), stop=True)
                        for hh in range(HEADS):
                            last = mm(bank(6 + b)[:, hh * P:(hh + 1) * P], kd[rows, hh, :], um[rows, hh, :],
                                      start=True, stop=True)
                        last.then_inc(S["snew"], 1)
                else:
                    pe.wait_ge(S["st_in"], 16)
                    for hh in range(HEADS):
                        o = bank(5)[:, hh * P:(hh + 1) * P]
                        for s in range(NSEQ):
                            c = slice(s * LS, (s + 1) * LS)
                            mm(o[:, c], states[:, s, hh, :], nwk[:, hh, c], start=(s == 0), stop=False,
                               skip_group_check=True)
                        last = mm(o, bv[:, hh, :], Fm[:, hh, :], start=False, stop=True, skip_group_check=True)
                    last.then_inc(S["u"], 1)
                    pe.wait_ge(S["utr"], 1)
                    for hh in range(HEADS):
                        last = tr(bank(2)[:, hh * P:(hh + 1) * P], uT[:, hh, :])
                    last.then_inc(S["u"], 1)
                    pe.wait_ge(S["uev"], 5)
                    for hh in range(HEADS):
                        o = bank(0)[:, hh * P:(hh + 1) * P]
                        for s in range(NSEQ):
                            c = slice(s * LS, (s + 1) * LS)
                            mm(o[:, c], states[:, s, hh, :], qd[:, hh, c], start=(s == 0), stop=False,
                               skip_group_check=True)
                        mm(o, um[:, hh, :], qkT[:, hh, :], start=False, stop=True, skip_group_check=True)
                    for hh in range(HEADS):
                        pe.wait_ge(S["um"], hh + 1)
                        if hh:
                            pe.wait_ge(S["st_upd"], 4 + hh)
                        for k in range(2):
                            last = mm(bank(6 + k), kd[:, hh, :], umask[:, 4 * k:4 * k + 4, :].rearrange("p s v -> p (s v)"),
                                      start=True, stop=True)
                        last.then_inc(S["snew"], 1)
                pe.wait_ge(S["oev"], t + 1)
                last = mm(bank(1), ones, osq.rearrange("p h n -> p (h n)"), start=True, stop=True)
                last.then_inc(S["osum"], 1)

            pe.wait_ge(S["yd"], 3)
            k = 0
            branches = ((0, 4, dg), (4, 2, sbb), (6, 2, mq))
            for half in range(2):
                for n in range(7 + 4 * half, 11 + 4 * half):
                    pe.wait_ge(loaded[n % 4], 16 * (n // 4 + 1))
                for c in range(4):
                    for b, (k0, kn, src) in enumerate(branches):
                        if k >= 4:
                            pe.wait_ge(S["mrg"], k - 3)
                        w = piece((7 + 4 * half + b) % 4)
                        for t in range(KT8):
                            last = mm(bank(2 * (k % 4))[:, 0:TOK], w[:, t, c * P:(c + 1) * P], xnT[:, t, :],
                                      start=(t == 0), stop=(t == KT8 - 1))
                        last.then_inc(S["gp"], 1)
                        w = piece((10 + 4 * half) % 4)
                        for j in range(kn):
                            last = mm(bank(2 * (k % 4) + 1)[:, 0:TOK], w[:, k0 + j, c * P:(c + 1) * P], src[:, j, :],
                                      start=(j == 0), stop=(j == kn - 1))
                        last.then_inc(S["gz"], 1)
                        k += 1

            pe.wait_ge(S["mrg"], 24)
            for half in range(2):
                n = 15 + half
                pe.wait_ge(loaded[n % 4], 16 * (n // 4 + 1))
                for a in range(TILES):
                    for j in range(KT8):
                        last = mm(bank(3 * half + a), mg[:, j, a * P:(a + 1) * P], piece(n % 4)[:, j, :],
                                  start=(j == 0), stop=(j == KT8 - 1))
                    last.then_inc(S["wo"], 1)

            pe.wait_ge(S["bdn_in"], 48)
            for k in range(2):
                for r in range(2):
                    last = tr(bank(6)[:, (2 * k + r) * P:(2 * k + r + 1) * P], brow[:, k, r, :])
            last.then_inc(S["brt"], 1)
            pe.wait_ge(S["hadd"], 6)
            for a in range(TILES):
                pe.wait_ge(S["x2"], a + 1)
                for k in range(KT8):
                    last = tr(bank(2 * a + k // 4)[:, (k % 4) * P:(k % 4 + 1) * P], x2[:, a, k::KT8])
                last.then_inc(S["x2tr"], 1)
            pe.wait_ge(S["x2T"], 3)
            pe.wait_ge(S["rout_in"], 48)
            for a in range(TILES):
                for t in range(KT8):
                    last = mm(bank(7)[:, a * E:(a + 1) * E], x2T[:, t, a * P:(a + 1) * P], wr[:, t, :],
                              start=(t == 0), stop=(t == KT8 - 1))
            last.then_inc(S["lgm"], 1)
            pe.wait_ge(S["sel"], 1)
            mask = rt[0]
            for a in range(TILES):
                for b in range(a):
                    mm(bank(0)[:, a * E:(a + 1) * E], ones, mask[:, b, :], start=(b == 0), stop=False)
                mm(bank(0)[:, a * E:(a + 1) * E], const("before"), mask[:, a, :], start=(a == 0), stop=True)
            for a in range(TILES):
                last = mm(bank(0)[:, 3 * E:4 * E], ones, mask[:, a, :], start=(a == 0), stop=(a == TILES - 1))
            last.then_inc(S["posm"], 1)
            for a in range(TILES):
                last = tr(bank(1)[0:E, a * P:(a + 1) * P], gate[:, a, 0:E])
            last.then_inc(S["gtr"], 1)
            pe.wait_ge(S["gT"], 1)
            for a in range(TILES):
                for k in range(2):
                    last = mm(bank(2 + 2 * a + k), gT[:, a * P:(a + 1) * P], bd[:, 512 * k:512 * k + 512], start=True, stop=True)
            last.then_inc(S["bdm"], 1)

            pe.wait_ge(S["accrd"], 1)

            def gather(n):
                pe.wait_ge(S["P"], n + 1)
                for t in range(KT8):
                    for a in range(TILES):
                        for k in range(3):
                            last = mm(bank(0)[:, t * CAP:(t + 1) * CAP], split[:, k, a, t::KT8], onehot[:, a, :],
                                      start=(a == 0 and k == 0), stop=(a == TILES - 1 and k == 2))
                last.then_inc(S["xg"], 1)

            def mlp(n, m, e_next):
                pe.wait_ge(S["xgev"], m + 1)
                for half in range(2):
                    pe.wait_ge(loaded[half], ld(n, half))
                    for t in range(4):
                        for f in range(8):
                            last = mm(bank(1)[:, f * CAP:(f + 1) * CAP], ring[:, half, t * 1024 + f * P:t * 1024 + (f + 1) * P],
                                      xg[:, (4 * half + t) * CAP:(4 * half + t + 1) * CAP],
                                      start=(half == 0 and t == 0 and f == 0), stop=(half == 1 and t == 3),
                                      skip_group_check=True)
                    last.then_inc(S["used"], 1)
                for a in range(TILES):
                    last = tr(bank(4)[0:CAP, a * P:(a + 1) * P], onehot_g[:, a, :])
                last.then_inc(S["pgt"], 1)
                for half in range(2):
                    pe.wait_ge(loaded[2 + half], ld(n, 2 + half))
                    for t in range(4):
                        for f in range(8):
                            last = mm(bank(2)[:, f * CAP:(f + 1) * CAP], ring[:, 2 + half, t * 1024 + f * P:t * 1024 + (f + 1) * P],
                                      xg[:, (4 * half + t) * CAP:(4 * half + t + 1) * CAP],
                                      start=(half == 0 and t == 0 and f == 0), stop=(half == 1 and t == 3),
                                      skip_group_check=True)
                    last.then_inc(S["used"], 1)
                if e_next:
                    gather(m + 1)
                pe.wait_ge(S["hh"], n + 1)
                for half in range(2):
                    pe.wait_ge(loaded[4 + half], ld(n, 4 + half))
                    for f in range(4):
                        for c in range(8):
                            last = mm(bank(3)[:, c * CAP:(c + 1) * CAP], ring[:, 4 + half, f * 1024 + c * P:f * 1024 + (c + 1) * P],
                                      hTt[:, (4 * half + f) * CAP:(4 * half + f + 1) * CAP],
                                      start=(half == 0 and f == 0 and c == 0), stop=(half == 1 and f == 3),
                                      skip_group_check=True)
                    last.then_inc(S["used"], 1)
                pe.wait_ge(S["pgtev"], n + 1)
                pe.wait_ge(S["ytev"], n + 1)
                mm(bank(4)[0:CAP, 0:P], yT[:, 0:CAP], ident, start=True, stop=True)
                for c in range(1, 8):
                    last = tr(bank(4 + c // 4)[0:CAP, (c % 4) * P:(c % 4 + 1) * P], yT[:, c * CAP:(c + 1) * CAP])
                last.then_inc(S["ytr"], 1)
                pe.wait_ge(S["yev"], n + 1)
                for a in range(TILES):
                    for k in range(2):
                        if a:
                            pe.wait_ge(S["accrd"], 6 * n + 2 * a + k)
                        mm(bank(6 + k), pgT[:, a * P:(a + 1) * P], y[:, 512 * k:512 * k + 512],
                           start=True, stop=True).then_inc(S["acc"], 1)

            def ld(n, s):
                return 16 * (sum(1 for k in range(TRUNK_PIECES) if s < 4 and k % 4 == s)) + 16 + 16 * n

            gather(0)
            with pe.Fori(0, E) as e:
                mlp(e, e, True)
            pe.wait_ge(S["overx"], 1)
            n_over = pe.value_load(over[0:1, 0:1], min_val=0, max_val=MAX_OVER)
            with pe.If(n_over > 0):
                with pe.Fori(0, MAX_OVER) as i:
                    with pe.If(n_over > i):
                        pe.wait_ge(S["accrd"], 6 * i + 6 * E + 1)
                        gather(i + E + 1)
                        mlp(i + E, i + E + 1, False)

        @block.scalar
        def _(act):
            f = nc.scalar.activation
            own = [0]

            def link(ins):
                own[0] += 1
                ins.then_inc(S["tabs"], 1)
                act.wait_ge(S["tabs"], own[0])

            act.wait_ge(S["x_in"], 32)
            for t in range(3):
                f(xs[:, t, :], h[:, t, :], ACT.Square, accum_out=small[:, 40 + t:41 + t])
            act.wait_ge(S["mem_in"], 16)
            for t in range(2):
                last = f(xs_mem[:, t, :], mem[:, t, :], ACT.Square, accum_out=small[:, 43 + t:44 + t])
            last.then_inc(S["ss"], 1)
            act.wait_ge(S["ss"], 2)
            f(small[:, 46:51], small[:, 40:45], ACT.Sqrt).then_inc(S["rt5"], 1)
            def xp_sample(c):
                return xp[:, c, LP:WP].rearrange("p (s k) -> p s k", k=3 + LS)[:, :, 3:3 + LS]

            act.wait_ge(S["cwtr"], 1)
            f(cw[:, :], bank(2)[:, 0:374], ACT.Copy).then_inc(S["cwT"], 1)
            for q in range(27):
                b = bank(q % 8)
                act.wait_ge(S["pj"], q + 1)
                if q < 2:
                    last = f(kvp[:, q, :], b, ACT.Copy)
                elif q < 14:
                    f(xp[:, q - 2, 3:LP], b[:, 0:256], ACT.Copy)
                    last = f(xp_sample(q - 2), b[:, 256:TOK].rearrange("p (s k) -> p s k", k=LS), ACT.Copy)
                elif q == 14:
                    last = f(small[:, 64:88], b[:, 0:24], ACT.Copy)
                elif q < 19:
                    last = f(dg[:, q - 15, :], b[:, 0:TOK], ACT.Silu)
                elif q < 21:
                    last = f(sbb[:, q - 19, :], b[:, 0:TOK], ACT.Copy)
                elif q < 23:
                    last = f(cT[:, q - 21, :], b[:, 0:TOK], ACT.Copy)
                elif q < 25:
                    last = f(hT[:, q - 23, :], b[:, 0:TOK], ACT.Copy)
                else:
                    last = f(mq[:, q - 25, :], b[:, 0:TOK], ACT.Copy)
                last.then_inc(S["pjev"], 1)
            for c in range(NQKV):
                act.wait_ge(S["conv"], c + 1)
                f(qkv[:, c, 0:256], conv_acc[:, 0:256], ACT.Silu)
                f(qkv[:, c, 256:TOK].rearrange("p (s k) -> p s k", k=LS),
                  conv_acc[:, LP:WP].rearrange("p (s k) -> p s k", k=3 + LS)[:, :, 0:LS], ACT.Silu).then_inc(S["silu"], 1)
            act.wait_ge(S["silu"], NQKV)
            act.wait_ge(S["conv"], NQKV)
            act.wait_ge(S["co"], 1)
            for g in range(2):
                if g:
                    act.wait_ge(S["nsum"], g)
                f(sq4, qkv[:, 4 * g:4 * g + 4, :], ACT.Square).then_inc(S["sq"], 1)
                act.wait_ge(S["nadd"], g + 1)
                f(nr4, nr4, ACT.Sqrt).then_inc(S["nsqrt"], 1)
            for k in range(3):
                act.wait_ge(S["cotr"], k + 1)
                f(cor[:, 512 * k:512 * k + 512], bank(4 + k)[0:27, :], ACT.Copy).then_inc(S["cor"], 1)
            act.wait_ge(S["cotr"], 4)
            f(scor[:, :], bank(7)[0:18, 0:256], ACT.Copy).then_inc(S["cor"], 1)
            act.wait_ge(S["vec_in"], 96)
            f(small[:, 108:112], hb[:, 0:4], ACT.Exp)
            act.wait_ge(S["ab"], 1)
            f(small[:, 128:140], small[:, 112:124], ACT.Exp, scale=-1.0).then_inc(S["abx"], 1)
            act.wait_ge(S["ab"], 2)
            f(small[:, 128:140], small[:, 128:140], ACT.Ln).then_inc(S["abl"], 1)
            f(small[:, 144:156], small[:, 88:100], ACT.Sigmoid).then_inc(S["abg"], 1)
            act.wait_ge(S["norm"], 2)
            for s in range(9):
                act.wait_ge(S["ktr"], s + 1)
                f(kT[:, :, s, :], bank(s % 8).rearrange("p (b m) -> p b m", b=2), ACT.Copy).then_inc(S["kT"], 1)
            for t in range(TILES):
                act.wait_ge(S["soft"], t + 1)
                if t:
                    act.wait_ge(S["ptr"], t)
                for hh in range(4):
                    last = f(prob[:, hh, :], bank(2 * t + hh // 2)[:, (hh % 2) * 256:(hh % 2) * 256 + 256], ACT.Exp,
                             bias=small[:, 160 + hh:161 + hh], scale=0.125, accum_out=small[:, 164 + hh:165 + hh])
                last.then_inc(S["pexp"], 1)
                act.wait_ge(S["ptr"], t + 1)
                if t:
                    act.wait_ge(S["pv"], t)
                f(probT, bank(6, 2).rearrange("p (c n) -> p c n", c=8), ACT.Copy).then_inc(S["pT"], 1)
                act.wait_ge(S["pv"], t + 1)
                f(mq[:, :, t * P:(t + 1) * P], bank(2 * t)[:, 0:256].rearrange("p (b n) -> p b n", b=2),
                  ACT.Copy).then_inc(S["ym"], 1)
            for t in range(TILES):
                act.wait_ge(S["gex"], 2 * t + 1)
                f(small[:, 180:188], small[:, 172:180], ACT.Exp).then_inc(S["gex"], 1)
                act.wait_ge(S["dexp"], 3 * t + 1)
                f(eB, bank(1).rearrange("p (h n) -> p h n", h=4), ACT.Exp)
                f(dTm, dTm, ACT.Exp)
                f(dec, dec, ACT.Exp, scale=-1.0).then_inc(S["dexp"], 2)
                act.wait_ge(S["dmul"], t + 1)
                for n in range(1, len(tile_levels[t])):
                    k = LEVEL_STEPS[t] + n
                    act.wait_ge(S["Yready"], k)
                    f(Ym, bank(7).rearrange("p (h n) -> p h n", h=4), ACT.Copy).then_inc(S["uready"], 1)
                act.wait_ge(S["wkt"], t + 1)
                f(nwk, bank(4).rearrange("p (h n) -> p h n", h=4), ACT.Copy, scale=-1.0).then_inc(S["nwk"], 1)
                if t < 2:
                    for b in range(2):
                        act.wait_ge(S["u"], 2 * t + b + 1)
                        f(um[64 * b:64 * b + 64, :, :], bank(5)[64 * b:64 * b + 64, :].rearrange("p (h n) -> p h n", h=4),
                          ACT.Copy).then_inc(S["uev"], 1)
                    act.wait_ge(S["snew"], 2 * t + 2)
                else:
                    act.wait_ge(S["u"], 5)
                    f(uT, bank(5).rearrange("p (h n) -> p h n", h=4), ACT.Copy).then_inc(S["utr"], 1)
                    act.wait_ge(S["u"], 6)
                    f(um, bank(2).rearrange("p (h n) -> p h n", h=4), ACT.Copy).then_inc(S["uev"], 1)
                    act.wait_ge(S["snew"], 5)
                f(oS, bank(0).rearrange("p (h n) -> p h n", h=4), ACT.Copy)
                f(osq, bank(0).rearrange("p (h n) -> p h n", h=4), ACT.Square).then_inc(S["oev"], 1)
                act.wait_ge(S["onorm"], 2 * t + 1)
                f(osq, osq, ACT.Sqrt).then_inc(S["onorm"], 1)
            act.wait_ge(S["yd"], 3)
            for k in range(24):
                act.wait_ge(S["gp"], k + 1)
                if k >= 4:
                    act.wait_ge(S["mrg"], k - 3)
                f(sig[:, k % 4, :], bank(2 * (k % 4))[:, 0:TOK], ACT.Sigmoid).then_inc(S["gsig"], 1)
            act.wait_ge(S["hadd"], 6)
            for t in range(TILES):
                last = f(x2[:, t, :], h[:, t, :], ACT.Square, accum_out=small[:, 40 + t:41 + t])
            last.then_inc(S["ss2"], 1)
            act.wait_ge(S["rt2"], 1)
            f(small[:, 46:49], small[:, 40:43], ACT.Sqrt).then_inc(S["rt2"], 1)
            act.wait_ge(S["brt"], 1)
            for k, dst in enumerate((bg, bu)):
                last = f(dst[:, 0:256], bank(6)[:, 256 * k:256 * k + 256], ACT.Copy)
            last.then_inc(S["bT"], 1)
            act.wait_ge(S["lgx"], 1)
            f(rt[2], rt[1], ACT.Exp).then_inc(S["lgx"], 1)
            act.wait_ge(S["gtr"], 1)
            act.wait_ge(S["x2T"], 3)
            f(gT, bank(1)[0:E, 0:TOK], ACT.Copy).then_inc(S["gT"], 1)
            act.wait_ge(S["accrd"], 1)

            def gathered(m):
                act.wait_ge(S["xg"], m + 1)
                f(xg, bank(0), ACT.Copy).then_inc(S["xgev"], 1)

            def item(n, m, e_next):
                act.wait_ge(S["hg"], n + 1)
                f(sg, hg, ACT.Sigmoid, scale=ALPHA).then_inc(S["sgm"], 1)
                act.wait_ge(S["pgt"], n + 1)
                f(pgT, bank(4)[0:CAP, 0:TOK], ACT.Copy).then_inc(S["pgtev"], 1)
                if e_next:
                    gathered(m + 1)
                act.wait_ge(S["used"], 6 * n + 6)
                f(yT, bank(3), ACT.Copy).then_inc(S["ytev"], 1)
                act.wait_ge(S["ytr"], n + 1)
                f(y, bank(4, 2)[0:CAP, :], ACT.Copy).then_inc(S["yev"], 1)

            gathered(0)
            with act.Fori(0, E) as e:
                item(e, e, True)
            act.wait_ge(S["overx"], 1)
            n_over = act.value_load(over[0:1, 0:1], min_val=0, max_val=MAX_OVER)
            with act.If(n_over > 0):
                with act.Fori(0, MAX_OVER) as i:
                    with act.If(n_over > i):
                        gathered(i + E + 1)
                        item(i + E, i + E + 1, False)
            act.wait_ge(S["fss"], 1)
            for t in range(TILES):
                last = f(bank(2 * t, 2), h[:, t, :], ACT.Square, accum_out=small[:, 40 + t:41 + t])
            last.then_inc(S["fss"], 1)
            act.wait_ge(S["frt"], 1)
            f(small[:, 46:49], small[:, 40:43], ACT.Sqrt).then_inc(S["frt"], 1)

        @block.vector
        def _(dve):
            v = nc.vector
            own = [0]

            def link(ins):
                own[0] += 1
                ins.then_inc(vlink, 1)
                dve.wait_ge(vlink, own[0])

            v.memset(xp[:, :, 0:3], 0.0)
            link(v.memset(sp[:, :, 0:2], 0.0))
            dve.wait_ge(S["ss"], 1)
            v.tensor_scalar(small[:, 40:45], small[:, 40:45], 1.0 / D, EPS, ALU.mult, ALU.add).then_inc(S["ss"], 1)
            dve.wait_ge(S["rt5"], 1)
            link(v.reciprocal(small[:, 52:57], small[:, 46:51]))
            for t in range(5):
                src, dst = (h[:, t, :], xs[:, t, :]) if t < 3 else (mem[:, t - 3, :], xs_mem[:, t - 3, :])
                v.tensor_scalar(dst, src, small[:, 52 + t:53 + t], None, ALU.mult).then_inc(S["xs"], 1)
            dve.wait_ge(S["vec_in"], 96)
            for t in range(5):
                dve.wait_ge(S["xtr"], t + 1)
                for k in range(2):
                    dst = xnT[:, 4 * k:4 * k + 4, t * P:(t + 1) * P] if t < 3 else mT[:, 4 * k:4 * k + 4, (t - 3) * P:(t - 2) * P]
                    c = 4 * k + (0 if t < 3 else 16)
                    last = v.tensor_tensor(dst, bank((2 * t + k) % 8).rearrange("p (t n) -> p t n", t=4),
                                           norms[:, c:c + 4].unsqueeze(2).to_broadcast([P, 4, P]), ALU.mult)
                last.then_inc(S["xT"], 1)
            dve.wait_ge(S["cwT"], 1)
            for c in range(NQKV):
                v.tensor_copy(xp[:, c, LP:WP].rearrange("p (s k) -> p s k", k=3 + LS)[:, :, 0:3],
                              cwv[:, c, 0:24].rearrange("p (s k) -> p s k", k=3))
            for c in range(2):
                last = v.tensor_copy(sp[:, c, SP2:WS].rearrange("p (s k) -> p s k", k=2 + LS)[:, :, 0:2],
                                     scwv[:, c, 0:16].rearrange("p (s k) -> p s k", k=2))
            link(last)
            dve.wait_ge(S["pjev"], 27)
            link(v.tensor_tensor(sp[:, :, 2:SP2], cT[:, :, 0:256], hT[:, :, 0:256], ALU.mult))
            for c in range(2):
                last = v.tensor_tensor(sp[:, c, SP2:WS].rearrange("p (s k) -> p s k", k=2 + LS)[:, :, 2:2 + LS],
                                       cT[:, c, 256:TOK].rearrange("p (s k) -> p s k", k=LS),
                                       hT[:, c, 256:TOK].rearrange("p (s k) -> p s k", k=LS), ALU.mult)
            link(last)
            for c in range(2):
                n = WS - 2
                link(v.tensor_scalar(conv_acc[:, 0:n], sp[:, c, 0:n], scwv[:, c, 16:17], None, ALU.mult))
                for j in range(1, 3):
                    link(v.scalar_tensor_tensor(out=conv_acc[:, 0:n], in0=sp[:, c, j:j + n], scalar=scwv[:, c, 16 + j:17 + j],
                                                in1=conv_acc[:, 0:n], op0=ALU.mult, op1=ALU.add))
                v.tensor_tensor(sbb[:, c, 0:256], sbb[:, c, 0:256], conv_acc[:, 0:256], ALU.mult)
                link(v.tensor_tensor(sbb[:, c, 256:TOK].rearrange("p (s k) -> p s k", k=LS),
                                     sbb[:, c, 256:TOK].rearrange("p (s k) -> p s k", k=LS),
                                     conv_acc[:, SP2:WS].rearrange("p (s k) -> p s k", k=2 + LS)[:, :, 0:LS], ALU.mult))
            for c in range(NQKV):
                n = WP - 3
                if c:
                    dve.wait_ge(S["silu"], c)
                link(v.tensor_scalar(conv_acc[:, 0:n], xp[:, c, 0:n], cwv[:, c, 24:25], None, ALU.mult))
                for j in range(1, 4):
                    ins = v.scalar_tensor_tensor(out=conv_acc[:, 0:n], in0=xp[:, c, j:j + n], scalar=cwv[:, c, 24 + j:25 + j],
                                                 in1=conv_acc[:, 0:n], op0=ALU.mult, op1=ALU.add)
                    if j < 3:
                        link(ins)
                ins.then_inc(S["conv"], 1)
            v.tensor_copy(cov[:, :, 0:3], xp[:, :, LP - 3:LP])
            for c in range(NQKV):
                last = v.tensor_copy(cov[:, c, 3:27].rearrange("p (s k) -> p s k", k=3),
                                     xp[:, c, LP:WP].rearrange("p (s k) -> p s k", k=3 + LS)[:, :, LS:LS + 3])
            last.then_inc(S["co"], 1)
            v.tensor_copy(scov[:, :, 0:2], sp[:, :, SP2 - 2:SP2])
            for c in range(2):
                last = v.tensor_copy(scov[:, c, 2:18].rearrange("p (s k) -> p s k", k=2),
                                     sp[:, c, SP2:WS].rearrange("p (s k) -> p s k", k=2 + LS)[:, :, LS:LS + 2])
            last.then_inc(S["co"], 1)
            for g in range(2):
                dve.wait_ge(S["nsum"], g + 1)
                if g:
                    dve.wait_ge(S["norm"], g)
                v.tensor_scalar(nr4, bank(0, 4).rearrange("p (c n) -> p c n", c=4)[:, :, 0:TOK], EPS, None,
                                ALU.add).then_inc(S["nadd"], 1)
                dve.wait_ge(S["nsqrt"], g + 1)
                link(v.reciprocal(nr4, nr4))
                v.scalar_tensor_tensor(out=qkv[:, 4 * g:4 * g + 4, :], in0=qkv[:, 4 * g:4 * g + 4, :],
                                       scalar=(float(P) ** -0.5 if g == 0 else 1.0), in1=nr4, op0=ALU.mult,
                                       op1=ALU.mult).then_inc(S["norm"], 1)
            lgt = small[:, 64:88].rearrange("p (a k) -> p a k", a=3)
            az = small[:, 192:204].rearrange("p (a k) -> p a k", a=3)
            link(v.tensor_tensor(az, lgt[:, :, 0:4], hb[:, 4:8].unsqueeze(1).to_broadcast([P, 3, 4]), ALU.add))
            v.tensor_copy(small[:, 88:100].rearrange("p (a k) -> p a k", a=3), lgt[:, :, 4:8])
            link(v.tensor_scalar(small[:, 112:124], small[:, 192:204], -1.0, None, ALU.mult))
            v.tensor_tensor(small[:, 112:124], small[:, 112:124], small[:, 192:204], ALU.max).then_inc(S["ab"], 1)
            dve.wait_ge(S["abx"], 1)
            v.tensor_scalar(small[:, 128:140], small[:, 128:140], 1.0, None, ALU.add).then_inc(S["ab"], 1)
            dve.wait_ge(S["abl"], 1)
            link(v.scalar_tensor_tensor(out=small[:, 192:204], in0=small[:, 192:204], scalar=0.0, in1=small[:, 128:140],
                                        op0=ALU.max, op1=ALU.add))
            gv = small[:, 0:36].rearrange("p (a k) -> p a k", a=3)
            v.scalar_tensor_tensor(out=gv[:, :, 0:4], in0=az, scalar=-1.0,
                                   in1=small[:, 108:112].unsqueeze(1).to_broadcast([P, 3, 4]), op0=ALU.mult, op1=ALU.mult)
            dve.wait_ge(S["abg"], 1)
            v.tensor_copy(gv[:, :, 4:8], small[:, 144:156].rearrange("p (a k) -> p a k", a=3)).then_inc(S["gates"], 1)
            dve.wait_ge(S["corout"], 32)
            link(v.memset(qm[:, :], 0.0))
            for s in range(NSEQ):
                last = v.tensor_copy(qmv[:, s, :, s * LS:(s + 1) * LS], mq[:, :, 256 + s * LS:256 + (s + 1) * LS])
            last.then_inc(S["qm"], 1)
            for t in range(TILES):
                dve.wait_ge(S["sc"], t + 1)
                link(v.tensor_reduce(small[:, 160:164], bank(2 * t, 2).rearrange("p (h m) -> p h m", h=4), AX.X, ALU.max))
                v.tensor_scalar(small[:, 160:164], small[:, 160:164], -0.125, None, ALU.mult).then_inc(S["soft"], 1)
                dve.wait_ge(S["pexp"], t + 1)
                link(v.reciprocal(small[:, 168:172], small[:, 164:168]))
                v.tensor_tensor(prob, prob, small[:, 168:172].unsqueeze(2).to_broadcast([P, 4, 256]), ALU.mult)\
                    .then_inc(S["pn"], 1)
            dve.wait_ge(S["gates"], 1)
            dve.wait_ge(S["ym"], 3)
            b3 = lambda x: x.unsqueeze(2).to_broadcast([P, HEADS, P])
            m3 = lambda x: x.unsqueeze(1).to_broadcast([P, HEADS, P])
            for t in range(TILES):
                cols = slice(t * P, (t + 1) * P)
                bv4 = lambda k: bank(k).rearrange("p (h n) -> p h n", h=HEADS)
                g = small[:, 12 * t:12 * t + 4]
                beta = small[:, 12 * t + 4:12 * t + 8]
                v.tensor_copy(gb, b3(g)).then_inc(S["gbr"], 1)
                dve.wait_ge(S["gcum"], t + 1)
                link(v.tensor_copy(small[:, 172:176], bank(0)[:, 0:4]))
                v.tensor_tensor(small[:, 176:180], bank(0)[:, 4:8], small[:, 172:176], ALU.subtract).then_inc(S["gex"], 1)
                dve.wait_ge(S["cumb"], t + 1)
                for hh in range(HEADS):
                    v.tensor_scalar(dTm[:, hh, :], bv4(1)[:, hh, :], small[:, 172 + hh:173 + hh], 0.0, ALU.subtract, ALU.min)
                    last = v.tensor_scalar(dec[:, hh, :], bv4(1)[:, hh, :], small[:, 172 + hh:173 + hh], 0.0, ALU.subtract, ALU.max)
                last.then_inc(S["dexp"], 1)
                dve.wait_ge(S["gex"], 2 * t + 2)
                link(v.tensor_tensor(small[:, 188:192], small[:, 180:184], beta, ALU.mult))
                dve.wait_ge(S["tok"], t + 1)
                v.tensor_tensor(bk, bv4(4), b3(small[:, 188:192]), ALU.mult)
                v.tensor_tensor(kd, bv4(4), b3(small[:, 184:188]), ALU.mult)
                v.tensor_tensor(bv, bv4(5), b3(beta), ALU.mult).then_inc(S["tokev"], 1)
                dve.wait_ge(S["dexp"], 3 * t + 3)
                dve.wait_ge(S["kk"], t + 1)
                link(v.tensor_tensor(dTm, dTm, m3(upto[t]), ALU.mult))
                v.tensor_tensor(qkT, bv4(3), dTm, ALU.mult)
                v.tensor_tensor(qd, qkv[:, 0:4, cols], eB, ALU.mult)
                link(v.tensor_tensor(dec, dec, b3(beta), ALU.mult))
                link(v.tensor_tensor(Am, bv4(2), dec, ALU.mult))
                link(v.tensor_tensor(Em, Am, m3(const("level1")), ALU.mult))
                v.tensor_tensor(Dm, m3(ident), Em, ALU.subtract).then_inc(S["lv"], 1)
                dve.wait_ge(S["lv"], LEVEL_STEPS[t] + 2 * t + 1)
                v.tensor_tensor(Em, Am, m3(const("level2")), ALU.mult).then_inc(S["dmul"], 1)
                dve.wait_ge(S["Fready"], t + 1)
                v.tensor_copy(Fm, bv4(6)).then_inc(S["lv"], 1)
                for n in range(1, len(tile_levels[t])):
                    k = LEVEL_STEPS[t] + n
                    last_level = n == len(tile_levels[t]) - 1
                    dve.wait_ge(S["Gready"], k)
                    v.tensor_tensor(Fm, Fm, bv4(6), ALU.subtract)
                    if not last_level:
                        v.tensor_tensor(Em, Am, m3(const(f"level{tile_levels[t][n + 1]}")), ALU.mult)
                    v.tensor_tensor(Dm, Dm, bv4(2), ALU.subtract).then_inc(S["lv"], 1)
                if t < 2:
                    for b in range(2):
                        k = 2 * t + b
                        dve.wait_ge(S["snew"], k + 1)
                        if k == 0:
                            v.tensor_copy(st[:, :, :], bv4(6)).then_inc(S["st_upd"], 1)
                        else:
                            for hh in range(HEADS):
                                last = v.scalar_tensor_tensor(out=st[:, hh, :], in0=st[:, hh, :],
                                                              scalar=eB[:, hh, 64 * b + 63:64 * b + 64],
                                                              in1=bv4(6 + b)[:, hh, :], op0=ALU.mult, op1=ALU.add)
                            last.then_inc(S["st_upd"], 1)
                    if t == 1:
                        dve.wait_ge(S["st_upd"], 4)
                        v.tensor_copy(small[:, 210:211], st[:, 0, 0:1]).then_inc(S["st_all"], 1)
                else:
                    dve.wait_ge(S["uev"], 5)
                    for hh in range(HEADS):
                        if hh:
                            dve.wait_ge(S["snew"], 4 + hh)
                        v.tensor_tensor(umask, um[:, hh, :].unsqueeze(1).to_broadcast([P, NSEQ, P]),
                                        const("seq").unsqueeze(2).to_broadcast([P, NSEQ, P]), ALU.mult).then_inc(S["um"], 1)
                        dve.wait_ge(S["snew"], 5 + hh)
                        for s in range(NSEQ):
                            c = s * LS + LS - 1
                            last = v.scalar_tensor_tensor(out=states[:, s, hh, :], in0=states[:, s, hh, :],
                                                          scalar=eB[:, hh, c:c + 1],
                                                          in1=bank(6 + s // 4)[:, (s % 4) * P:(s % 4 + 1) * P],
                                                          op0=ALU.mult, op1=ALU.add)
                        last.then_inc(S["st_upd"], 1)
                    dve.wait_ge(S["st_upd"], 8)
                    v.tensor_copy(small[:, 210:211], states[:, 0, 0, 0:1]).then_inc(S["st_all"], 1)
                dve.wait_ge(S["osum"], t + 1)
                v.tensor_scalar(osq, bv4(1), 1.0 / P, EPS, ALU.mult, ALU.add).then_inc(S["onorm"], 1)
                dve.wait_ge(S["onorm"], 2 * t + 2)
                link(v.reciprocal(osq, osq))
                link(v.scalar_tensor_tensor(out=oS, in0=oS, scalar=norms[:, 24:25], in1=osq, op0=ALU.mult, op1=ALU.mult))
                v.tensor_tensor(dg[:, :, cols], dg[:, :, cols], oS, ALU.mult).then_inc(S["yd"], 1)
            for k in range(24):
                half, c, b = k // 12, k // 3 % 4, k % 3
                dst = mg[:, 4 * half + c, :]
                dve.wait_ge(S["gsig"], k + 1)
                dve.wait_ge(S["gz"], k + 1)
                z = bank(2 * (k % 4) + 1)[:, 0:TOK]
                if b == 0:
                    ins = v.tensor_tensor(dst, sig[:, k % 4, :], z, ALU.mult)
                else:
                    link(v.tensor_tensor(sig[:, k % 4, :], sig[:, k % 4, :], z, ALU.mult))
                    dve.wait_ge(S["mrg"], k)
                    ins = v.tensor_tensor(dst, dst, sig[:, k % 4, :], ALU.add)
                ins.then_inc(S["mrg"], 1)
            for k in range(2):
                for a in range(TILES):
                    n = 3 * k + a
                    dve.wait_ge(S["wo"], n + 1)
                    v.tensor_tensor(h[:, a, 512 * k:512 * k + 512], h[:, a, 512 * k:512 * k + 512], bank(n),
                                    ALU.add).then_inc(S["hadd"], 1)
            dve.wait_ge(S["ss2"], 1)
            v.tensor_scalar(small[:, 40:43], small[:, 40:43], 1.0 / D, EPS, ALU.mult, ALU.add).then_inc(S["rt2"], 1)
            dve.wait_ge(S["rt2"], 2)
            dve.wait_ge(S["rout_in"], 48)
            link(v.reciprocal(small[:, 52:55], small[:, 46:49]))
            for a in range(TILES):
                v.scalar_tensor_tensor(out=x2[:, a, :], in0=h[:, a, :], scalar=small[:, 52 + a:53 + a], in1=w2b,
                                       op0=ALU.mult, op1=ALU.mult).then_inc(S["x2"], 1)
            for a in range(TILES):
                dve.wait_ge(S["x2tr"], a + 1)
                v.tensor_copy(x2T[:, :, a * P:(a + 1) * P], bank(2 * a, 2).rearrange("p (t n) -> p t n", t=KT8))\
                    .then_inc(S["x2T"], 1)
            dve.wait_ge(S["wo"], 6)
            link(v.tensor_copy(split[:, 0, :, :], x2))
            link(v.tensor_tensor(x2, x2, split[:, 0, :, :], ALU.subtract))
            link(v.tensor_copy(split[:, 1, :, :], x2))
            link(v.tensor_tensor(x2, x2, split[:, 1, :, :], ALU.subtract))
            link(v.tensor_copy(split[:, 2, :, :], x2))
            dve.wait_ge(S["lgm"], 1)
            link(v.tensor_tensor(lg, bank(7)[:, 0:3 * E].rearrange("p (a e) -> p a e", a=3),
                                 br.unsqueeze(1).to_broadcast([P, 3, E]), ALU.add))
            top = small[:, 216:240].rearrange("p (a k) -> p a k", a=3)
            for a in range(TILES):
                last = v.max(top[:, a, :], lg[:, a, :])
            link(last)
            be = lambda x: x.to_broadcast([P, 3, E])
            mask, t1, t2, t3, t4_, t5 = rt
            v.memset(t5, 0.0)
            v.tensor_tensor(mask, lg, be(top[:, :, 3:4]), ALU.is_gt)
            link(v.tensor_tensor(t3, lg, be(top[:, :, 3:4]), ALU.is_equal))
            v.tensor_reduce(small[:, 240:243], mask, AX.X, ALU.add)
            for a in range(TILES):
                last = v.tensor_tensor_scan(t4_[:, a, :], t3[:, a, :], t5[:, a, :], 0.0, ALU.add, ALU.add)
            link(last)
            link(v.tensor_scalar(small[:, 244:247], small[:, 240:243], -1.0, 4.0, ALU.mult, ALU.add))
            link(v.tensor_tensor(t4_, t4_, be(small[:, 244:247].unsqueeze(2)), ALU.is_le))
            link(v.tensor_tensor(t4_, t4_, t3, ALU.mult))
            link(v.tensor_tensor(mask, mask, t4_, ALU.add))
            v.tensor_tensor(t1, lg, be(top[:, :, 0:1]), ALU.subtract).then_inc(S["lgx"], 1)
            dve.wait_ge(S["lgx"], 2)
            link(v.tensor_tensor(t2, t2, mask, ALU.mult))
            link(v.tensor_reduce(small[:, 248:251], t2, AX.X, ALU.add))
            link(v.reciprocal(small[:, 252:255], small[:, 248:251]))
            v.memset(gate[:, :, E:E + 1], 0.0)
            v.memset(pos[:, :, E:E + 1], -1.0)
            v.tensor_tensor(gate[:, :, 0:E], t2, be(small[:, 252:255].unsqueeze(2)), ALU.mult).then_inc(S["sel"], 1)
            dve.wait_ge(S["posm"], 1)
            link(v.tensor_scalar(t1, bank(0)[:, 0:3 * E].rearrange("p (a e) -> p a e", a=3), 1.0, None, ALU.add))
            link(v.tensor_tensor(t1, t1, mask, ALU.mult))
            link(v.tensor_scalar(pos[:, :, 0:E], t1, -1.0, None, ALU.add))
            cnt = t2[:, 0, :]
            nb = t2[:, 1, :]
            end = t2[:, 2, :]
            link(v.tensor_copy(cnt, bank(0)[:, 3 * E:4 * E]))
            link(v.tensor_scalar(nb, cnt, float(CAP), None, ALU.is_gt))
            for r in range(2, 6):
                link(v.tensor_scalar(t3[:, 0, :], cnt, float(CAP * r), None, ALU.is_gt))
                link(v.tensor_tensor(nb, nb, t3[:, 0, :], ALU.add))
            link(v.tensor_tensor_scan(end, nb, t5[:, 0, :], 0.0, ALU.add, ALU.add))
            big = qm[:, 1024:1024 + MAX_OVER * E].rearrange("p (i e) -> p i e", i=MAX_OVER)
            lst = qm[:, 1800:1800 + 2 * MAX_OVER].rearrange("p (k i) -> p k i", k=2)
            link(v.tensor_tensor(big, const("rounds").unsqueeze(2).to_broadcast([P, MAX_OVER, E]),
                                 end.unsqueeze(1).to_broadcast([P, MAX_OVER, E]), ALU.is_ge))
            link(v.tensor_reduce(lst[:, 0, :], big, AX.X, ALU.add))
            link(v.tensor_tensor(big, big, nb.unsqueeze(1).to_broadcast([P, MAX_OVER, E]), ALU.mult))
            link(v.tensor_reduce(lst[:, 1, :], big, AX.X, ALU.add))
            link(v.tensor_tensor(lst[:, 1, :], const("rounds"), lst[:, 1, :], ALU.subtract))
            v.tensor_scalar(shift[:, :], lst[:, 1, :], 1.0, float(CAP), ALU.add, ALU.mult)
            v.tensor_scalar(over[0:1, 1:1 + MAX_OVER], lst[0:1, 0, :], float(E - 1), None, ALU.min)
            v.tensor_copy(over[0:1, 0:1], end[0:1, E - 1:E]).then_inc(S["overx"], 1)
            dve.wait_ge(S["bdm"], 1)
            dve.wait_ge(S["bT"], 1)
            for a in range(TILES):
                last = v.tensor_tensor(h[:, a, :], h[:, a, :], bank(2 + 2 * a, 2), ALU.add)
            last.then_inc(S["accrd"], 1)

            def place(e, position):
                v.tensor_tensor(onehot, const("slots").unsqueeze(1).to_broadcast([P, 3, CAP]),
                                position.to_broadcast([P, 3, CAP]), ALU.is_equal)
                link_p(v.tensor_tensor(onehot_g, const("slots").unsqueeze(1).to_broadcast([P, 3, CAP]),
                                       position.to_broadcast([P, 3, CAP]), ALU.is_equal))
                v.tensor_tensor(onehot_g, onehot_g, gate[:, :, bass.ds(e, 1)].to_broadcast([P, 3, CAP]),
                                ALU.mult).then_inc(S["P"], 1)

            state = {}

            def link_p(ins):
                ins.then_inc(plink, 1)
                dve.wait_ge(plink, state["p"])

            def item(n, e, e_next):
                biased = lambda b: b[:, bass.ds(e * 8, 8)].unsqueeze(2).to_broadcast([P, 8, CAP])
                c8 = lambda x: x.rearrange("p (f c) -> p f c", f=8)
                if e_next is not None:
                    dve.wait_ge(S["xg"], n + 1)
                    dve.wait_ge(S["pgt"], n + 1)
                    state["p"] = n + 2
                    place(e_next, pos[:, :, bass.ds(e_next, 1)])
                dve.wait_ge(S["used"], 6 * n + 2)
                v.tensor_tensor(c8(hg), c8(bank(1)), biased(bg), ALU.add).then_inc(mlink, 1)
                dve.wait_ge(mlink, 4 * n + 1)
                v.tensor_scalar(hg, hg, LIMIT, None, ALU.min).then_inc(S["hg"], 1)
                dve.wait_ge(S["sgm"], n + 1)
                v.tensor_tensor(sg, sg, hg, ALU.mult).then_inc(mlink, 1)
                dve.wait_ge(S["used"], 6 * n + 4)
                v.tensor_tensor(c8(hu), c8(bank(2)), biased(bu), ALU.add).then_inc(mlink, 1)
                dve.wait_ge(mlink, 4 * n + 3)
                v.tensor_scalar(hu, hu, -LIMIT, LIMIT, ALU.max, ALU.min).then_inc(mlink, 1)
                dve.wait_ge(mlink, 4 * n + 4)
                v.scalar_tensor_tensor(out=hTt, in0=hu, scalar=1.0, in1=sg, op0=ALU.add, op1=ALU.mult).then_inc(S["hh"], 1)
                dve.wait_ge(S["accrd"], 6 * n + 1)
                for a in range(TILES):
                    for k in range(2):
                        dve.wait_ge(S["acc"], 6 * n + 2 * a + k + 1)
                        o = h[:, a, 512 * k:512 * k + 512]
                        v.tensor_tensor(o, o, bank(6 + k), ALU.add).then_inc(S["accrd"], 1)

            state["p"] = 1
            place(0, pos[:, :, 0:1])
            with dve.Fori(0, E) as e:
                item(e, e, e + 1)
            n_over = dve.value_load(over[0:1, 0:1], min_val=0, max_val=MAX_OVER)
            with dve.If(n_over > 0):
                with dve.Fori(0, MAX_OVER) as i:
                    with dve.If(n_over > i):
                        expert = dve.value_load(over[0:1, bass.ds(i + 1, 1)], min_val=0, max_val=E - 1)
                        dve.wait_ge(S["xg"], i + E + 1)
                        dve.wait_ge(S["pgt"], i + E)
                        v.tensor_scalar(small[:, 216:219], pos[:, :, bass.ds(expert, 1)].rearrange("p a o -> p (a o)"),
                                        shift[:, bass.ds(i, 1)], None, ALU.subtract).then_inc(olink, 1)
                        dve.wait_ge(olink, i + 1)
                        state["p"] = i + E + 2
                        place(expert, small[:, 216:219].unsqueeze(2))
                        item(i + E, expert, None)
            v.memset(small[:, 210:211], 0.0).then_inc(S["fss"], 1)
            dve.wait_ge(S["fss"], 2)
            v.tensor_scalar(small[:, 40:43], small[:, 40:43], 1.0 / D, EPS, ALU.mult, ALU.add).then_inc(S["frt"], 1)
            dve.wait_ge(S["frt"], 2)
            dve.wait_ge(S["fw_in"], 16)
            link(v.reciprocal(small[:, 52:55], small[:, 46:49]))
            for t in range(TILES):
                if t == 2:
                    dve.wait_ge(S["fout"], 32)
                v.scalar_tensor_tensor(out=outb[:, t % 2, :], in0=h[:, t, :], scalar=small[:, 52 + t:53 + t], in1=fw,
                                       op0=ALU.mult, op1=ALU.mult).then_inc(S["fo"], 1)


_INS = ['x_prompt', 'x_sample', 'mem_prompt', 'state_dn', 'state_dn_conv', 'state_sc_conv', 'cache_mem_k', 'cache_mem_v',
        'w_in', 'dn_conv_w', 'dn_A_log', 'dn_dt_bias', 'dn_norm_w', 'sc_conv_w', 'mem_norm_w', 'w_mem_kv', 'w_br', 'w_o',
        'norm1_w', 'norm2_w', 'w_router', 'b_router', 'w_gate', 'b_gate', 'w_up', 'b_up', 'w_down', 'b_down',
        'final_norm_w']
_OUTS = [(1, 256, 1024), (8, 16, 1024), (1, 1, 4, 128, 128), (1, 1, 3, 1536), (1, 1, 2, 256), (1, 1, 256, 4, 64),
         (1, 1, 256, 4, 64), (1, 8, 4, 128, 128), (1, 8, 3, 1536), (1, 8, 2, 256)]


def kernel(**inputs):
    import concourse.bacc as _bacc
    from concourse.bass_utils import run_bass_kernel_spmd as _run

    nc = _bacc.Bacc("TRN2", target_bir_lowering=False, num_devices=1)
    arrays, aps = {}, {}
    for name in _INS:
        a = np.ascontiguousarray(inputs[name])
        arrays[f"in_{name}_dram"] = a
        aps[name] = nc.dram_tensor(f"in_{name}_dram", a.shape, mybir.dt.from_np(a.dtype), kind="ExternalInput").ap()
    arrays["in_consts_dram"] = constant_table()
    aps["consts"] = nc.dram_tensor("in_consts_dram", (P, CONST_WIDTH), F32, kind="ExternalInput").ap()
    for i, shape in enumerate(_OUTS):
        aps[f"out_{i}"] = nc.dram_tensor(f"out_{i}_dram", shape, F32, kind="ExternalOutput").ap()
    build(nc, aps)
    r = _run(nc, [arrays], core_ids=[0])
    return tuple(r.results[0][f"out_{i}_dram"] for i in range(len(_OUTS)))
```

```python
from contextlib import ExitStack

import concourse.bass as bass
import numpy as np
from concourse import mybir

P = 128
F32 = mybir.dt.float32
F32R = mybir.dt.float32r
BF16 = mybir.dt.bfloat16
I32 = mybir.dt.int32
ALU = mybir.AluOpType
ACT = mybir.ActivationFunctionType
AX = mybir.AxisListType

EPS = 1e-6
HEADS = 4
CAP = 64
LIMIT = 7.0
ALPHA = 1.702
LEVELS = (1, 2, 4, 8, 16, 32)

CONST_COLS = {}
_at = 0
for _name, _n in (
    ("ident", P), ("ones", P), ("upto_prompt", P), ("upto_sample", P), ("block_prompt", P), ("block_sample", P),
    ("before", P), *((f"level{s}", P) for s in LEVELS), ("seq", 8), ("slots2", 2 * CAP), ("fold", CAP), ("rounds", 24),
):
    CONST_COLS[_name] = (_at, _n)
    _at += _n
CONST_WIDTH = _at


def constant_table():
    i = np.arange(P)[:, None]
    j = np.arange(P)[None, :]
    table = np.zeros((P, CONST_WIDTH), np.float32)

    def put(name, value):
        a, n = CONST_COLS[name]
        table[:, a:a + n] = value

    put("ident", i == j)
    put("ones", 1.0)
    for name, block in (("prompt", 64), ("sample", 16)):
        put(f"upto_{name}", (i // block == j // block) & (i <= j))
        put(f"block_{name}", i // block == j // block)
    put("before", i < j)
    for s in LEVELS:
        put(f"level{s}", (i // (2 * s) == j // (2 * s)) & (i // s % 2 == 1) & (j // s % 2 == 0))
    put("seq", i // 16 == np.arange(8)[None, :])
    put("slots2", np.arange(2 * CAP)[None, :] % CAP)
    put("rounds", np.arange(24)[None, :])
    put("fold", i % CAP == np.arange(CAP)[None, :])
    return table


def build(nc, A):
    D = A["x_prompt"].shape[2]
    KT8 = D // P
    E = A["w_router"].shape[2]
    TILES = 3
    TOK = TILES * P
    NSEQ = A["x_sample"].shape[0]
    LS = A["x_sample"].shape[1]
    MAX_OVER = TOK * 4 // CAP
    NQKV = 12
    LP = 3 + 256
    WP = LP + NSEQ * (3 + LS)
    SP2 = 2 + 256
    WS = SP2 + NSEQ * (2 + LS)
    TRUNK_PIECES = 17
    LAST_TRUNK = [max(n for n in range(TRUNK_PIECES) if n % 4 == s) for s in range(4)]

    ctx = ExitStack()
    with ctx:
        def sb(name, shape, dt=F32):
            return ctx.enter_context(nc.sbuf_tensor("sb_" + name, shape, dt))

        def sem(name):
            return ctx.enter_context(nc.semaphore("s_" + name))

        slab_words = 53056
        slab_at = (nc.sbuf_base + 31) // 32 * 32
        sb("slab", [P, slab_words])
        at = {}
        cursor = [0]

        def lay(name, shape, dt=F32, over=None, skip=0):
            words = int(np.prod(shape[1:]))
            words = (words + 7) // 8 * 8
            if over is None:
                at[name] = cursor[0]
                cursor[0] += words
                assert cursor[0] <= slab_words, (name, cursor[0])
            else:
                at[name] = at[over] + skip
            return nc.alloc_sbuf_tensor_at("sb_" + name, shape, dt, offset=slab_at + 4 * at[name])

        ring = lay("ring", [P, 6, 4096])
        h = lay("h", [P, TILES, D])
        r1 = lay("r1", [P, NQKV * WP])
        xn = lay("xn", [P, 3072])
        rq = lay("rq", [P, 4608])
        dg = lay("dg", [P, HEADS, TOK])
        sbb = lay("sbb", [P, 2, TOK])
        sp = lay("sp", [P, 2, WS])
        qm = lay("qm", [P, 2048])
        kvp = lay("kvp", [P, 2, 512])
        wk = lay("wk", [P, 2048])
        mq = lay("mq", [P, 2, TOK])
        st = lay("st", [P, HEADS, P])
        cw = lay("cw", [P, 12 * 28 + 2 * 19])
        co = lay("co", [P, 12 * 27 + 2 * 18])
        scor = lay("scor", [18, 256])
        cst = lay("cst", [P, CONST_WIDTH])
        wab = lay("wab", [P, KT8, 8])
        norms = lay("norms", [P, 3 * KT8 + 1])
        hb = lay("hb", [P, 8])
        small = lay("small", [P, 256])
        over = lay("over", [1, 1 + MAX_OVER], I32)
        pos = lay("pos", [P, 3, E], over="scor")
        gate = lay("gate", [P, 3, E], over="scor", skip=96)
        shift = lay("shift", [P, MAX_OVER], over="scor", skip=192)
        w_hi = [lay(f"w_hi{k}", [P, 2048], F32R, over="dg", skip=2048 * k) for k in range(2)]
        w_lo = [lay(f"w_lo{k}", [P, 2048], F32R, over="dg", skip=4096 + 2048 * k) for k in range(2)]
        assert at["dg"] + 8192 <= at["mq"]
        xparts = lay("xparts", [P, KT8, P], F32R, over="r1")
        hparts = lay("hparts", [P, 8, P], F32R, over="r1", skip=1024)
        g_sb = lay("g_sb", [P, 1024], over="r1", skip=2048)
        u_sb = lay("u_sb", [P, 1024], over="r1", skip=3072)
        y_sb = lay("y_sb", [P, 1024], over="r1", skip=4096)
        hg = lay("hg", [P, 512], over="r1", skip=5120)
        hu = lay("hu", [P, 512], over="r1", skip=5632)
        sg = lay("sg", [P, 512], over="r1", skip=6144)
        pgT = lay("pgT", [P, TOK], over="r1", skip=6656)
        onehot = lay("onehot", [P, 3, 2, CAP], BF16, over="r1", skip=7040)
        onehot_g = lay("onehot_g", [P, 3, 2, CAP], over="r1", skip=7232)
        assert at["r1"] + 7616 <= at["rq"]
        fw = lay("fw", [P, 1024], over="st")
        outb = lay("outb", [P, 2, 1024], over="r1", skip=2048)
        assert at["st"] + 1024 <= at["scor"]

        ps = ctx.enter_context(nc.psum_tensor("ps", [P, 8 * 512], F32))

        def bank(b, n=1):
            return ps[:, b * 512:(b + n) * 512]

        def const(name):
            a, n = CONST_COLS[name]
            return cst[:, a:a + n]

        ident = const("ident")
        ones = const("ones")

        def piece(slot):
            return ring[:, slot, :].rearrange("p (t n) -> p t n", t=KT8)

        rd = ring[:, 4:6, :].rearrange("p a n -> p (a n)")
        mem = rd[:, 0:2048].rearrange("p (a n) -> p a n", a=2)
        xs_mem = rd[:, 2048:4096].rearrange("p (a n) -> p a n", a=2)
        mT = rd[:, 4096:6144].rearrange("p (t n) -> p t n", t=KT8)
        xs = rq[:, 0:3072].rearrange("p (a n) -> p a n", a=3)
        cwr = rq[0:28, 3072:4608]
        scr = dg[0:19, 0, 0:256]
        xnT = xn[:, :].rearrange("p (t n) -> p t n", t=KT8)
        xp = r1[:, :].rearrange("p (c n) -> p c n", c=NQKV)
        qkv = rq[:, :].rearrange("p (c n) -> p c n", c=NQKV)
        cwv = cw[:, 0:336].rearrange("p (c n) -> p c n", n=28)
        scwv = cw[:, 336:374].rearrange("p (c n) -> p c n", n=19)
        cov = co[:, 0:324].rearrange("p (c n) -> p c n", n=27)
        scov = co[:, 324:360].rearrange("p (c n) -> p c n", n=18)
        conv_acc = wk[:, 0:WP]
        cT = wk[:, 512:1280].rearrange("p (c n) -> p c n", c=2)
        hT = wk[:, 1280:2048].rearrange("p (c n) -> p c n", c=2)
        sq4 = r1[:, 0:1536].rearrange("p (c n) -> p c n", c=4)
        nr4 = r1[:, 1536:3072].rearrange("p (c n) -> p c n", c=4)
        cor = qm[0:27, 0:1536]
        kc = rd[:, 0:4096].rearrange("p (s m n) -> p s m n", s=NSEQ, m=2)
        vc = rd[:, 4096:8192].rearrange("p (s m n) -> p s m n", s=NSEQ, m=2)
        kT = r1[:, 0:4608].rearrange("p (b s m) -> p b s m", b=2, s=9)
        qmv = qm[:, :].rearrange("p (s b n) -> p s b n", s=NSEQ, b=2)
        prob = wk[:, 0:1024].rearrange("p (h m) -> p h m", h=4)
        probT = wk[:, 1024:2048].rearrange("p (c n) -> p c n", c=8)
        states = rd[:, 0:4096].rearrange("p (s h v) -> p s h v", s=NSEQ, h=HEADS)

        def t4(region, k):
            return region[:, k * 512:(k + 1) * 512].rearrange("p (h n) -> p h n", h=HEADS)

        gb, dTm, dec, eB, Am, Dm, Fm, Ym, Em = (t4(r1, k) for k in range(9))
        qkT, qd, bk, kd, bv, nwk, um, uT = (t4(rd, 8 + k) for k in range(8))
        oS, osq = t4(wk, 0), t4(wk, 1)
        umask = wk[:, 1024:2048].rearrange("p (s v) -> p s v", s=NSEQ)
        mg = rq[:, 0:3072].rearrange("p (t n) -> p t n", t=KT8)
        sig = wk[:, 0:1536].rearrange("p (a n) -> p a n", a=4)
        x2 = xn[:, :].rearrange("p (a n) -> p a n", a=3)
        x2T = r1[:, 0:3072].rearrange("p (t n) -> p t n", t=KT8)
        w2b = r1[:, 3072:4096]
        split = rq[:, :].bitcast(BF16).rearrange("p (k a n) -> p k a n", k=3, a=3)
        wr = qm[:, 0:256].rearrange("p (t e) -> p t e", t=KT8)
        br = qm[:, 256:256 + E]
        lg = qm[:, 288:384].rearrange("p (a e) -> p a e", a=3)
        rt = [qm[:, 384 + 96 * k:480 + 96 * k].rearrange("p (a e) -> p a e", a=3) for k in range(6)]
        bg = mq[:, 0, 0:256]
        bu = mq[:, 1, 0:256]
        gT = dg[0:E, 3, :]
        bd = dg[0:E, :, :].rearrange("p a n -> p (a n)")[:, 0:D]
        brow = wk[:, 0:512].rearrange("p (b r n) -> p b r n", b=2, r=2)
        halves = 4

        def stream(kind, n):
            if isinstance(n, int) and n < E:
                return {"gate": max(12 * n - 4, 0), "up": 12 * n + 4, "down": 12 * n + (12 if n < E - 1 else 8)}[kind]
            return {"gate": 12 * n - 4, "up": 12 * n + 4, "down": 12 * n + 12}[kind]

        def stream_over(kind, n):
            return 12 * n + {"gate": 0, "up": 4, "down": 8}[kind]

        MATS = ("gate", "up", "down")

        names = """cst x_in mem_in rows_in vec_in wab_in kc_in vc_in st_in rout_in bdn_in
            ss rt5 rs5 xs xtr xT cwtr cwT wabstep pj pjev pads conv silu sc_in sc_done
            sq nsum nadd nsqrt norm co cotr cor kv_out corout
            ktr kT qm sc soft pexp pn ptr pT pv ym
            gates gcum gex gbr cumb dexp dmul kk kkev tok tokev lv Fready Yready Gready wkt nwk u uev utr uready oT oev osum onorm snew st_upd um yd st_all
            ab abx abl abg
            gp gz gsig mrg wo hadd ss2 rt2 x2 x2tr x2T lgm lgx sel posm posx brt bT gtr gT bdm  overx
            P Pg xg xhi xlo gev gT2 hg sgm uout uT2 hf hhi hlo yev pgt pgtev acc accrd hi lo used
            fw_in fss frt fo fout out tabs""".split()
        S = {n: sem(n) for n in dict.fromkeys(names)}
        loaded = [sem(f"loaded{k}") for k in range(6)]
        vlink, plink, mlink, olink = sem("vlink"), sem("plink"), sem("mlink"), sem("olink")

        block = ctx.enter_context(nc.Block())

        win = A["w_in"][0].rearrange("(p t) n -> p t n", t=KT8)
        wbr = A["w_br"][0].rearrange("(k p) n -> p k n", p=P)
        wo = A["w_o"][0].rearrange("(k p) n -> p k n", p=P)
        gcol = 3080
        trunk = [A["w_mem_kv"][0].rearrange("(p t) n -> p t n", t=KT8)]
        trunk += [win[:, :, c:c + 512] for c in (0, 512, 1024, 1544, 2056, 2568)]
        for half in range(2):
            trunk += [win[:, :, gcol + 1024 * b + 512 * half:gcol + 1024 * b + 512 * half + 512] for b in range(3)]
            trunk += [wbr[:, :, 512 * half:512 * half + 512]]
        trunk += [wo[:, :, 512 * k:512 * k + 512] for k in range(2)]
        assert len(trunk) == TRUNK_PIECES
        wg = A["w_gate"][0].rearrange("e (p t) n -> e p t n", t=KT8)
        wu = A["w_up"][0].rearrange("e (p t) n -> e p t n", t=KT8)
        wd = A["w_down"][0].rearrange("e (f p) n -> e p f n", p=P)

        x_s = A["x_sample"].rearrange("s l d -> (s l) d")
        outs = [A[f"out_{k}"] for k in range(10)]
        yp = outs[0][0].rearrange("(a p) d -> a p d", p=P)
        ys = outs[1].rearrange("s l d -> (s l) d")

        @block.sync
        def _(sp_):
            dma = sp_.dma_start

            def through(n):
                if n < 7:
                    sp_.wait_ge(S["pj"], 2 + 4 * n + (1 if n >= 4 else 0))
                elif n < 15:
                    sp_.wait_ge(S["gz"], 12 if n < 11 else 24)
                else:
                    sp_.wait_ge(S["wo"], 3 * (n - 14))

            def trunk_piece(n):
                if n >= 4:
                    through(n - 4)
                dma(piece(n % 4), trunk[n]).then_inc(loaded[n % 4], 16)

            dma(h[:, 0:2, :], A["x_prompt"][0].rearrange("(a p) d -> p a d", p=P)).then_inc(S["x_in"], 16)
            dma(h[:, 2, :], x_s).then_inc(S["x_in"], 16)
            dma(cst[:, :], A["consts"]).then_inc(S["cst"], 16)
            dma(mem, A["mem_prompt"][0].rearrange("(a p) d -> p a d", p=P)).then_inc(S["mem_in"], 16)
            trunk_piece(0)
            dma(cwr[0:24, :], A["state_dn_conv"][0].rearrange("s r c -> (s r) c")).then_inc(S["rows_in"], 16)
            dma(cwr[24:28, :], A["dn_conv_w"][0]).then_inc(S["rows_in"], 16)
            dma(scr[0:16, :], A["state_sc_conv"][0].rearrange("s r c -> (s r) c")).then_inc(S["rows_in"], 16)
            dma(scr[16:19, :], A["sc_conv_w"][0]).then_inc(S["rows_in"], 16)
            for k, name in enumerate(("norm1_w", "norm2_w", "mem_norm_w")):
                dma(norms[:, k * KT8:(k + 1) * KT8], A[name][0].rearrange("(p t) -> p t", t=KT8)).then_inc(S["vec_in"], 16)
            dma(norms[:, 24:25], A["dn_norm_w"][0].rearrange("(p o) -> p o", o=1)).then_inc(S["vec_in"], 16)
            dma(hb[:, 0:4], A["dn_A_log"].partition_broadcast(P).rearrange("p o h -> p (o h)")).then_inc(S["vec_in"], 16)
            dma(hb[:, 4:8], A["dn_dt_bias"].partition_broadcast(P).rearrange("p o h -> p (o h)")).then_inc(S["vec_in"], 16)
            trunk_piece(1)
            trunk_piece(2)
            trunk_piece(3)
            dma(wab[:, :, :], win[:, :, 1536:1544]).then_inc(S["wab_in"], 16)
            trunk_piece(4)
            sp_.wait_ge(S["pjev"], 2)
            for k in range(2):
                dma(outs[5 + k][0, 0].rearrange("(a p) h d -> p a (h d)", p=P),
                    kvp[:, :, 256 * k:256 * k + 256]).then_inc(S["kv_out"], 16)
            dma(kc, A["cache_mem_k"][0].rearrange("s (m p) h d -> p s m (h d)", p=P)).then_inc(S["kc_in"], 16)
            dma(vc, A["cache_mem_v"][0].rearrange("s (m p) h d -> p s m (h d)", p=P)).then_inc(S["vc_in"], 16)
            for n in range(5, 10):
                trunk_piece(n)
            sp_.wait_ge(S["cor"], 4)
            dma(outs[3][0, 0], cor[0:3, :]).then_inc(S["corout"], 16)
            dma(outs[8][0].rearrange("s r c -> (s r) c"), cor[3:27, :]).then_inc(S["corout"], 16)
            dma(outs[4][0, 0], scor[0:2, :]).then_inc(S["out"], 16)
            dma(outs[9][0].rearrange("s r c -> (s r) c"), scor[2:18, :]).then_inc(S["out"], 16)
            sp_.wait_ge(S["ktr"], 9)
            dma(states, A["state_dn"][0].rearrange("s h k v -> k s h v")).then_inc(S["st_in"], 16)
            sp_.wait_ge(S["st_all"], 1)
            dma(outs[2][0, 0].rearrange("h k v -> k h v"), st[:, :, :]).then_inc(S["out"], 16)
            sp_.wait_ge(S["st_all"], 2)
            dma(outs[7][0].rearrange("s h k v -> k s h v"), states).then_inc(S["out"], 16)
            for n in range(10, TRUNK_PIECES):
                trunk_piece(n)
            sp_.wait_ge(S["ym"], 3)
            dma(wr, A["w_router"][0].rearrange("(p t) e -> p t e", t=KT8)).then_inc(S["rout_in"], 16)
            dma(br, A["b_router"].partition_broadcast(P).rearrange("p o e -> p (o e)")).then_inc(S["rout_in"], 16)
            sp_.wait_ge(S["mrg"], 24)
            dma(w2b, A["norm2_w"].partition_broadcast(P).rearrange("p o d -> p (o d)")).then_inc(S["rout_in"], 16)
            dma(bd, A["b_down"][0]).then_inc(S["bdn_in"], 16)
            for k, name in enumerate(("b_gate", "b_up")):
                dma(brow[:, k, :, :], A[name][0].rearrange("(r e) (f p) -> (e f) r p", r=2, p=P)).then_inc(S["bdn_in"], 16)

            weights = {"gate": wg, "up": wu, "down": wd}

            def matrix(kind, expert, free=None):
                for k in range(2):
                    if free is not None:
                        sp_.wait_ge(S["lo"], free + 2 * k)
                    s = 2 * MATS.index(kind) + k
                    src = weights[kind][bass.ds(expert, 1), :, 4 * k:4 * k + 4, :]
                    dma(ring[:, s, :], src.rearrange("e p t n -> p (e t) n")).then_inc(loaded[s], 16)

            through(LAST_TRUNK[0])
            through(LAST_TRUNK[1])
            matrix("gate", 0)
            through(LAST_TRUNK[2])
            through(LAST_TRUNK[3])
            matrix("up", 0)
            sp_.wait_ge(S["out"], 64)
            matrix("down", 0)
            sp_.wait_ge(S["accrd"], 1)
            dma(fw[:, :], A["final_norm_w"].partition_broadcast(P)).then_inc(S["fw_in"], 16)
            matrix("gate", 1, stream("gate", 0) + 2)
            matrix("up", 1, stream("up", 0) + 2)
            with sp_.Fori(1, E - 1) as e:
                matrix("gate", e + 1, stream("gate", e) + 2)
                matrix("down", e, stream("down", e - 1) + 2)
                matrix("up", e + 1, stream("up", e) + 2)
            matrix("down", E - 1, stream("down", E - 2) + 2)
            sp_.wait_ge(S["overx"], 1)
            n_over = sp_.value_load(over[0:1, 0:1], min_val=0, max_val=MAX_OVER)
            with sp_.If(n_over > 0):
                with sp_.Fori(0, MAX_OVER) as i:
                    with sp_.If(n_over > i):
                        expert = sp_.value_load(over[0:1, bass.ds(i + 1, 1)], min_val=0, max_val=E - 1)
                        for kind in MATS:
                            matrix(kind, expert, stream_over(kind, i + E - 1) + 2)
            for t in range(TILES):
                sp_.wait_ge(S["fo"], t + 1)
                dma(yp[t] if t < 2 else ys, outb[:, t % 2, :]).then_inc(S["fout"], 16)
            sp_.wait_ge(S["fout"], 48)
            sp_.wait_ge(S["out"], 64)
            sp_.wait_ge(S["kv_out"], 32)
            sp_.wait_ge(S["corout"], 32)

        upto = [const("upto_prompt"), const("upto_prompt"), const("upto_sample")]
        blockones = [const("block_prompt"), const("block_prompt"), const("block_sample")]
        tile_levels = [LEVELS, LEVELS, LEVELS[:4]]
        LEVEL_STEPS = [sum(len(tile_levels[u]) - 1 for u in range(t)) for t in range(TILES + 1)]

        @block.tensor
        def _(pe):
            mm = nc.tensor.matmul

            def tr(out, in_, n=P):
                return nc.tensor.transpose(out, in_, ident[0:n, 0:n])

            pe.wait_ge(S["cst"], 16)
            for t in range(5):
                pe.wait_ge(S["xs"], t + 1)
                if t >= 4:
                    pe.wait_ge(S["xT"], t - 3)
                src = xs[:, t, :] if t < 3 else xs_mem[:, t - 3, :]
                for k in range(KT8):
                    last = tr(bank((2 * t + k // 4) % 8)[:, (k % 4) * P:(k % 4 + 1) * P], src[:, k::KT8])
                last.then_inc(S["xtr"], 1)
            pe.wait_ge(S["rows_in"], 64)
            pe.wait_ge(S["xT"], 2)
            for c in range(12):
                tr(bank(2)[:, c * 28:(c + 1) * 28], cwr[:, c * P:(c + 1) * P], 28)
            for c in range(2):
                last = tr(bank(2)[:, 336 + c * 19:336 + (c + 1) * 19], scr[:, c * P:(c + 1) * P], 19)
            last.then_inc(S["cwtr"], 1)

            def step_start(q):
                if q >= 8:
                    pe.wait_ge(S["pjev"], q - 7)

            pe.wait_ge(S["xT"], 5)
            pe.wait_ge(S["cwT"], 1)
            pe.wait_ge(loaded[0], 16)
            for q in range(2):
                for t in range(KT8):
                    last = mm(bank(q), mT[:, t, q * P:(q + 1) * P], piece(0)[:, t, :], start=(t == 0), stop=(t == KT8 - 1))
                last.then_inc(S["pj"], 1)

            q = 2
            for n in range(1, 7):
                pe.wait_ge(loaded[n % 4], 16 * (n // 4 + 1))
                if n == 4:
                    pe.wait_ge(S["wab_in"], 16)
                    step_start(q)
                    for a in range(TILES):
                        for t in range(KT8):
                            last = mm(bank(q % 8)[:, a * 8:(a + 1) * 8], xnT[:, t, a * P:(a + 1) * P], wab[:, t, :],
                                      start=(t == 0), stop=(t == KT8 - 1))
                    last.then_inc(S["pj"], 1)
                    q += 1
                for c in range(4):
                    step_start(q)
                    for t in range(KT8):
                        last = mm(bank(q % 8)[:, 0:TOK], piece(n % 4)[:, t, c * P:(c + 1) * P], xnT[:, t, :],
                                  start=(t == 0), stop=(t == KT8 - 1))
                    last.then_inc(S["pj"], 1)
                    q += 1
            assert q == 27

            pe.wait_ge(S["pjev"], 27)
            for g in range(2):
                pe.wait_ge(S["sq"], g + 1)
                if g:
                    pe.wait_ge(S["nadd"], g)
                for c in range(4):
                    last = mm(bank(c)[:, 0:TOK], ones, sq4[:, c, :], start=True, stop=True)
                last.then_inc(S["nsum"], 1)
            pe.wait_ge(S["co"], 2)
            for c in range(12):
                last = tr(bank(4 + c // 4)[0:27, (c % 4) * P:(c % 4 + 1) * P], cov[:, c, :])
                if c % 4 == 3:
                    last.then_inc(S["cotr"], 1)
            for c in range(2):
                last = tr(bank(7)[0:18, c * P:(c + 1) * P], scov[:, c, :])
            last.then_inc(S["cotr"], 1)

            pe.wait_ge(S["kc_in"], 16)
            pe.wait_ge(S["nadd"], 2)
            pe.wait_ge(S["cor"], 4)
            for s in range(9):
                if s >= 8:
                    pe.wait_ge(S["kT"], s - 7)
                for b in range(2):
                    for m in range(2):
                        src = kc[:, s, m, b * P:(b + 1) * P] if s < 8 else kvp[:, m, b * P:(b + 1) * P]
                        last = tr(bank(s % 8)[:, (2 * b + m) * P:(2 * b + m + 1) * P], src)
                last.then_inc(S["ktr"], 1)
            pe.wait_ge(S["kT"], 9)
            pe.wait_ge(S["qm"], 1)
            pe.wait_ge(S["vc_in"], 16)
            for t in range(TILES):
                if t >= 1:
                    pe.wait_ge(S["ym"], t)
                for hh in range(4):
                    o = bank(2 * t + hh % 2)[:, (hh // 2) * 256:(hh // 2) * 256 + 256]
                    rows = slice(64 * (hh % 2), 64 * (hh % 2) + 64)
                    if t < 2:
                        last = mm(o, mq[rows, hh // 2, t * P:(t + 1) * P], kT[rows, hh // 2, 8, :], start=True, stop=True)
                    else:
                        for s in range(NSEQ):
                            last = mm(o, qmv[rows, s, hh // 2, :], kT[rows, hh // 2, s, :], start=(s == 0), stop=(s == NSEQ - 1))
                last.then_inc(S["sc"], 1)
                pe.wait_ge(S["pn"], t + 1)
                for hh in range(4):
                    for m in range(2):
                        k = 2 * hh + m
                        last = tr(bank(6 + k // 4)[:, (k % 4) * P:(k % 4 + 1) * P],
                                  prob[:, 2 * (hh % 2) + hh // 2, m * P:(m + 1) * P])
                last.then_inc(S["ptr"], 1)
                pe.wait_ge(S["pT"], t + 1)
                for hh in range(4):
                    rows = slice(64 * (hh % 2), 64 * (hh % 2) + 64)
                    o = bank(2 * t)[rows, (hh // 2) * P:(hh // 2 + 1) * P]
                    if t < 2:
                        for m in range(2):
                            last = mm(o, kvp[:, m, 256 + 64 * hh:320 + 64 * hh], probT[:, 2 * hh + m, :],
                                      start=(m == 0), stop=(m == 1))
                    else:
                        for s in range(NSEQ):
                            for m in range(2):
                                last = mm(o[:, s * LS:(s + 1) * LS], vc[:, s, m, 64 * hh:64 * hh + 64],
                                          probT[:, 2 * hh + m, s * LS:(s + 1) * LS], start=(m == 0), stop=(m == 1))
                last.then_inc(S["pv"], 1)

            pe.wait_ge(S["norm"], 2)
            pe.wait_ge(S["gates"], 1)
            pe.wait_ge(S["ym"], 3)
            for t in range(TILES):
                cols = slice(t * P, (t + 1) * P)
                if t >= 1:
                    pe.wait_ge(S["yd"], t)
                mm(bank(0)[:, 0:4], upto[t], small[:, 12 * t:12 * t + 4], start=True, stop=True)
                mm(bank(0)[:, 4:8], blockones[t], small[:, 12 * t:12 * t + 4], start=True, stop=True).then_inc(S["gcum"], 1)
                pe.wait_ge(S["gbr"], t + 1)
                for hh in range(HEADS):
                    last = mm(bank(1)[:, hh * P:(hh + 1) * P], gb[:, hh, :], upto[t], start=True, stop=True)
                last.then_inc(S["cumb"], 1)
                for hh in range(HEADS):
                    mm(bank(2)[:, hh * P:(hh + 1) * P], qkv[:, 4 + hh, cols], qkv[:, 4 + hh, cols], start=True, stop=True)
                    last = mm(bank(3)[:, hh * P:(hh + 1) * P], qkv[:, 4 + hh, cols], qkv[:, hh, cols], start=True, stop=True)
                last.then_inc(S["kk"], 1)
                for hh in range(HEADS):
                    tr(bank(4)[:, hh * P:(hh + 1) * P], qkv[:, 4 + hh, cols])
                    last = tr(bank(5)[:, hh * P:(hh + 1) * P], qkv[:, 8 + hh, cols])
                last.then_inc(S["tok"], 1)
                pe.wait_ge(S["lv"], LEVEL_STEPS[t] + 2 * t + 1)
                for hh in range(HEADS):
                    last = tr(bank(6)[:, hh * P:(hh + 1) * P], Dm[:, hh, :])
                last.then_inc(S["Fready"], 1)
                for n in range(1, len(tile_levels[t])):
                    k = LEVEL_STEPS[t] + n
                    pe.wait_ge(S["lv"], k + 2 * t + 1)
                    for hh in range(HEADS):
                        last = mm(bank(7)[:, hh * P:(hh + 1) * P], Em[:, hh, :], Fm[:, hh, :], start=True, stop=True)
                    last.then_inc(S["Yready"], 1)
                    pe.wait_ge(S["uready"], k)
                    for hh in range(HEADS):
                        mm(bank(6)[:, hh * P:(hh + 1) * P], Dm[:, hh, :], Ym[:, hh, :], start=True, stop=True)
                        last = mm(bank(2)[:, hh * P:(hh + 1) * P], Ym[:, hh, :], Dm[:, hh, :], start=True, stop=True)
                    last.then_inc(S["Gready"], 1)
                pe.wait_ge(S["lv"], LEVEL_STEPS[t + 1] + 2 * t + 2)
                pe.wait_ge(S["tokev"], t + 1)
                for hh in range(HEADS):
                    last = mm(bank(4)[:, hh * P:(hh + 1) * P], bk[:, hh, :], Fm[:, hh, :], start=True, stop=True)
                last.then_inc(S["wkt"], 1)
                pe.wait_ge(S["nwk"], t + 1)
                if t < 2:
                    for b in range(2):
                        g = 2 * t + b
                        rows = slice(64 * b, 64 * b + 64)
                        if g >= 1:
                            pe.wait_ge(S["st_upd"], g)
                        for hh in range(HEADS):
                            o = bank(5)[rows, hh * P:(hh + 1) * P]
                            last = mm(o, Fm[:, hh, rows], bv[:, hh, :], start=True, stop=(g == 0))
                            if g >= 1:
                                last = mm(o, nwk[:, hh, rows], st[:, hh, :], start=False, stop=True)
                        last.then_inc(S["u"], 1)
                        for hh in range(HEADS):
                            if g >= 1:
                                mm(bank(0)[:, hh * P + 64 * b:hh * P + 64 * b + 64], st[:, hh, :], qd[:, hh, rows],
                                   start=True, stop=False)
                            if hh == 0:
                                pe.wait_ge(S["uev"], g + 1)
                            mm(bank(0)[:, hh * P + 64 * b:hh * P + 64 * b + 64], um[rows, hh, :], qkT[rows, hh, rows],
                               start=(g == 0), stop=True)
                        for hh in range(HEADS):
                            last = mm(bank(6 + b)[:, hh * P:(hh + 1) * P], kd[rows, hh, :], um[rows, hh, :],
                                      start=True, stop=True)
                        last.then_inc(S["snew"], 1)
                else:
                    pe.wait_ge(S["st_in"], 16)
                    for hh in range(HEADS):
                        o = bank(5)[:, hh * P:(hh + 1) * P]
                        for s in range(NSEQ):
                            c = slice(s * LS, (s + 1) * LS)
                            mm(o[:, c], states[:, s, hh, :], nwk[:, hh, c], start=(s == 0), stop=False,
                               skip_group_check=True)
                        last = mm(o, bv[:, hh, :], Fm[:, hh, :], start=False, stop=True, skip_group_check=True)
                    last.then_inc(S["u"], 1)
                    pe.wait_ge(S["utr"], 1)
                    for hh in range(HEADS):
                        last = tr(bank(2)[:, hh * P:(hh + 1) * P], uT[:, hh, :])
                    last.then_inc(S["u"], 1)
                    pe.wait_ge(S["uev"], 5)
                    for hh in range(HEADS):
                        o = bank(0)[:, hh * P:(hh + 1) * P]
                        for s in range(NSEQ):
                            c = slice(s * LS, (s + 1) * LS)
                            mm(o[:, c], states[:, s, hh, :], qd[:, hh, c], start=(s == 0), stop=False,
                               skip_group_check=True)
                        mm(o, um[:, hh, :], qkT[:, hh, :], start=False, stop=True, skip_group_check=True)
                    for hh in range(HEADS):
                        pe.wait_ge(S["um"], hh + 1)
                        if hh:
                            pe.wait_ge(S["st_upd"], 4 + hh)
                        for k in range(2):
                            last = mm(bank(6 + k), kd[:, hh, :], umask[:, 4 * k:4 * k + 4, :].rearrange("p s v -> p (s v)"),
                                      start=True, stop=True)
                        last.then_inc(S["snew"], 1)
                pe.wait_ge(S["oev"], t + 1)
                last = mm(bank(1), ones, osq.rearrange("p h n -> p (h n)"), start=True, stop=True)
                last.then_inc(S["osum"], 1)

            pe.wait_ge(S["yd"], 3)
            k = 0
            branches = ((0, 4, dg), (4, 2, sbb), (6, 2, mq))
            for half in range(2):
                for n in range(7 + 4 * half, 11 + 4 * half):
                    pe.wait_ge(loaded[n % 4], 16 * (n // 4 + 1))
                for c in range(4):
                    for b, (k0, kn, src) in enumerate(branches):
                        if k >= 4:
                            pe.wait_ge(S["mrg"], k - 3)
                        w = piece((7 + 4 * half + b) % 4)
                        for t in range(KT8):
                            last = mm(bank(2 * (k % 4))[:, 0:TOK], w[:, t, c * P:(c + 1) * P], xnT[:, t, :],
                                      start=(t == 0), stop=(t == KT8 - 1))
                        last.then_inc(S["gp"], 1)
                        w = piece((10 + 4 * half) % 4)
                        for j in range(kn):
                            last = mm(bank(2 * (k % 4) + 1)[:, 0:TOK], w[:, k0 + j, c * P:(c + 1) * P], src[:, j, :],
                                      start=(j == 0), stop=(j == kn - 1))
                        last.then_inc(S["gz"], 1)
                        k += 1

            pe.wait_ge(S["mrg"], 24)
            for half in range(2):
                n = 15 + half
                pe.wait_ge(loaded[n % 4], 16 * (n // 4 + 1))
                for a in range(TILES):
                    for j in range(KT8):
                        last = mm(bank(3 * half + a), mg[:, j, a * P:(a + 1) * P], piece(n % 4)[:, j, :],
                                  start=(j == 0), stop=(j == KT8 - 1))
                    last.then_inc(S["wo"], 1)

            pe.wait_ge(S["bdn_in"], 48)
            for k in range(2):
                for r in range(2):
                    last = tr(bank(6)[:, (2 * k + r) * P:(2 * k + r + 1) * P], brow[:, k, r, :])
            last.then_inc(S["brt"], 1)
            pe.wait_ge(S["hadd"], 6)
            for a in range(TILES):
                pe.wait_ge(S["x2"], a + 1)
                for k in range(KT8):
                    last = tr(bank(2 * a + k // 4)[:, (k % 4) * P:(k % 4 + 1) * P], x2[:, a, k::KT8])
                last.then_inc(S["x2tr"], 1)
            pe.wait_ge(S["x2T"], 3)
            pe.wait_ge(S["rout_in"], 48)
            for a in range(TILES):
                for t in range(KT8):
                    last = mm(bank(7)[:, a * E:(a + 1) * E], x2T[:, t, a * P:(a + 1) * P], wr[:, t, :],
                              start=(t == 0), stop=(t == KT8 - 1))
            last.then_inc(S["lgm"], 1)
            pe.wait_ge(S["sel"], 1)
            mask = rt[0]
            for a in range(TILES):
                for b in range(a):
                    mm(bank(0)[:, a * E:(a + 1) * E], ones, mask[:, b, :], start=(b == 0), stop=False)
                mm(bank(0)[:, a * E:(a + 1) * E], const("before"), mask[:, a, :], start=(a == 0), stop=True)
            for a in range(TILES):
                last = mm(bank(0)[:, 3 * E:4 * E], ones, mask[:, a, :], start=(a == 0), stop=(a == TILES - 1))
            last.then_inc(S["posm"], 1)
            for a in range(TILES):
                last = tr(bank(1)[0:E, a * P:(a + 1) * P], gate[:, a, 0:E])
            last.then_inc(S["gtr"], 1)
            pe.wait_ge(S["gT"], 1)
            for a in range(TILES):
                for k in range(2):
                    last = mm(bank(2 + 2 * a + k), gT[:, a * P:(a + 1) * P], bd[:, 512 * k:512 * k + 512], start=True, stop=True)
            last.then_inc(S["bdm"], 1)

            pe.wait_ge(S["accrd"], 1)

            def gather(n):
                pe.wait_ge(S["P"], n + 1)
                for t in range(KT8):
                    for a in range(TILES):
                        for k in range(3):
                            last = mm(bank(6, 2)[:, t * P:(t + 1) * P], split[:, k, a, t::KT8],
                                      onehot[:, a, :, :].rearrange("p r c -> p (r c)"),
                                      start=(a == 0 and k == 0), stop=(a == TILES - 1 and k == 2))
                last.then_inc(S["xg"], 1)

            def product(q0, b, x):
                for j in range(halves):
                    pe.wait_ge(S["lo"], q0 + j + 1)
                    for i in range(2):
                        k = 2 * j + i
                        for c in range(2):
                            cols = slice(1024 * i + 512 * c, 1024 * i + 512 * c + 512)
                            mm(bank(b + c), x[:, k, :], w_hi[j % 2][:, cols], start=(k == 0), stop=False)
                            last = mm(bank(b + c), x[:, k, :], w_lo[j % 2][:, cols], start=False, stop=(k == 7))
                    last.then_inc(S["used"], 1)

            def turned(b, src, done):
                for f in range(8):
                    last = mm(bank(b)[:, f * CAP:(f + 1) * CAP], src[:, f * P:(f + 1) * P], const("fold"), start=True, stop=True)
                last.then_inc(done, 1)

            def gate_product(n, q0):
                pe.wait_ge(S["xlo"], n + 1)
                product(q0, 0, xparts)

            def gate_turned(n):
                pe.wait_ge(S["gev"], n + 1)
                turned(4, g_sb, S["gT2"])

            def up_turned(n):
                pe.wait_ge(S["uout"], n + 1)
                turned(5, u_sb, S["uT2"])

            def slots_turned(n):
                pe.wait_ge(S["Pg"], n + 1)
                pe.wait_ge(S["hg"], n + 1)
                for a in range(TILES):
                    last = tr(bank(4)[:, a * P:(a + 1) * P], onehot_g[:, a, :, :].rearrange("p r c -> p (r c)"))
                last.then_inc(S["pgt"], 1)

            def down_product(n, q0):
                pe.wait_ge(S["hlo"], n + 1)
                product(q0, 2, hparts)

            def scatter(n):
                pe.wait_ge(S["yev"], n + 1)
                pe.wait_ge(S["pgtev"], n + 1)
                for a in range(TILES):
                    for k in range(2):
                        if a:
                            pe.wait_ge(S["accrd"], 6 * n + 2 * a + k)
                        mm(bank(6 + k), pgT[:, a * P:(a + 1) * P], y_sb[:, 512 * k:512 * k + 512],
                           start=True, stop=True).then_inc(S["acc"], 1)

            def item(n, first=False, last=False):
                gate_turned(n)
                if not first:
                    pe.wait_ge(S["yev"], n)
                product(stream("up", n), 2, xparts)
                if not last:
                    if not first:
                        pe.wait_ge(S["accrd"], 6 * n - 5)
                    gather(n + 1)
                up_turned(n)
                if not first:
                    if not last:
                        pe.wait_ge(S["xlo"], n + 2)
                    scatter(n - 1)
                slots_turned(n)
                if not last:
                    gate_product(n + 1, stream("gate", n + 1))
                down_product(n, stream("down", n))

            gather(0)
            gate_product(0, 0)
            item(0, first=True)
            with pe.Fori(1, E - 1) as e:
                item(e)
            item(E - 1, last=True)
            scatter(E - 1)
            pe.wait_ge(S["overx"], 1)
            n_over = pe.value_load(over[0:1, 0:1], min_val=0, max_val=MAX_OVER)
            with pe.If(n_over > 0):
                with pe.Fori(0, MAX_OVER) as i:
                    with pe.If(n_over > i):
                        n = i + E
                        pe.wait_ge(S["accrd"], 6 * n + 1)
                        gather(n)
                        gate_product(n, stream_over("gate", n))
                        gate_turned(n)
                        product(stream_over("up", n), 2, xparts)
                        up_turned(n)
                        slots_turned(n)
                        down_product(n, stream_over("down", n))
                        scatter(n)

        @block.scalar
        def _(act):
            f = nc.scalar.activation
            own = [0]

            def link(ins):
                own[0] += 1
                ins.then_inc(S["tabs"], 1)
                act.wait_ge(S["tabs"], own[0])

            act.wait_ge(S["x_in"], 32)
            for t in range(3):
                f(xs[:, t, :], h[:, t, :], ACT.Square, accum_out=small[:, 40 + t:41 + t])
            act.wait_ge(S["mem_in"], 16)
            for t in range(2):
                last = f(xs_mem[:, t, :], mem[:, t, :], ACT.Square, accum_out=small[:, 43 + t:44 + t])
            last.then_inc(S["ss"], 1)
            act.wait_ge(S["ss"], 2)
            f(small[:, 46:51], small[:, 40:45], ACT.Sqrt).then_inc(S["rt5"], 1)
            def xp_sample(c):
                return xp[:, c, LP:WP].rearrange("p (s k) -> p s k", k=3 + LS)[:, :, 3:3 + LS]

            act.wait_ge(S["cwtr"], 1)
            f(cw[:, :], bank(2)[:, 0:374], ACT.Copy).then_inc(S["cwT"], 1)
            for q in range(27):
                b = bank(q % 8)
                act.wait_ge(S["pj"], q + 1)
                if q < 2:
                    last = f(kvp[:, q, :], b, ACT.Copy)
                elif q < 14:
                    f(xp[:, q - 2, 3:LP], b[:, 0:256], ACT.Copy)
                    last = f(xp_sample(q - 2), b[:, 256:TOK].rearrange("p (s k) -> p s k", k=LS), ACT.Copy)
                elif q == 14:
                    last = f(small[:, 64:88], b[:, 0:24], ACT.Copy)
                elif q < 19:
                    last = f(dg[:, q - 15, :], b[:, 0:TOK], ACT.Silu)
                elif q < 21:
                    last = f(sbb[:, q - 19, :], b[:, 0:TOK], ACT.Copy)
                elif q < 23:
                    last = f(cT[:, q - 21, :], b[:, 0:TOK], ACT.Copy)
                elif q < 25:
                    last = f(hT[:, q - 23, :], b[:, 0:TOK], ACT.Copy)
                else:
                    last = f(mq[:, q - 25, :], b[:, 0:TOK], ACT.Copy)
                last.then_inc(S["pjev"], 1)
            for c in range(NQKV):
                act.wait_ge(S["conv"], c + 1)
                f(qkv[:, c, 0:256], conv_acc[:, 0:256], ACT.Silu)
                f(qkv[:, c, 256:TOK].rearrange("p (s k) -> p s k", k=LS),
                  conv_acc[:, LP:WP].rearrange("p (s k) -> p s k", k=3 + LS)[:, :, 0:LS], ACT.Silu).then_inc(S["silu"], 1)
            act.wait_ge(S["silu"], NQKV)
            act.wait_ge(S["conv"], NQKV)
            act.wait_ge(S["co"], 1)
            for g in range(2):
                if g:
                    act.wait_ge(S["nsum"], g)
                f(sq4, qkv[:, 4 * g:4 * g + 4, :], ACT.Square).then_inc(S["sq"], 1)
                act.wait_ge(S["nadd"], g + 1)
                f(nr4, nr4, ACT.Sqrt).then_inc(S["nsqrt"], 1)
            for k in range(3):
                act.wait_ge(S["cotr"], k + 1)
                f(cor[:, 512 * k:512 * k + 512], bank(4 + k)[0:27, :], ACT.Copy).then_inc(S["cor"], 1)
            act.wait_ge(S["cotr"], 4)
            f(scor[:, :], bank(7)[0:18, 0:256], ACT.Copy).then_inc(S["cor"], 1)
            act.wait_ge(S["vec_in"], 96)
            f(small[:, 108:112], hb[:, 0:4], ACT.Exp)
            act.wait_ge(S["ab"], 1)
            f(small[:, 128:140], small[:, 112:124], ACT.Exp, scale=-1.0).then_inc(S["abx"], 1)
            act.wait_ge(S["ab"], 2)
            f(small[:, 128:140], small[:, 128:140], ACT.Ln).then_inc(S["abl"], 1)
            f(small[:, 144:156], small[:, 88:100], ACT.Sigmoid).then_inc(S["abg"], 1)
            act.wait_ge(S["norm"], 2)
            for s in range(9):
                act.wait_ge(S["ktr"], s + 1)
                f(kT[:, :, s, :], bank(s % 8).rearrange("p (b m) -> p b m", b=2), ACT.Copy).then_inc(S["kT"], 1)
            for t in range(TILES):
                act.wait_ge(S["soft"], t + 1)
                if t:
                    act.wait_ge(S["ptr"], t)
                for hh in range(4):
                    last = f(prob[:, hh, :], bank(2 * t + hh // 2)[:, (hh % 2) * 256:(hh % 2) * 256 + 256], ACT.Exp,
                             bias=small[:, 160 + hh:161 + hh], scale=0.125, accum_out=small[:, 164 + hh:165 + hh])
                last.then_inc(S["pexp"], 1)
                act.wait_ge(S["ptr"], t + 1)
                if t:
                    act.wait_ge(S["pv"], t)
                f(probT, bank(6, 2).rearrange("p (c n) -> p c n", c=8), ACT.Copy).then_inc(S["pT"], 1)
                act.wait_ge(S["pv"], t + 1)
                f(mq[:, :, t * P:(t + 1) * P], bank(2 * t)[:, 0:256].rearrange("p (b n) -> p b n", b=2),
                  ACT.Copy).then_inc(S["ym"], 1)
            for t in range(TILES):
                act.wait_ge(S["gex"], 2 * t + 1)
                f(small[:, 180:188], small[:, 172:180], ACT.Exp).then_inc(S["gex"], 1)
                act.wait_ge(S["dexp"], 3 * t + 1)
                f(eB, bank(1).rearrange("p (h n) -> p h n", h=4), ACT.Exp)
                f(dTm, dTm, ACT.Exp)
                f(dec, dec, ACT.Exp, scale=-1.0).then_inc(S["dexp"], 2)
                act.wait_ge(S["dmul"], t + 1)
                for n in range(1, len(tile_levels[t])):
                    k = LEVEL_STEPS[t] + n
                    act.wait_ge(S["Yready"], k)
                    f(Ym, bank(7).rearrange("p (h n) -> p h n", h=4), ACT.Copy).then_inc(S["uready"], 1)
                act.wait_ge(S["wkt"], t + 1)
                f(nwk, bank(4).rearrange("p (h n) -> p h n", h=4), ACT.Copy, scale=-1.0).then_inc(S["nwk"], 1)
                if t < 2:
                    for b in range(2):
                        act.wait_ge(S["u"], 2 * t + b + 1)
                        f(um[64 * b:64 * b + 64, :, :], bank(5)[64 * b:64 * b + 64, :].rearrange("p (h n) -> p h n", h=4),
                          ACT.Copy).then_inc(S["uev"], 1)
                    act.wait_ge(S["snew"], 2 * t + 2)
                else:
                    act.wait_ge(S["u"], 5)
                    f(uT, bank(5).rearrange("p (h n) -> p h n", h=4), ACT.Copy).then_inc(S["utr"], 1)
                    act.wait_ge(S["u"], 6)
                    f(um, bank(2).rearrange("p (h n) -> p h n", h=4), ACT.Copy).then_inc(S["uev"], 1)
                    act.wait_ge(S["snew"], 5)
                f(oS, bank(0).rearrange("p (h n) -> p h n", h=4), ACT.Copy)
                f(osq, bank(0).rearrange("p (h n) -> p h n", h=4), ACT.Square).then_inc(S["oev"], 1)
                act.wait_ge(S["onorm"], 2 * t + 1)
                f(osq, osq, ACT.Sqrt).then_inc(S["onorm"], 1)
            act.wait_ge(S["yd"], 3)
            for k in range(24):
                act.wait_ge(S["gp"], k + 1)
                if k >= 4:
                    act.wait_ge(S["mrg"], k - 3)
                f(sig[:, k % 4, :], bank(2 * (k % 4))[:, 0:TOK], ACT.Sigmoid).then_inc(S["gsig"], 1)
            act.wait_ge(S["hadd"], 6)
            for t in range(TILES):
                last = f(x2[:, t, :], h[:, t, :], ACT.Square, accum_out=small[:, 40 + t:41 + t])
            last.then_inc(S["ss2"], 1)
            act.wait_ge(S["rt2"], 1)
            f(small[:, 46:49], small[:, 40:43], ACT.Sqrt).then_inc(S["rt2"], 1)
            act.wait_ge(S["brt"], 1)
            for k, dst in enumerate((bg, bu)):
                last = f(dst[:, 0:256], bank(6)[:, 256 * k:256 * k + 256], ACT.Copy)
            last.then_inc(S["bT"], 1)
            act.wait_ge(S["lgx"], 1)
            f(rt[2], rt[1], ACT.Exp).then_inc(S["lgx"], 1)
            act.wait_ge(S["gtr"], 1)
            act.wait_ge(S["x2T"], 3)
            f(gT, bank(1)[0:E, 0:TOK], ACT.Copy).then_inc(S["gT"], 1)
            act.wait_ge(S["accrd"], 1)

            def hi(kind, n, q0, j, free=True):
                s = 2 * MATS.index(kind) + j // 2
                act.wait_ge(loaded[s], 16 * len(range(s, TRUNK_PIECES, 4)) * (s < 4) + 16 + 16 * n)
                if free:
                    act.wait_ge(S["used"], q0 + j - 1)
                f(w_hi[j % 2][:, :], ring[:, s, 2048 * (j % 2):2048 * (j % 2) + 2048], ACT.Copy).then_inc(S["hi"], 1)

            def x_hi(n):
                act.wait_ge(S["xg"], n + 1)
                f(xparts[:, :, 0:CAP], bank(6, 2).rearrange("p (t c) -> p t c", t=KT8)[:, :, 0:CAP], ACT.Copy).then_inc(S["xhi"], 1)

            def g_out(n, q0):
                act.wait_ge(S["used"], q0 + halves)
                f(g_sb[:, :], bank(0, 2), ACT.Copy).then_inc(S["gev"], 1)

            def u_out(n, q0):
                act.wait_ge(S["used"], q0 + halves)
                f(u_sb[:, :], bank(2, 2), ACT.Copy).then_inc(S["uout"], 1)

            def y_out(n, q0):
                act.wait_ge(S["used"], q0 + halves)
                f(y_sb[:, :], bank(2, 2), ACT.Copy).then_inc(S["yev"], 1)

            def slots_out(n):
                act.wait_ge(S["pgt"], n + 1)
                f(pgT[:, :], bank(4)[:, 0:TOK], ACT.Copy).then_inc(S["pgtev"], 1)

            def sigmoid(n):
                act.wait_ge(S["hg"], n + 1)
                f(sg[:, :], hg[:, :], ACT.Sigmoid, scale=ALPHA).then_inc(S["sgm"], 1)

            def h_hi(n):
                act.wait_ge(S["hf"], n + 1)
                f(hparts[:, :, 0:CAP], hu[:, :].rearrange("p (f c) -> p f c", f=8), ACT.Copy).then_inc(S["hhi"], 1)

            def item(n, last=False):
                up, down = stream("up", n), stream("down", n)
                hi("up", n, up, 1)
                sigmoid(n)
                hi("up", n, up, 2)
                hi("up", n, up, 3)
                if not last:
                    gate_ = stream("gate", n + 1)
                    hi("gate", n + 1, gate_, 0)
                u_out(n, up)
                if not last:
                    x_hi(n + 1)
                    hi("gate", n + 1, gate_, 1)
                h_hi(n)
                slots_out(n)
                if not last:
                    hi("gate", n + 1, gate_, 2)
                    hi("gate", n + 1, gate_, 3)
                hi("down", n, down, 0)
                if not last:
                    g_out(n + 1, gate_)
                for j in range(1, halves):
                    hi("down", n, down, j)
                if not last:
                    hi("up", n + 1, stream("up", n + 1), 0)
                y_out(n, down)

            for j in range(2):
                hi("gate", 0, 0, j, free=False)
            x_hi(0)
            for j in range(2, 4):
                hi("gate", 0, 0, j)
            hi("up", 0, stream("up", 0), 0)
            g_out(0, 0)
            item(0)
            with act.Fori(1, E - 1) as e:
                item(e)
            item(E - 1, last=True)
            act.wait_ge(S["overx"], 1)
            n_over = act.value_load(over[0:1, 0:1], min_val=0, max_val=MAX_OVER)
            with act.If(n_over > 0):
                with act.Fori(0, MAX_OVER) as i:
                    with act.If(n_over > i):
                        n = i + E
                        x_hi(n)
                        for j in range(halves):
                            hi("gate", n, stream_over("gate", n), j)
                        g_out(n, stream_over("gate", n))
                        sigmoid(n)
                        for j in range(halves):
                            hi("up", n, stream_over("up", n), j)
                        u_out(n, stream_over("up", n))
                        h_hi(n)
                        slots_out(n)
                        for j in range(halves):
                            hi("down", n, stream_over("down", n), j)
                        y_out(n, stream_over("down", n))
            act.wait_ge(S["fss"], 1)
            for t in range(TILES):
                last = f(bank(2 * t, 2), h[:, t, :], ACT.Square, accum_out=small[:, 40 + t:41 + t])
            last.then_inc(S["fss"], 1)
            act.wait_ge(S["frt"], 1)
            f(small[:, 46:49], small[:, 40:43], ACT.Sqrt).then_inc(S["frt"], 1)

        @block.vector
        def _(dve):
            v = nc.vector
            own = [0]

            def link(ins):
                own[0] += 1
                ins.then_inc(vlink, 1)
                dve.wait_ge(vlink, own[0])

            v.memset(xp[:, :, 0:3], 0.0)
            link(v.memset(sp[:, :, 0:2], 0.0))
            dve.wait_ge(S["ss"], 1)
            v.tensor_scalar(small[:, 40:45], small[:, 40:45], 1.0 / D, EPS, ALU.mult, ALU.add).then_inc(S["ss"], 1)
            dve.wait_ge(S["rt5"], 1)
            link(v.reciprocal(small[:, 52:57], small[:, 46:51]))
            for t in range(5):
                src, dst = (h[:, t, :], xs[:, t, :]) if t < 3 else (mem[:, t - 3, :], xs_mem[:, t - 3, :])
                v.tensor_scalar(dst, src, small[:, 52 + t:53 + t], None, ALU.mult).then_inc(S["xs"], 1)
            dve.wait_ge(S["vec_in"], 96)
            for t in range(5):
                dve.wait_ge(S["xtr"], t + 1)
                for k in range(2):
                    dst = xnT[:, 4 * k:4 * k + 4, t * P:(t + 1) * P] if t < 3 else mT[:, 4 * k:4 * k + 4, (t - 3) * P:(t - 2) * P]
                    c = 4 * k + (0 if t < 3 else 16)
                    last = v.tensor_tensor(dst, bank((2 * t + k) % 8).rearrange("p (t n) -> p t n", t=4),
                                           norms[:, c:c + 4].unsqueeze(2).to_broadcast([P, 4, P]), ALU.mult)
                last.then_inc(S["xT"], 1)
            dve.wait_ge(S["cwT"], 1)
            for c in range(NQKV):
                v.tensor_copy(xp[:, c, LP:WP].rearrange("p (s k) -> p s k", k=3 + LS)[:, :, 0:3],
                              cwv[:, c, 0:24].rearrange("p (s k) -> p s k", k=3))
            for c in range(2):
                last = v.tensor_copy(sp[:, c, SP2:WS].rearrange("p (s k) -> p s k", k=2 + LS)[:, :, 0:2],
                                     scwv[:, c, 0:16].rearrange("p (s k) -> p s k", k=2))
            link(last)
            dve.wait_ge(S["pjev"], 27)
            link(v.tensor_tensor(sp[:, :, 2:SP2], cT[:, :, 0:256], hT[:, :, 0:256], ALU.mult))
            for c in range(2):
                last = v.tensor_tensor(sp[:, c, SP2:WS].rearrange("p (s k) -> p s k", k=2 + LS)[:, :, 2:2 + LS],
                                       cT[:, c, 256:TOK].rearrange("p (s k) -> p s k", k=LS),
                                       hT[:, c, 256:TOK].rearrange("p (s k) -> p s k", k=LS), ALU.mult)
            link(last)
            for c in range(2):
                n = WS - 2
                link(v.tensor_scalar(conv_acc[:, 0:n], sp[:, c, 0:n], scwv[:, c, 16:17], None, ALU.mult))
                for j in range(1, 3):
                    link(v.scalar_tensor_tensor(out=conv_acc[:, 0:n], in0=sp[:, c, j:j + n], scalar=scwv[:, c, 16 + j:17 + j],
                                                in1=conv_acc[:, 0:n], op0=ALU.mult, op1=ALU.add))
                v.tensor_tensor(sbb[:, c, 0:256], sbb[:, c, 0:256], conv_acc[:, 0:256], ALU.mult)
                link(v.tensor_tensor(sbb[:, c, 256:TOK].rearrange("p (s k) -> p s k", k=LS),
                                     sbb[:, c, 256:TOK].rearrange("p (s k) -> p s k", k=LS),
                                     conv_acc[:, SP2:WS].rearrange("p (s k) -> p s k", k=2 + LS)[:, :, 0:LS], ALU.mult))
            for c in range(NQKV):
                n = WP - 3
                if c:
                    dve.wait_ge(S["silu"], c)
                link(v.tensor_scalar(conv_acc[:, 0:n], xp[:, c, 0:n], cwv[:, c, 24:25], None, ALU.mult))
                for j in range(1, 4):
                    ins = v.scalar_tensor_tensor(out=conv_acc[:, 0:n], in0=xp[:, c, j:j + n], scalar=cwv[:, c, 24 + j:25 + j],
                                                 in1=conv_acc[:, 0:n], op0=ALU.mult, op1=ALU.add)
                    if j < 3:
                        link(ins)
                ins.then_inc(S["conv"], 1)
            v.tensor_copy(cov[:, :, 0:3], xp[:, :, LP - 3:LP])
            for c in range(NQKV):
                last = v.tensor_copy(cov[:, c, 3:27].rearrange("p (s k) -> p s k", k=3),
                                     xp[:, c, LP:WP].rearrange("p (s k) -> p s k", k=3 + LS)[:, :, LS:LS + 3])
            last.then_inc(S["co"], 1)
            v.tensor_copy(scov[:, :, 0:2], sp[:, :, SP2 - 2:SP2])
            for c in range(2):
                last = v.tensor_copy(scov[:, c, 2:18].rearrange("p (s k) -> p s k", k=2),
                                     sp[:, c, SP2:WS].rearrange("p (s k) -> p s k", k=2 + LS)[:, :, LS:LS + 2])
            last.then_inc(S["co"], 1)
            for g in range(2):
                dve.wait_ge(S["nsum"], g + 1)
                if g:
                    dve.wait_ge(S["norm"], g)
                v.tensor_scalar(nr4, bank(0, 4).rearrange("p (c n) -> p c n", c=4)[:, :, 0:TOK], EPS, None,
                                ALU.add).then_inc(S["nadd"], 1)
                dve.wait_ge(S["nsqrt"], g + 1)
                link(v.reciprocal(nr4, nr4))
                v.scalar_tensor_tensor(out=qkv[:, 4 * g:4 * g + 4, :], in0=qkv[:, 4 * g:4 * g + 4, :],
                                       scalar=(float(P) ** -0.5 if g == 0 else 1.0), in1=nr4, op0=ALU.mult,
                                       op1=ALU.mult).then_inc(S["norm"], 1)
            lgt = small[:, 64:88].rearrange("p (a k) -> p a k", a=3)
            az = small[:, 192:204].rearrange("p (a k) -> p a k", a=3)
            link(v.tensor_tensor(az, lgt[:, :, 0:4], hb[:, 4:8].unsqueeze(1).to_broadcast([P, 3, 4]), ALU.add))
            v.tensor_copy(small[:, 88:100].rearrange("p (a k) -> p a k", a=3), lgt[:, :, 4:8])
            link(v.tensor_scalar(small[:, 112:124], small[:, 192:204], -1.0, None, ALU.mult))
            v.tensor_tensor(small[:, 112:124], small[:, 112:124], small[:, 192:204], ALU.max).then_inc(S["ab"], 1)
            dve.wait_ge(S["abx"], 1)
            v.tensor_scalar(small[:, 128:140], small[:, 128:140], 1.0, None, ALU.add).then_inc(S["ab"], 1)
            dve.wait_ge(S["abl"], 1)
            link(v.scalar_tensor_tensor(out=small[:, 192:204], in0=small[:, 192:204], scalar=0.0, in1=small[:, 128:140],
                                        op0=ALU.max, op1=ALU.add))
            gv = small[:, 0:36].rearrange("p (a k) -> p a k", a=3)
            v.scalar_tensor_tensor(out=gv[:, :, 0:4], in0=az, scalar=-1.0,
                                   in1=small[:, 108:112].unsqueeze(1).to_broadcast([P, 3, 4]), op0=ALU.mult, op1=ALU.mult)
            dve.wait_ge(S["abg"], 1)
            v.tensor_copy(gv[:, :, 4:8], small[:, 144:156].rearrange("p (a k) -> p a k", a=3)).then_inc(S["gates"], 1)
            dve.wait_ge(S["corout"], 32)
            link(v.memset(qm[:, :], 0.0))
            for s in range(NSEQ):
                last = v.tensor_copy(qmv[:, s, :, s * LS:(s + 1) * LS], mq[:, :, 256 + s * LS:256 + (s + 1) * LS])
            last.then_inc(S["qm"], 1)
            for t in range(TILES):
                dve.wait_ge(S["sc"], t + 1)
                link(v.tensor_reduce(small[:, 160:164], bank(2 * t, 2).rearrange("p (h m) -> p h m", h=4), AX.X, ALU.max))
                v.tensor_scalar(small[:, 160:164], small[:, 160:164], -0.125, None, ALU.mult).then_inc(S["soft"], 1)
                dve.wait_ge(S["pexp"], t + 1)
                link(v.reciprocal(small[:, 168:172], small[:, 164:168]))
                v.tensor_tensor(prob, prob, small[:, 168:172].unsqueeze(2).to_broadcast([P, 4, 256]), ALU.mult)\
                    .then_inc(S["pn"], 1)
            dve.wait_ge(S["gates"], 1)
            dve.wait_ge(S["ym"], 3)
            b3 = lambda x: x.unsqueeze(2).to_broadcast([P, HEADS, P])
            m3 = lambda x: x.unsqueeze(1).to_broadcast([P, HEADS, P])
            for t in range(TILES):
                cols = slice(t * P, (t + 1) * P)
                bv4 = lambda k: bank(k).rearrange("p (h n) -> p h n", h=HEADS)
                g = small[:, 12 * t:12 * t + 4]
                beta = small[:, 12 * t + 4:12 * t + 8]
                v.tensor_copy(gb, b3(g)).then_inc(S["gbr"], 1)
                dve.wait_ge(S["gcum"], t + 1)
                link(v.tensor_copy(small[:, 172:176], bank(0)[:, 0:4]))
                v.tensor_tensor(small[:, 176:180], bank(0)[:, 4:8], small[:, 172:176], ALU.subtract).then_inc(S["gex"], 1)
                dve.wait_ge(S["cumb"], t + 1)
                for hh in range(HEADS):
                    v.tensor_scalar(dTm[:, hh, :], bv4(1)[:, hh, :], small[:, 172 + hh:173 + hh], 0.0, ALU.subtract, ALU.min)
                    last = v.tensor_scalar(dec[:, hh, :], bv4(1)[:, hh, :], small[:, 172 + hh:173 + hh], 0.0, ALU.subtract, ALU.max)
                last.then_inc(S["dexp"], 1)
                dve.wait_ge(S["gex"], 2 * t + 2)
                link(v.tensor_tensor(small[:, 188:192], small[:, 180:184], beta, ALU.mult))
                dve.wait_ge(S["tok"], t + 1)
                v.tensor_tensor(bk, bv4(4), b3(small[:, 188:192]), ALU.mult)
                v.tensor_tensor(kd, bv4(4), b3(small[:, 184:188]), ALU.mult)
                v.tensor_tensor(bv, bv4(5), b3(beta), ALU.mult).then_inc(S["tokev"], 1)
                dve.wait_ge(S["dexp"], 3 * t + 3)
                dve.wait_ge(S["kk"], t + 1)
                link(v.tensor_tensor(dTm, dTm, m3(upto[t]), ALU.mult))
                v.tensor_tensor(qkT, bv4(3), dTm, ALU.mult)
                v.tensor_tensor(qd, qkv[:, 0:4, cols], eB, ALU.mult)
                link(v.tensor_tensor(dec, dec, b3(beta), ALU.mult))
                link(v.tensor_tensor(Am, bv4(2), dec, ALU.mult))
                link(v.tensor_tensor(Em, Am, m3(const("level1")), ALU.mult))
                v.tensor_tensor(Dm, m3(ident), Em, ALU.subtract).then_inc(S["lv"], 1)
                dve.wait_ge(S["lv"], LEVEL_STEPS[t] + 2 * t + 1)
                v.tensor_tensor(Em, Am, m3(const("level2")), ALU.mult).then_inc(S["dmul"], 1)
                dve.wait_ge(S["Fready"], t + 1)
                v.tensor_copy(Fm, bv4(6)).then_inc(S["lv"], 1)
                for n in range(1, len(tile_levels[t])):
                    k = LEVEL_STEPS[t] + n
                    last_level = n == len(tile_levels[t]) - 1
                    dve.wait_ge(S["Gready"], k)
                    v.tensor_tensor(Fm, Fm, bv4(6), ALU.subtract)
                    if not last_level:
                        v.tensor_tensor(Em, Am, m3(const(f"level{tile_levels[t][n + 1]}")), ALU.mult)
                    v.tensor_tensor(Dm, Dm, bv4(2), ALU.subtract).then_inc(S["lv"], 1)
                if t < 2:
                    for b in range(2):
                        k = 2 * t + b
                        dve.wait_ge(S["snew"], k + 1)
                        if k == 0:
                            v.tensor_copy(st[:, :, :], bv4(6)).then_inc(S["st_upd"], 1)
                        else:
                            for hh in range(HEADS):
                                last = v.scalar_tensor_tensor(out=st[:, hh, :], in0=st[:, hh, :],
                                                              scalar=eB[:, hh, 64 * b + 63:64 * b + 64],
                                                              in1=bv4(6 + b)[:, hh, :], op0=ALU.mult, op1=ALU.add)
                            last.then_inc(S["st_upd"], 1)
                    if t == 1:
                        dve.wait_ge(S["st_upd"], 4)
                        v.tensor_copy(small[:, 210:211], st[:, 0, 0:1]).then_inc(S["st_all"], 1)
                else:
                    dve.wait_ge(S["uev"], 5)
                    for hh in range(HEADS):
                        if hh:
                            dve.wait_ge(S["snew"], 4 + hh)
                        v.tensor_tensor(umask, um[:, hh, :].unsqueeze(1).to_broadcast([P, NSEQ, P]),
                                        const("seq").unsqueeze(2).to_broadcast([P, NSEQ, P]), ALU.mult).then_inc(S["um"], 1)
                        dve.wait_ge(S["snew"], 5 + hh)
                        for s in range(NSEQ):
                            c = s * LS + LS - 1
                            last = v.scalar_tensor_tensor(out=states[:, s, hh, :], in0=states[:, s, hh, :],
                                                          scalar=eB[:, hh, c:c + 1],
                                                          in1=bank(6 + s // 4)[:, (s % 4) * P:(s % 4 + 1) * P],
                                                          op0=ALU.mult, op1=ALU.add)
                        last.then_inc(S["st_upd"], 1)
                    dve.wait_ge(S["st_upd"], 8)
                    v.tensor_copy(small[:, 210:211], states[:, 0, 0, 0:1]).then_inc(S["st_all"], 1)
                dve.wait_ge(S["osum"], t + 1)
                v.tensor_scalar(osq, bv4(1), 1.0 / P, EPS, ALU.mult, ALU.add).then_inc(S["onorm"], 1)
                dve.wait_ge(S["onorm"], 2 * t + 2)
                link(v.reciprocal(osq, osq))
                link(v.scalar_tensor_tensor(out=oS, in0=oS, scalar=norms[:, 24:25], in1=osq, op0=ALU.mult, op1=ALU.mult))
                v.tensor_tensor(dg[:, :, cols], dg[:, :, cols], oS, ALU.mult).then_inc(S["yd"], 1)
            for k in range(24):
                half, c, b = k // 12, k // 3 % 4, k % 3
                dst = mg[:, 4 * half + c, :]
                dve.wait_ge(S["gsig"], k + 1)
                dve.wait_ge(S["gz"], k + 1)
                z = bank(2 * (k % 4) + 1)[:, 0:TOK]
                if b == 0:
                    ins = v.tensor_tensor(dst, sig[:, k % 4, :], z, ALU.mult)
                else:
                    link(v.tensor_tensor(sig[:, k % 4, :], sig[:, k % 4, :], z, ALU.mult))
                    dve.wait_ge(S["mrg"], k)
                    ins = v.tensor_tensor(dst, dst, sig[:, k % 4, :], ALU.add)
                ins.then_inc(S["mrg"], 1)
            for k in range(2):
                for a in range(TILES):
                    n = 3 * k + a
                    dve.wait_ge(S["wo"], n + 1)
                    v.tensor_tensor(h[:, a, 512 * k:512 * k + 512], h[:, a, 512 * k:512 * k + 512], bank(n),
                                    ALU.add).then_inc(S["hadd"], 1)
            dve.wait_ge(S["ss2"], 1)
            v.tensor_scalar(small[:, 40:43], small[:, 40:43], 1.0 / D, EPS, ALU.mult, ALU.add).then_inc(S["rt2"], 1)
            dve.wait_ge(S["rt2"], 2)
            dve.wait_ge(S["rout_in"], 48)
            link(v.reciprocal(small[:, 52:55], small[:, 46:49]))
            for a in range(TILES):
                v.scalar_tensor_tensor(out=x2[:, a, :], in0=h[:, a, :], scalar=small[:, 52 + a:53 + a], in1=w2b,
                                       op0=ALU.mult, op1=ALU.mult).then_inc(S["x2"], 1)
            for a in range(TILES):
                dve.wait_ge(S["x2tr"], a + 1)
                v.tensor_copy(x2T[:, :, a * P:(a + 1) * P], bank(2 * a, 2).rearrange("p (t n) -> p t n", t=KT8))\
                    .then_inc(S["x2T"], 1)
            dve.wait_ge(S["wo"], 6)
            link(v.tensor_copy(split[:, 0, :, :], x2))
            link(v.tensor_tensor(x2, x2, split[:, 0, :, :], ALU.subtract))
            link(v.tensor_copy(split[:, 1, :, :], x2))
            link(v.tensor_tensor(x2, x2, split[:, 1, :, :], ALU.subtract))
            link(v.tensor_copy(split[:, 2, :, :], x2))
            dve.wait_ge(S["out"], 64)
            dve.wait_ge(S["lgm"], 1)
            link(v.tensor_tensor(lg, bank(7)[:, 0:3 * E].rearrange("p (a e) -> p a e", a=3),
                                 br.unsqueeze(1).to_broadcast([P, 3, E]), ALU.add))
            top = small[:, 216:240].rearrange("p (a k) -> p a k", a=3)
            for a in range(TILES):
                last = v.max(top[:, a, :], lg[:, a, :])
            link(last)
            be = lambda x: x.to_broadcast([P, 3, E])
            mask, t1, t2, t3, t4_, t5 = rt
            v.memset(t5, 0.0)
            v.tensor_tensor(mask, lg, be(top[:, :, 3:4]), ALU.is_gt)
            link(v.tensor_tensor(t3, lg, be(top[:, :, 3:4]), ALU.is_equal))
            v.tensor_reduce(small[:, 240:243], mask, AX.X, ALU.add)
            for a in range(TILES):
                last = v.tensor_tensor_scan(t4_[:, a, :], t3[:, a, :], t5[:, a, :], 0.0, ALU.add, ALU.add)
            link(last)
            link(v.tensor_scalar(small[:, 244:247], small[:, 240:243], -1.0, 4.0, ALU.mult, ALU.add))
            link(v.tensor_tensor(t4_, t4_, be(small[:, 244:247].unsqueeze(2)), ALU.is_le))
            link(v.tensor_tensor(t4_, t4_, t3, ALU.mult))
            link(v.tensor_tensor(mask, mask, t4_, ALU.add))
            v.tensor_tensor(t1, lg, be(top[:, :, 0:1]), ALU.subtract).then_inc(S["lgx"], 1)
            dve.wait_ge(S["lgx"], 2)
            link(v.tensor_tensor(t2, t2, mask, ALU.mult))
            link(v.tensor_reduce(small[:, 248:251], t2, AX.X, ALU.add))
            link(v.reciprocal(small[:, 252:255], small[:, 248:251]))
            v.tensor_tensor(gate[:, :, 0:E], t2, be(small[:, 252:255].unsqueeze(2)), ALU.mult).then_inc(S["sel"], 1)
            dve.wait_ge(S["posm"], 1)
            link(v.tensor_scalar(t1, bank(0)[:, 0:3 * E].rearrange("p (a e) -> p a e", a=3), 1.0, None, ALU.add))
            link(v.tensor_tensor(t1, t1, mask, ALU.mult))
            link(v.tensor_scalar(pos[:, :, 0:E], t1, -1.0, None, ALU.add))
            cnt = t2[:, 0, :]
            nb = t2[:, 1, :]
            end = t2[:, 2, :]
            link(v.tensor_copy(cnt, bank(0)[:, 3 * E:4 * E]))
            link(v.tensor_scalar(nb, cnt, float(CAP), None, ALU.is_gt))
            for r in range(2, 6):
                link(v.tensor_scalar(t3[:, 0, :], cnt, float(CAP * r), None, ALU.is_gt))
                link(v.tensor_tensor(nb, nb, t3[:, 0, :], ALU.add))
            link(v.tensor_tensor_scan(end, nb, t5[:, 0, :], 0.0, ALU.add, ALU.add))
            big = qm[:, 1024:1024 + MAX_OVER * E].rearrange("p (i e) -> p i e", i=MAX_OVER)
            lst = qm[:, 1800:1800 + 2 * MAX_OVER].rearrange("p (k i) -> p k i", k=2)
            link(v.tensor_tensor(big, const("rounds").unsqueeze(2).to_broadcast([P, MAX_OVER, E]),
                                 end.unsqueeze(1).to_broadcast([P, MAX_OVER, E]), ALU.is_ge))
            link(v.tensor_reduce(lst[:, 0, :], big, AX.X, ALU.add))
            link(v.tensor_tensor(big, big, nb.unsqueeze(1).to_broadcast([P, MAX_OVER, E]), ALU.mult))
            link(v.tensor_reduce(lst[:, 1, :], big, AX.X, ALU.add))
            link(v.tensor_tensor(lst[:, 1, :], const("rounds"), lst[:, 1, :], ALU.subtract))
            v.tensor_scalar(shift[:, :], lst[:, 1, :], 1.0, float(CAP), ALU.add, ALU.mult)
            v.tensor_scalar(over[0:1, 1:1 + MAX_OVER], lst[0:1, 0, :], float(E - 1), None, ALU.min)
            v.tensor_copy(over[0:1, 0:1], end[0:1, E - 1:E]).then_inc(S["overx"], 1)
            dve.wait_ge(S["bdm"], 1)
            dve.wait_ge(S["bT"], 1)
            for a in range(TILES):
                last = v.tensor_tensor(h[:, a, :], h[:, a, :], bank(2 + 2 * a, 2), ALU.add)
            last.then_inc(S["accrd"], 1)

            def place(position):
                v.tensor_tensor(onehot[:, :, :, :].rearrange("p a r c -> p a (r c)"), slots2,
                                position.to_broadcast([P, 3, 2 * CAP]), ALU.is_equal).then_inc(S["P"], 1)

            def place_gated(position, gates, n):
                og = onehot_g[:, :, :, :].rearrange("p a r c -> p a (r c)")
                v.tensor_tensor(og, slots2, position.to_broadcast([P, 3, 2 * CAP]), ALU.is_equal).then_inc(plink, 1)
                dve.wait_ge(plink, n + 1)
                v.tensor_tensor(og, og, gates.to_broadcast([P, 3, 2 * CAP]), ALU.mult).then_inc(S["Pg"], 1)

            def lo(kind, q0, j):
                s = 2 * MATS.index(kind) + j // 2
                dve.wait_ge(S["hi"], q0 + j + 1)
                v.tensor_tensor(w_lo[j % 2][:, :], ring[:, s, 2048 * (j % 2):2048 * (j % 2) + 2048],
                                w_hi[j % 2][:, :].bitcast(F32), ALU.subtract).then_inc(S["lo"], 1)

            def x_lo(n):
                dve.wait_ge(S["xhi"], n + 1)
                v.tensor_tensor(xparts[:, :, CAP:2 * CAP], bank(6, 2).rearrange("p (t c) -> p t c", t=KT8)[:, :, CAP:2 * CAP],
                                xparts[:, :, 0:CAP].bitcast(F32), ALU.subtract).then_inc(S["xlo"], 1)

            c8 = lambda x: x.rearrange("p (f c) -> p f c", f=8)
            biased = lambda b, e: b[:, bass.ds(e * 8, 8)].unsqueeze(2).to_broadcast([P, 8, CAP])

            def gate_in(n, e):
                dve.wait_ge(S["gT2"], n + 1)
                v.tensor_tensor(c8(hg[:, :]), c8(bank(4)), biased(bg, e), ALU.add).then_inc(mlink, 1)
                dve.wait_ge(mlink, 4 * n + 1)
                v.tensor_scalar(hg[:, :], hg[:, :], LIMIT, None, ALU.min).then_inc(S["hg"], 1)

            def gate_mul(n):
                dve.wait_ge(S["sgm"], n + 1)
                v.tensor_tensor(hg[:, :], hg[:, :], sg[:, :], ALU.mult).then_inc(mlink, 1)

            def up_in(n, e):
                dve.wait_ge(S["uT2"], n + 1)
                v.tensor_tensor(c8(hu[:, :]), c8(bank(5)), biased(bu, e), ALU.add).then_inc(mlink, 1)
                dve.wait_ge(mlink, 4 * n + 3)
                v.tensor_scalar(hu[:, :], hu[:, :], -LIMIT, LIMIT, ALU.max, ALU.min).then_inc(mlink, 1)
                dve.wait_ge(mlink, 4 * n + 4)
                v.scalar_tensor_tensor(out=hu[:, :], in0=hu[:, :], scalar=1.0, in1=hg[:, :], op0=ALU.add, op1=ALU.mult)\
                    .then_inc(S["hf"], 1)

            def h_lo(n):
                dve.wait_ge(S["hhi"], n + 1)
                v.tensor_tensor(hparts[:, :, CAP:2 * CAP], c8(hu[:, :]), hparts[:, :, 0:CAP].bitcast(F32),
                                ALU.subtract).then_inc(S["hlo"], 1)

            def add(n):
                dve.wait_ge(S["accrd"], 6 * n + 1)
                for a in range(TILES):
                    for k in range(2):
                        dve.wait_ge(S["acc"], 6 * n + 2 * a + k + 1)
                        o = h[:, a, 512 * k:512 * k + 512]
                        v.tensor_tensor(o, o, bank(6 + k), ALU.add).then_inc(S["accrd"], 1)

            slots2 = const("slots2").unsqueeze(1).to_broadcast([P, 3, 2 * CAP])
            column = lambda x, e: x[:, :, bass.ds(e, 1)]

            def item(n, first=False, last=False):
                if not last:
                    place(column(pos, n + 1))
                if not first:
                    dve.wait_ge(S["pgt"], n)
                place_gated(column(pos, n), column(gate, n), n)
                gate_in(n, n)
                lo("up", stream("up", n), 1)
                gate_mul(n)
                lo("up", stream("up", n), 2)
                lo("up", stream("up", n), 3)
                if not last:
                    gate_ = stream("gate", n + 1)
                    lo("gate", gate_, 0)
                    x_lo(n + 1)
                    lo("gate", gate_, 1)
                up_in(n, n)
                h_lo(n)
                if not first:
                    add(n - 1)
                if not last:
                    lo("gate", gate_, 2)
                    lo("gate", gate_, 3)
                for j in range(halves):
                    lo("down", stream("down", n), j)
                if not last:
                    lo("up", stream("up", n + 1), 0)

            dve.wait_ge(S["accrd"], 1)
            place(column(pos, 0))
            for j in range(2):
                lo("gate", 0, j)
            x_lo(0)
            for j in range(2, 4):
                lo("gate", 0, j)
            lo("up", stream("up", 0), 0)
            item(0, first=True)
            with dve.Fori(1, E - 1) as e:
                item(e)
            item(E - 1, last=True)
            add(E - 1)
            n_over = dve.value_load(over[0:1, 0:1], min_val=0, max_val=MAX_OVER)
            with dve.If(n_over > 0):
                with dve.Fori(0, MAX_OVER) as i:
                    with dve.If(n_over > i):
                        n = i + E
                        expert = dve.value_load(over[0:1, bass.ds(i + 1, 1)], min_val=0, max_val=E - 1)
                        slot = small[:, 216:219]
                        v.tensor_scalar(slot, column(pos, expert).rearrange("p a o -> p (a o)"),
                                        shift[:, bass.ds(i, 1)], None, ALU.subtract).then_inc(olink, 1)
                        dve.wait_ge(olink, i + 1)
                        place(slot.unsqueeze(2))
                        place_gated(slot.unsqueeze(2), column(gate, expert), n)
                        x_lo(n)
                        for j in range(halves):
                            lo("gate", stream_over("gate", n), j)
                        gate_in(n, expert)
                        gate_mul(n)
                        for j in range(halves):
                            lo("up", stream_over("up", n), j)
                        up_in(n, expert)
                        h_lo(n)
                        for j in range(halves):
                            lo("down", stream_over("down", n), j)
                        add(n)
            v.memset(small[:, 210:211], 0.0).then_inc(S["fss"], 1)
            dve.wait_ge(S["fss"], 2)
            v.tensor_scalar(small[:, 40:43], small[:, 40:43], 1.0 / D, EPS, ALU.mult, ALU.add).then_inc(S["frt"], 1)
            dve.wait_ge(S["frt"], 2)
            dve.wait_ge(S["fw_in"], 16)
            link(v.reciprocal(small[:, 52:55], small[:, 46:49]))
            for t in range(TILES):
                if t == 2:
                    dve.wait_ge(S["fout"], 32)
                v.scalar_tensor_tensor(out=outb[:, t % 2, :], in0=h[:, t, :], scalar=small[:, 52 + t:53 + t], in1=fw[:, :],
                                       op0=ALU.mult, op1=ALU.mult).then_inc(S["fo"], 1)


_INS = ['x_prompt', 'x_sample', 'mem_prompt', 'state_dn', 'state_dn_conv', 'state_sc_conv', 'cache_mem_k', 'cache_mem_v',
        'w_in', 'dn_conv_w', 'dn_A_log', 'dn_dt_bias', 'dn_norm_w', 'sc_conv_w', 'mem_norm_w', 'w_mem_kv', 'w_br', 'w_o',
        'norm1_w', 'norm2_w', 'w_router', 'b_router', 'w_gate', 'b_gate', 'w_up', 'b_up', 'w_down', 'b_down',
        'final_norm_w']
_OUTS = [(1, 256, 1024), (8, 16, 1024), (1, 1, 4, 128, 128), (1, 1, 3, 1536), (1, 1, 2, 256), (1, 1, 256, 4, 64),
         (1, 1, 256, 4, 64), (1, 8, 4, 128, 128), (1, 8, 3, 1536), (1, 8, 2, 256)]


def kernel(**inputs):
    import concourse.bacc as _bacc
    from concourse.bass_utils import run_bass_kernel_spmd as _run

    nc = _bacc.Bacc("TRN2", target_bir_lowering=False, num_devices=1)
    arrays, aps = {}, {}
    for name in _INS:
        a = np.ascontiguousarray(inputs[name])
        arrays[f"in_{name}_dram"] = a
        aps[name] = nc.dram_tensor(f"in_{name}_dram", a.shape, mybir.dt.from_np(a.dtype), kind="ExternalInput").ap()
    arrays["in_consts_dram"] = constant_table()
    aps["consts"] = nc.dram_tensor("in_consts_dram", (P, CONST_WIDTH), F32, kind="ExternalInput").ap()
    for i, shape in enumerate(_OUTS):
        aps[f"out_{i}"] = nc.dram_tensor(f"out_{i}_dram", shape, F32, kind="ExternalOutput").ap()
    build(nc, aps)
    r = _run(nc, [arrays], core_ids=[0])
    return tuple(r.results[0][f"out_{i}_dram"] for i in range(len(_OUTS)))
```

```python
from contextlib import ExitStack

import concourse.bass as bass
import numpy as np
from concourse import mybir

P = 128
F32 = mybir.dt.float32
F32R = mybir.dt.float32r
BF16 = mybir.dt.bfloat16
I32 = mybir.dt.int32
ALU = mybir.AluOpType
ACT = mybir.ActivationFunctionType
AX = mybir.AxisListType

EPS = 1e-6
HEADS = 4
CAP = 64
LIMIT = 7.0
ALPHA = 1.702
LEVELS = (1, 2, 4, 8, 16, 32)

CONST_COLS = {}
_at = 0
for _name, _n in (
    ("ident", P), ("ones", P), ("upto_prompt", P), ("upto_sample", P), ("block_prompt", P), ("block_sample", P),
    ("before", P), *((f"level{s}", P) for s in LEVELS), ("seq", 8), ("slots2", 2 * CAP), ("fold", CAP), ("rounds", 24),
):
    CONST_COLS[_name] = (_at, _n)
    _at += _n
CONST_WIDTH = _at


def constant_table():
    i = np.arange(P)[:, None]
    j = np.arange(P)[None, :]
    table = np.zeros((P, CONST_WIDTH), np.float32)

    def put(name, value):
        a, n = CONST_COLS[name]
        table[:, a:a + n] = value

    put("ident", i == j)
    put("ones", 1.0)
    for name, block in (("prompt", 64), ("sample", 16)):
        put(f"upto_{name}", (i // block == j // block) & (i <= j))
        put(f"block_{name}", i // block == j // block)
    put("before", i < j)
    for s in LEVELS:
        put(f"level{s}", (i // (2 * s) == j // (2 * s)) & (i // s % 2 == 1) & (j // s % 2 == 0))
    put("seq", i // 16 == np.arange(8)[None, :])
    put("slots2", np.arange(2 * CAP)[None, :] % CAP)
    put("rounds", np.arange(24)[None, :])
    put("fold", i % CAP == np.arange(CAP)[None, :])
    return table


def build(nc, A):
    D = A["x_prompt"].shape[2]
    KT8 = D // P
    E = A["w_router"].shape[2]
    TILES = 3
    TOK = TILES * P
    NSEQ = A["x_sample"].shape[0]
    LS = A["x_sample"].shape[1]
    MAX_OVER = TOK * 4 // CAP
    NQKV = 12
    LP = 3 + 256
    WP = LP + NSEQ * (3 + LS)
    SP2 = 2 + 256
    WS = SP2 + NSEQ * (2 + LS)
    TRUNK_PIECES = 17
    LAST_TRUNK = [max(n for n in range(TRUNK_PIECES) if n % 4 == s) for s in range(4)]

    ctx = ExitStack()
    with ctx:
        def sb(name, shape, dt=F32):
            return ctx.enter_context(nc.sbuf_tensor("sb_" + name, shape, dt))

        def sem(name):
            return ctx.enter_context(nc.semaphore("s_" + name))

        slab_words = 53056
        slab_at = (nc.sbuf_base + 31) // 32 * 32
        sb("slab", [P, slab_words])
        at = {}
        cursor = [0]

        def lay(name, shape, dt=F32, over=None, skip=0):
            words = int(np.prod(shape[1:]))
            words = (words + 7) // 8 * 8
            if over is None:
                at[name] = cursor[0]
                cursor[0] += words
                assert cursor[0] <= slab_words, (name, cursor[0])
            else:
                at[name] = at[over] + skip
            return nc.alloc_sbuf_tensor_at("sb_" + name, shape, dt, offset=slab_at + 4 * at[name])

        ring = lay("ring", [P, 6, 4096])
        h = lay("h", [P, TILES, D])
        r1 = lay("r1", [P, NQKV * WP])
        xn = lay("xn", [P, 3072])
        rq = lay("rq", [P, 4608])
        dg = lay("dg", [P, HEADS, TOK])
        sbb = lay("sbb", [P, 2, TOK])
        sp = lay("sp", [P, 2, WS])
        qm = lay("qm", [P, 2048])
        kvp = lay("kvp", [P, 2, 512])
        wk = lay("wk", [P, 2048])
        mq = lay("mq", [P, 2, TOK])
        st = lay("st", [P, HEADS, P])
        cw = lay("cw", [P, 12 * 28 + 2 * 19])
        co = lay("co", [P, 12 * 27 + 2 * 18])
        scor = lay("scor", [18, 256])
        cst = lay("cst", [P, CONST_WIDTH])
        wab = lay("wab", [P, KT8, 8])
        norms = lay("norms", [P, 3 * KT8 + 1])
        hb = lay("hb", [P, 8])
        small = lay("small", [P, 256])
        over = lay("over", [1, 1 + MAX_OVER], I32)
        pos = lay("pos", [P, 3, E], over="scor")
        gate3 = lay("gate3", [P, 3, 3, E], BF16, over="scor", skip=96)
        gate = lay("gate", [P, 3, E], over="mq", skip=256)
        shift = lay("shift", [P, MAX_OVER], over="mq", skip=384 + 256)
        w_hi = [lay(f"w_hi{k}", [P, 2048], F32R, over="dg", skip=2048 * k) for k in range(4)]
        w_lo = lay("w_lo", [P, 6, 4096], F32R, over="ring")
        assert at["dg"] + 8192 <= at["mq"]
        xparts = lay("xparts", [P, 2, KT8, P], F32R, over="r1")
        hparts = lay("hparts", [P, 8, P], F32R, over="r1", skip=2048)
        g_sb = lay("g_sb", [P, 1024], over="r1", skip=3072)
        u_sb = lay("u_sb", [P, 1024], over="r1", skip=4096)
        y_sb = lay("y_sb", [P, 2, 1024], over="r1", skip=5120)
        pgT = lay("pgT", [P, 2, TOK], over="r1", skip=7168)
        assert at["r1"] + 7936 <= at["rq"]
        sg, hg, hu = g_sb[:, 0:512], g_sb[:, 512:1024], u_sb[:, 0:512]
        ident_b = lay("ident_b", [P, P], BF16, over="wab")
        fw = lay("fw", [P, 1024], over="st")
        onehot = lay("onehot", [P, 3, 2, 2 * CAP], BF16, over="cst", skip=CONST_COLS["level1"][0])
        outb = lay("outb", [P, 2, 1024], over="r1", skip=3072)
        gates_t = lay("gates_t", [P, TOK], over="cst", skip=CONST_COLS["level1"][0] + 384)
        down_bias = lay("down_bias", [P, D], over="st")
        assert at["st"] + 1024 <= at["scor"]

        ps = ctx.enter_context(nc.psum_tensor("ps", [P, 8 * 512], F32))

        def bank(b, n=1):
            return ps[:, b * 512:(b + n) * 512]

        def const(name):
            a, n = CONST_COLS[name]
            return cst[:, a:a + n]

        ident = const("ident")
        ones = const("ones")

        def piece(slot):
            return ring[:, slot, :].rearrange("p (t n) -> p t n", t=KT8)

        rd = ring[:, 4:6, :].rearrange("p a n -> p (a n)")
        mem = rd[:, 0:2048].rearrange("p (a n) -> p a n", a=2)
        xs_mem = rd[:, 2048:4096].rearrange("p (a n) -> p a n", a=2)
        mT = rd[:, 4096:6144].rearrange("p (t n) -> p t n", t=KT8)
        xs = rq[:, 0:3072].rearrange("p (a n) -> p a n", a=3)
        cwr = rq[0:28, 3072:4608]
        scr = dg[0:19, 0, 0:256]
        xnT = xn[:, :].rearrange("p (t n) -> p t n", t=KT8)
        xp = r1[:, :].rearrange("p (c n) -> p c n", c=NQKV)
        qkv = rq[:, :].rearrange("p (c n) -> p c n", c=NQKV)
        cwv = cw[:, 0:336].rearrange("p (c n) -> p c n", n=28)
        scwv = cw[:, 336:374].rearrange("p (c n) -> p c n", n=19)
        cov = co[:, 0:324].rearrange("p (c n) -> p c n", n=27)
        scov = co[:, 324:360].rearrange("p (c n) -> p c n", n=18)
        conv_acc = wk[:, 0:WP]
        cT = wk[:, 512:1280].rearrange("p (c n) -> p c n", c=2)
        hT = wk[:, 1280:2048].rearrange("p (c n) -> p c n", c=2)
        sq4 = rd[:, 0:1536].rearrange("p (c n) -> p c n", c=4)
        nr4 = rd[:, 1536:3072].rearrange("p (c n) -> p c n", c=4)
        cor = qm[0:27, 0:1536]
        NORM_BANKS = ((2, 3, 4, 5), (0, 1, 4, 5))
        kc = rd[:, 0:4096].rearrange("p (s m n) -> p s m n", s=NSEQ, m=2)
        vc = rd[:, 4096:8192].rearrange("p (s m n) -> p s m n", s=NSEQ, m=2)
        kT = r1[:, 0:4608].rearrange("p (b s m) -> p b s m", b=2, s=9)
        qmv = qm[:, :].rearrange("p (s b n) -> p s b n", s=NSEQ, b=2)
        prob = wk[:, 0:1024].rearrange("p (h m) -> p h m", h=4)
        probT = wk[:, 1024:2048].rearrange("p (c n) -> p c n", c=8)
        states = rd[:, 0:4096].rearrange("p (s h v) -> p s h v", s=NSEQ, h=HEADS)

        def t4(region, k):
            return region[:, k * 512:(k + 1) * 512].rearrange("p (h n) -> p h n", h=HEADS)

        gb, dTm, dec, eB, Am, Dm, Fm, Ym, Em = (t4(r1, k) for k in range(9))
        qkT, qd, bk, kd, bv, nwk, um, uT = (t4(rd, 8 + k) for k in range(8))
        oS, osq = t4(wk, 0), t4(wk, 1)
        umask = [x.rearrange("p (s v) -> p s v", s=NSEQ) for x in (wk[:, 1024:2048], r1[:, 2048:3072])]
        EARLY = 10
        FILL = (2, 2, 4)
        early_at = nc.alloc_sbuf_tensor_at("sb_early", [P, EARLY * TOK], F32, offset=slab_at + 4 * at["sp"])
        early = early_at[:, :].rearrange("p (k n) -> p k n", k=EARLY)
        assert at["sp"] + EARLY * TOK <= at["wk"]
        mg = rq[:, 0:3072].rearrange("p (t n) -> p t n", t=KT8)
        sig = r1[:, 0:1536].rearrange("p (a n) -> p a n", a=4)
        x2 = xn[:, :].rearrange("p (a n) -> p a n", a=3)
        x2T = r1[:, 0:3072].rearrange("p (t n) -> p t n", t=KT8)
        w2b = r1[:, 3072:4096]
        split = rq[:, :].bitcast(BF16).rearrange("p (k a n) -> p k a n", k=3, a=3)
        wr = qm[:, 0:256].rearrange("p (t e) -> p t e", t=KT8)
        tables = r1[:, 4096:4800]
        br = tables[:, 0:E]
        lg = tables[:, 32:128].rearrange("p (a e) -> p a e", a=3)
        rt = [tables[:, 128 + 96 * k:224 + 96 * k].rearrange("p (a e) -> p a e", a=3) for k in range(6)]
        gs = small[:, 228:230]
        bg = mq[:, 0, 0:256]
        bu = mq[:, 1, 0:256]
        gT = gates_t[0:E, :]
        bd = down_bias[0:E, :]
        brow = wk[:, 0:512].rearrange("p (b r n) -> p b r n", b=2, r=2)
        halves = 4

        def stream(kind, n):
            if isinstance(n, int) and n < E:
                return {"gate": max(12 * n - 4, 0), "up": 12 * n + 4, "down": 12 * n + (12 if n < E - 1 else 8)}[kind]
            return {"gate": 12 * n - 4, "up": 12 * n + 4, "down": 12 * n + 12}[kind]

        def stream_over(kind, n):
            return 12 * n + {"gate": 0, "up": 4, "down": 8}[kind]

        MATS = ("gate", "up", "down")

        names = """cst x_in mem_in rows_in vec_in wab_in kc_in vc_in st_in rout_in bdn_in fw_in
            ss rt5 xs xtr xT cwtr cwT pj pjev conv silu co cotr cor kv_out corout
            sq nsum nadd nsqrt norm
            ktr kT qm sc soft pexp pn ptr pT pv ym
            gates gcum gex gbr cumb dexp dmul kk tok tokev lv Fready Yready Gready wkt nwk u uev utr uready oready oev
            osum onorm snew st_upd um yd st_all
            ab abx abl abg early earlyout
            gp gz gsig mrg wo hadd ss2 rt2 x2 x2tr x2T lgm lgx sel posm brt bT gtr gT bdm bdd split rest overx
            P xg xhi xlo gev gT2 hg sgm uout uT2 hf hhi hlo yev pgt gsc pgtev acc accrd hi lo used
            fss frt fo fout out""".split()
        assert len(set(names)) == len(names)
        S = {n: sem(n) for n in names}
        loaded = [sem(f"loaded{k}") for k in range(6)]
        vlink, mlink, olink = sem("vlink"), sem("mlink"), sem("olink")

        block = ctx.enter_context(nc.Block())

        win = A["w_in"][0].rearrange("(p t) n -> p t n", t=KT8)
        wbr = A["w_br"][0].rearrange("(k p) n -> p k n", p=P)
        wo = A["w_o"][0].rearrange("(k p) n -> p k n", p=P)
        gcol = 3080
        trunk = [A["w_mem_kv"][0].rearrange("(p t) n -> p t n", t=KT8)]
        trunk += [win[:, :, c:c + 512] for c in (0, 512, 1024, 1544, 2056, 2568)]
        for half in range(2):
            trunk += [win[:, :, gcol + 1024 * b + 512 * half:gcol + 1024 * b + 512 * half + 512] for b in range(3)]
            trunk += [wbr[:, :, 512 * half:512 * half + 512]]
        trunk += [wo[:, :, 512 * k:512 * k + 512] for k in range(2)]
        assert len(trunk) == TRUNK_PIECES
        wg = A["w_gate"][0].rearrange("e (p t) n -> e p t n", t=KT8)
        wu = A["w_up"][0].rearrange("e (p t) n -> e p t n", t=KT8)
        wd = A["w_down"][0].rearrange("e (f p) n -> e p f n", p=P)

        x_s = A["x_sample"].rearrange("s l d -> (s l) d")
        outs = [A[f"out_{k}"] for k in range(10)]
        yp = outs[0][0].rearrange("(a p) d -> a p d", p=P)
        ys = outs[1].rearrange("s l d -> (s l) d")

        @block.sync
        def _(sp_):
            dma = sp_.dma_start

            def through(n):
                if n in (7, 8):
                    sp_.wait_ge(S["early"], 4 * (n - 6))
                elif n < 7:
                    sp_.wait_ge(S["pj"], 2 + 4 * n + (1 if n >= 4 else 0))
                elif n < 15:
                    sp_.wait_ge(S["gz"], 12 * ((n - 7) // 4) + min(4 * ((n - 7) % 4) + 4, 12))
                else:
                    sp_.wait_ge(S["wo"], 3 * (n - 14))

            def trunk_piece(n):
                if n >= 4:
                    through(n - 4)
                dma(piece(n % 4), trunk[n]).then_inc(loaded[n % 4], 16)

            dma(h[:, 0:2, :], A["x_prompt"][0].rearrange("(a p) d -> p a d", p=P)).then_inc(S["x_in"], 16)
            dma(h[:, 2, :], x_s).then_inc(S["x_in"], 16)
            dma(cst[:, :], A["consts"]).then_inc(S["cst"], 16)
            dma(mem, A["mem_prompt"][0].rearrange("(a p) d -> p a d", p=P)).then_inc(S["mem_in"], 16)
            trunk_piece(0)
            dma(cwr[0:24, :], A["state_dn_conv"][0].rearrange("s r c -> (s r) c")).then_inc(S["rows_in"], 16)
            dma(cwr[24:28, :], A["dn_conv_w"][0]).then_inc(S["rows_in"], 16)
            dma(scr[0:16, :], A["state_sc_conv"][0].rearrange("s r c -> (s r) c")).then_inc(S["rows_in"], 16)
            dma(scr[16:19, :], A["sc_conv_w"][0]).then_inc(S["rows_in"], 16)
            for k, name in enumerate(("norm1_w", "norm2_w", "mem_norm_w")):
                dma(norms[:, k * KT8:(k + 1) * KT8], A[name][0].rearrange("(p t) -> p t", t=KT8)).then_inc(S["vec_in"], 16)
            dma(norms[:, 24:25], A["dn_norm_w"][0].rearrange("(p o) -> p o", o=1)).then_inc(S["vec_in"], 16)
            dma(hb[:, 0:4], A["dn_A_log"].partition_broadcast(P).rearrange("p o h -> p (o h)")).then_inc(S["vec_in"], 16)
            dma(hb[:, 4:8], A["dn_dt_bias"].partition_broadcast(P).rearrange("p o h -> p (o h)")).then_inc(S["vec_in"], 16)
            trunk_piece(1)
            trunk_piece(2)
            trunk_piece(3)
            dma(wab[:, :, :], win[:, :, 1536:1544]).then_inc(S["wab_in"], 16)
            trunk_piece(4)
            sp_.wait_ge(S["pjev"], 2)
            for k in range(2):
                dma(outs[5 + k][0, 0].rearrange("(a p) h d -> p a (h d)", p=P),
                    kvp[:, :, 256 * k:256 * k + 256]).then_inc(S["kv_out"], 16)
            dma(kc, A["cache_mem_k"][0].rearrange("s (m p) h d -> p s m (h d)", p=P)).then_inc(S["kc_in"], 16)
            dma(vc, A["cache_mem_v"][0].rearrange("s (m p) h d -> p s m (h d)", p=P)).then_inc(S["vc_in"], 16)
            for n in range(5, 11):
                trunk_piece(n)
            sp_.wait_ge(S["cor"], 4)
            dma(outs[3][0, 0], cor[0:3, :]).then_inc(S["corout"], 16)
            dma(outs[8][0].rearrange("s r c -> (s r) c"), cor[3:27, :]).then_inc(S["corout"], 16)
            dma(outs[4][0, 0], scor[0:2, :]).then_inc(S["out"], 16)
            dma(outs[9][0].rearrange("s r c -> (s r) c"), scor[2:18, :]).then_inc(S["out"], 16)
            sp_.wait_ge(S["norm"], 2)
            dma(states, A["state_dn"][0].rearrange("s h k v -> k s h v")).then_inc(S["st_in"], 16)
            trunk_piece(11)
            sp_.wait_ge(S["st_all"], 1)
            dma(outs[2][0, 0].rearrange("h k v -> k h v"), st[:, :, :]).then_inc(S["out"], 16)
            trunk_piece(12)
            sp_.wait_ge(S["st_all"], 2)
            dma(outs[7][0].rearrange("s h k v -> k s h v"), states).then_inc(S["out"], 16)
            for n in (14, 13, 15, 16):
                trunk_piece(n)
            sp_.wait_ge(S["mrg"], EARLY)
            dma(wr, A["w_router"][0].rearrange("(p t) e -> p t e", t=KT8)).then_inc(S["rout_in"], 16)
            dma(br, A["b_router"].partition_broadcast(P).rearrange("p o e -> p (o e)")).then_inc(S["rout_in"], 16)
            sp_.wait_ge(S["mrg"], 24)
            dma(w2b, A["norm2_w"].partition_broadcast(P).rearrange("p o d -> p (o d)")).then_inc(S["rout_in"], 16)
            sp_.wait_ge(S["out"], 64)
            dma(bd, A["b_down"][0]).then_inc(S["bdn_in"], 16)
            for k, name in enumerate(("b_gate", "b_up")):
                dma(brow[:, k, :, :], A[name][0].rearrange("(r e) (f p) -> (e f) r p", r=2, p=P)).then_inc(S["bdn_in"], 16)

            weights = {"gate": wg, "up": wu, "down": wd}

            def matrix(kind, expert, free=None):
                for k in range(2):
                    if free is not None:
                        sp_.wait_ge(S["used"], free + 2 * k)
                    s = 2 * MATS.index(kind) + k
                    src = weights[kind][bass.ds(expert, 1), :, 4 * k:4 * k + 4, :]
                    dma(ring[:, s, :], src.rearrange("e p t n -> p (e t) n")).then_inc(loaded[s], 16)

            through(LAST_TRUNK[0])
            through(LAST_TRUNK[1])
            matrix("gate", 0)
            through(LAST_TRUNK[2])
            through(LAST_TRUNK[3])
            matrix("up", 0)
            sp_.wait_ge(S["out"], 64)
            matrix("down", 0)
            matrix("gate", 1, stream("gate", 0) + 2)
            matrix("up", 1, stream("up", 0) + 2)
            sp_.wait_ge(S["accrd"], 1)
            dma(fw[:, :], A["final_norm_w"].partition_broadcast(P)).then_inc(S["fw_in"], 16)
            with sp_.Fori(1, E - 1) as e:
                matrix("gate", e + 1, stream("gate", e) + 2)
                matrix("down", e, stream("down", e - 1) + 2)
                matrix("up", e + 1, stream("up", e) + 2)
            matrix("down", E - 1, stream("down", E - 2) + 2)
            sp_.wait_ge(S["overx"], 1)
            n_over = sp_.value_load(over[0:1, 0:1], min_val=0, max_val=MAX_OVER)
            with sp_.If(n_over > 0):
                with sp_.Fori(0, MAX_OVER) as i:
                    with sp_.If(n_over > i):
                        expert = sp_.value_load(over[0:1, bass.ds(i + 1, 1)], min_val=0, max_val=E - 1)
                        for kind in MATS:
                            matrix(kind, expert, stream_over(kind, i + E - 1) + 2)
            for t in range(TILES):
                sp_.wait_ge(S["fo"], t + 1)
                dma(yp[t] if t < 2 else ys, outb[:, t % 2, :]).then_inc(S["fout"], 16)
            sp_.wait_ge(S["fout"], 48)
            sp_.wait_ge(S["out"], 64)
            sp_.wait_ge(S["kv_out"], 32)
            sp_.wait_ge(S["corout"], 32)

        upto = [const("upto_prompt"), const("upto_prompt"), const("upto_sample")]
        blockones = [const("block_prompt"), const("block_prompt"), const("block_sample")]
        tile_levels = [LEVELS, LEVELS, LEVELS[:4]]
        LEVEL_STEPS = [sum(len(tile_levels[u]) - 1 for u in range(t)) for t in range(TILES + 1)]

        @block.tensor
        def _(pe):
            mm = nc.tensor.matmul

            def tr(out, in_, n=P):
                return nc.tensor.transpose(out, in_, ident[0:n, 0:n])

            pe.wait_ge(S["cst"], 16)
            for t in range(5):
                pe.wait_ge(S["xs"], t + 1)
                if t >= 4:
                    pe.wait_ge(S["xT"], t - 3)
                src = xs[:, t, :] if t < 3 else xs_mem[:, t - 3, :]
                for k in range(KT8):
                    last = tr(bank((2 * t + k // 4) % 8)[:, (k % 4) * P:(k % 4 + 1) * P], src[:, k::KT8])
                last.then_inc(S["xtr"], 1)
            pe.wait_ge(S["rows_in"], 64)
            pe.wait_ge(S["xT"], 2)
            for c in range(12):
                tr(bank(2)[:, c * 28:(c + 1) * 28], cwr[:, c * P:(c + 1) * P], 28)
            for c in range(2):
                last = tr(bank(2)[:, 336 + c * 19:336 + (c + 1) * 19], scr[:, c * P:(c + 1) * P], 19)
            last.then_inc(S["cwtr"], 1)

            def step_start(q):
                if q >= 8:
                    pe.wait_ge(S["pjev"], q - 7)

            pe.wait_ge(S["xT"], 5)
            pe.wait_ge(S["cwT"], 1)
            pe.wait_ge(loaded[0], 16)
            for q in range(2):
                for t in range(KT8):
                    last = mm(bank(q), mT[:, t, q * P:(q + 1) * P], piece(0)[:, t, :], start=(t == 0), stop=(t == KT8 - 1))
                last.then_inc(S["pj"], 1)

            q = 2
            for n in range(1, 7):
                pe.wait_ge(loaded[n % 4], 16 * (n // 4 + 1))
                if n == 4:
                    pe.wait_ge(S["wab_in"], 16)
                    step_start(q)
                    for a in range(TILES):
                        for t in range(KT8):
                            last = mm(bank(q % 8)[:, a * 8:(a + 1) * 8], xnT[:, t, a * P:(a + 1) * P], wab[:, t, :],
                                      start=(t == 0), stop=(t == KT8 - 1))
                    last.then_inc(S["pj"], 1)
                    q += 1
                for c in range(4):
                    step_start(q)
                    for t in range(KT8):
                        last = mm(bank(q % 8)[:, 0:TOK], piece(n % 4)[:, t, c * P:(c + 1) * P], xnT[:, t, :],
                                  start=(t == 0), stop=(t == KT8 - 1))
                    last.then_inc(S["pj"], 1)
                    q += 1
            assert q == 27

            pe.wait_ge(S["pjev"], 27)
            pe.wait_ge(S["co"], 2)
            for c in range(12):
                last = tr(bank(4 + c // 4)[0:27, (c % 4) * P:(c % 4 + 1) * P], cov[:, c, :])
                if c % 4 == 3:
                    last.then_inc(S["cotr"], 1)
            for c in range(2):
                last = tr(bank(7)[0:18, c * P:(c + 1) * P], scov[:, c, :])
            last.then_inc(S["cotr"], 1)

            pe.wait_ge(S["kc_in"], 16)
            pe.wait_ge(S["cor"], 4)
            for s in range(9):
                if s >= 8:
                    pe.wait_ge(S["kT"], s - 7)
                for b in range(2):
                    for m in range(2):
                        src = kc[:, s, m, b * P:(b + 1) * P] if s < 8 else kvp[:, m, b * P:(b + 1) * P]
                        last = tr(bank(s % 8)[:, (2 * b + m) * P:(2 * b + m + 1) * P], src)
                last.then_inc(S["ktr"], 1)
            def norm_sums(g):
                pe.wait_ge(S["sq"], g + 1)
                for c in range(4):
                    last = mm(bank(NORM_BANKS[g][c])[:, 0:TOK], ones, sq4[:, c, :], start=True, stop=True)
                last.then_inc(S["nsum"], 1)

            pe.wait_ge(S["kT"], 9)
            for t in range(TILES):
                if t >= 1:
                    pe.wait_ge(S["ym"], t)
                if t == 2:
                    pe.wait_ge(S["qm"], 1)
                    pe.wait_ge(S["nadd"], 2)
                    pe.wait_ge(S["vc_in"], 16)
                for hh in range(4):
                    o = bank(2 * t + hh % 2)[:, (hh // 2) * 256:(hh // 2) * 256 + 256]
                    rows = slice(64 * (hh % 2), 64 * (hh % 2) + 64)
                    if t < 2:
                        last = mm(o, mq[rows, hh // 2, t * P:(t + 1) * P], kT[rows, hh // 2, 8, :], start=True, stop=True)
                    else:
                        for s in range(NSEQ):
                            last = mm(o, qmv[rows, s, hh // 2, :], kT[rows, hh // 2, s, :], start=(s == 0), stop=(s == NSEQ - 1))
                last.then_inc(S["sc"], 1)
                if t < 2:
                    norm_sums(t)
                pe.wait_ge(S["pn"], t + 1)
                for hh in range(4):
                    for m in range(2):
                        k = 2 * hh + m
                        last = tr(bank(6 + k // 4)[:, (k % 4) * P:(k % 4 + 1) * P],
                                  prob[:, 2 * (hh % 2) + hh // 2, m * P:(m + 1) * P])
                last.then_inc(S["ptr"], 1)
                pe.wait_ge(S["pT"], t + 1)
                for hh in range(4):
                    rows = slice(64 * (hh % 2), 64 * (hh % 2) + 64)
                    o = bank(2 * t)[rows, (hh // 2) * P:(hh // 2 + 1) * P]
                    if t < 2:
                        for m in range(2):
                            last = mm(o, kvp[:, m, 256 + 64 * hh:320 + 64 * hh], probT[:, 2 * hh + m, :],
                                      start=(m == 0), stop=(m == 1))
                    else:
                        for s in range(NSEQ):
                            for m in range(2):
                                last = mm(o[:, s * LS:(s + 1) * LS], vc[:, s, m, 64 * hh:64 * hh + 64],
                                          probT[:, 2 * hh + m, s * LS:(s + 1) * LS], start=(m == 0), stop=(m == 1))
                last.then_inc(S["pv"], 1)

            filled = [0]

            def fill(steps):
                for _ in range(steps):
                    k, t = divmod(filled[0], KT8)
                    if k == EARLY:
                        return
                    n = 7 + k // 4
                    if t == 0:
                        pe.wait_ge(loaded[n % 4], 16 * (n // 4 + 1))
                        if k >= 2:
                            pe.wait_ge(S["earlyout"], k - 1)
                    c = k % 4
                    ins = mm(bank(3 - 2 * (k % 2))[:, 0:TOK], piece(n % 4)[:, t, c * P:(c + 1) * P], xnT[:, t, :],
                             start=(t == 0), stop=(t == KT8 - 1))
                    if t == KT8 - 1:
                        ins.then_inc(S["early"], 1)
                    filled[0] += 1

            pe.wait_ge(S["norm"], 2)
            pe.wait_ge(S["gates"], 1)
            pe.wait_ge(S["ym"], 3)
            for t in range(TILES):
                cols = slice(t * P, (t + 1) * P)
                mm(bank(0)[:, 0:4], upto[t], small[:, 12 * t:12 * t + 4], start=True, stop=True)
                mm(bank(0)[:, 4:8], blockones[t], small[:, 12 * t:12 * t + 4], start=True, stop=True).then_inc(S["gcum"], 1)
                for hh in range(HEADS):
                    mm(bank(2)[:, hh * P:(hh + 1) * P], qkv[:, 4 + hh, cols], qkv[:, 4 + hh, cols], start=True, stop=True)
                    last = mm(bank(3)[:, hh * P:(hh + 1) * P], qkv[:, 4 + hh, cols], qkv[:, hh, cols], start=True, stop=True)
                last.then_inc(S["kk"], 1)
                for hh in range(HEADS):
                    tr(bank(4)[:, hh * P:(hh + 1) * P], qkv[:, 4 + hh, cols])
                    last = tr(bank(5)[:, hh * P:(hh + 1) * P], qkv[:, 8 + hh, cols])
                last.then_inc(S["tok"], 1)
                pe.wait_ge(S["gbr"], t + 1)
                if t >= 1:
                    pe.wait_ge(S["onorm"], 2 * t - 1)
                for hh in range(HEADS):
                    last = mm(bank(1)[:, hh * P:(hh + 1) * P], gb[:, hh, :], upto[t], start=True, stop=True)
                last.then_inc(S["cumb"], 1)
                pe.wait_ge(S["lv"], LEVEL_STEPS[t] + 2 * t + 1)
                for hh in range(HEADS):
                    last = tr(bank(6)[:, hh * P:(hh + 1) * P], Dm[:, hh, :])
                last.then_inc(S["Fready"], 1)
                fill(FILL[0])
                for n in range(1, len(tile_levels[t])):
                    k = LEVEL_STEPS[t] + n
                    pe.wait_ge(S["lv"], k + 2 * t + 1)
                    for hh in range(HEADS):
                        last = mm(bank(7)[:, hh * P:(hh + 1) * P], Em[:, hh, :], Fm[:, hh, :], start=True, stop=True)
                    last.then_inc(S["Yready"], 1)
                    fill(FILL[1])
                    pe.wait_ge(S["uready"], k)
                    for hh in range(HEADS):
                        mm(bank(6)[:, hh * P:(hh + 1) * P], Dm[:, hh, :], Ym[:, hh, :], start=True, stop=True)
                        last = mm(bank(2)[:, hh * P:(hh + 1) * P], Ym[:, hh, :], Dm[:, hh, :], start=True, stop=True)
                    last.then_inc(S["Gready"], 1)
                    fill(FILL[2])
                pe.wait_ge(S["lv"], LEVEL_STEPS[t + 1] + 2 * t + 2)
                pe.wait_ge(S["tokev"], t + 1)
                for hh in range(HEADS):
                    last = mm(bank(4)[:, hh * P:(hh + 1) * P], bk[:, hh, :], Fm[:, hh, :], start=True, stop=True)
                last.then_inc(S["wkt"], 1)
                pe.wait_ge(S["nwk"], t + 1)
                if t < 2:
                    for b in range(2):
                        g = 2 * t + b
                        rows = slice(64 * b, 64 * b + 64)
                        if g >= 1:
                            pe.wait_ge(S["st_upd"], g)
                        for hh in range(HEADS):
                            o = bank(5)[rows, hh * P:(hh + 1) * P]
                            last = mm(o, Fm[:, hh, rows], bv[:, hh, :], start=True, stop=(g == 0))
                            if g >= 1:
                                last = mm(o, nwk[:, hh, rows], st[:, hh, :], start=False, stop=True)
                        last.then_inc(S["u"], 1)
                        for hh in range(HEADS):
                            if g >= 1:
                                mm(bank(0)[:, hh * P + 64 * b:hh * P + 64 * b + 64], st[:, hh, :], qd[:, hh, rows],
                                   start=True, stop=False)
                            if hh == 0:
                                pe.wait_ge(S["uev"], g + 1)
                            mm(bank(0)[:, hh * P + 64 * b:hh * P + 64 * b + 64], um[rows, hh, :], qkT[rows, hh, rows],
                               start=(g == 0), stop=True)
                        for hh in range(HEADS):
                            last = mm(bank(6 + b)[:, hh * P:(hh + 1) * P], kd[rows, hh, :], um[rows, hh, :],
                                      start=True, stop=True)
                        last.then_inc(S["snew"], 1)
                else:
                    pe.wait_ge(S["st_in"], 16)
                    for hh in range(HEADS):
                        o = bank(5)[:, hh * P:(hh + 1) * P]
                        for s in range(NSEQ):
                            c = slice(s * LS, (s + 1) * LS)
                            mm(o[:, c], states[:, s, hh, :], nwk[:, hh, c], start=(s == 0), stop=False,
                               skip_group_check=True)
                        last = mm(o, bv[:, hh, :], Fm[:, hh, :], start=False, stop=True, skip_group_check=True)
                    last.then_inc(S["u"], 1)
                    pe.wait_ge(S["utr"], 1)
                    for hh in range(HEADS):
                        last = tr(bank(2)[:, hh * P:(hh + 1) * P], uT[:, hh, :])
                    last.then_inc(S["u"], 1)
                    pe.wait_ge(S["uev"], 5)
                    for hh in range(HEADS):
                        o = bank(0)[:, hh * P:(hh + 1) * P]
                        for s in range(NSEQ):
                            c = slice(s * LS, (s + 1) * LS)
                            mm(o[:, c], states[:, s, hh, :], qd[:, hh, c], start=(s == 0), stop=False,
                               skip_group_check=True)
                        last = mm(o, um[:, hh, :], qkT[:, hh, :], start=False, stop=True, skip_group_check=True)
                    last.then_inc(S["oready"], 1)

                def state_product(hh):
                    pe.wait_ge(S["um"], hh + 1)
                    if hh >= 2:
                        pe.wait_ge(S["st_upd"], 3 + hh)
                    for k in range(2):
                        last = mm(bank((6, 2)[hh % 2] + k), kd[:, hh, :],
                                  umask[hh % 2][:, 4 * k:4 * k + 4, :].rearrange("p s v -> p (s v)"), start=True, stop=True)
                    last.then_inc(S["snew"], 1)

                if t == 2:
                    state_product(0)
                pe.wait_ge(S["oev"], t + 1)
                pe.wait_ge(S["earlyout"], filled[0] // KT8)
                last = mm(bank(1), ones, osq.rearrange("p h n -> p (h n)"), start=True, stop=True)
                last.then_inc(S["osum"], 1)
                if t == 2:
                    for hh in range(1, HEADS):
                        state_product(hh)

            pe.wait_ge(S["yd"], 3)
            k = 0
            branches = ((0, 4, dg), (4, 2, sbb), (6, 2, mq))
            for half in range(2):
                for b, (k0, kn, src) in enumerate(branches):
                    for c in range(4):
                        if k >= 4:
                            pe.wait_ge(S["mrg"], k - 3)
                        if k == 1:
                            pe.wait_ge(S["st_upd"], 8)
                        n = 7 + 4 * half + b
                        pe.wait_ge(loaded[n % 4], 16 * (n // 4 + 1))
                        w = piece(n % 4)
                        if k >= EARLY:
                            for t in range(KT8):
                                last = mm(bank(2 * (k % 4))[:, 0:TOK], w[:, t, c * P:(c + 1) * P], xnT[:, t, :],
                                          start=(t == 0), stop=(t == KT8 - 1))
                            last.then_inc(S["gp"], 1)
                        n = 10 + 4 * half
                        pe.wait_ge(loaded[n % 4], 16 * (n // 4 + 1))
                        w = piece(n % 4)
                        for j in range(kn):
                            last = mm(bank(2 * (k % 4) + 1)[:, 0:TOK], w[:, k0 + j, c * P:(c + 1) * P], src[:, j, :],
                                      start=(j == 0), stop=(j == kn - 1))
                        last.then_inc(S["gz"], 1)
                        k += 1

            pe.wait_ge(S["mrg"], 24)
            for half in range(2):
                n = 15 + half
                pe.wait_ge(loaded[n % 4], 16 * (n // 4 + 1))
                for a in range(TILES):
                    for j in range(KT8):
                        last = mm(bank(3 * half + a), mg[:, j, a * P:(a + 1) * P], piece(n % 4)[:, j, :],
                                  start=(j == 0), stop=(j == KT8 - 1))
                    last.then_inc(S["wo"], 1)

            pe.wait_ge(S["bdn_in"], 48)
            for k in range(2):
                for r in range(2):
                    last = tr(bank(6)[:, (2 * k + r) * P:(2 * k + r + 1) * P], brow[:, k, r, :])
            last.then_inc(S["brt"], 1)
            def logits(a):
                pe.wait_ge(S["x2T"], a + 1)
                for t in range(KT8):
                    last = mm(bank(7)[:, a * E:(a + 1) * E], x2T[:, t, a * P:(a + 1) * P], wr[:, t, :],
                              start=(t == 0), stop=(t == KT8 - 1))
                return last

            pe.wait_ge(S["hadd"], 6)
            pe.wait_ge(S["rout_in"], 48)
            for a in range(TILES):
                pe.wait_ge(S["x2"], a + 1)
                for k in range(KT8):
                    last = tr(bank(2 * a + k // 4)[:, (k % 4) * P:(k % 4 + 1) * P], x2[:, a, k::KT8])
                last.then_inc(S["x2tr"], 1)
                if a:
                    logits(a - 1)
            logits(TILES - 1).then_inc(S["lgm"], 1)
            pe.wait_ge(S["sel"], 1)
            mask = rt[0]
            for a in range(TILES):
                for b in range(a):
                    mm(bank(0)[:, a * E:(a + 1) * E], ones, mask[:, b, :], start=(b == 0), stop=False)
                mm(bank(0)[:, a * E:(a + 1) * E], const("before"), mask[:, a, :], start=(a == 0), stop=True)
            for a in range(TILES):
                last = mm(bank(0)[:, 3 * E:4 * E], ones, mask[:, a, :], start=(a == 0), stop=(a == TILES - 1))
            last.then_inc(S["posm"], 1)
            for a in range(TILES):
                last = tr(bank(1)[0:E, a * P:(a + 1) * P], gate[:, a, :])
            last.then_inc(S["gtr"], 1)
            pe.wait_ge(S["split"], 3)

            def gather(m, half, slots=2):
                pe.wait_ge(S["P"], m + 1)
                for t in range(4 * half, 4 * half + 4):
                    for a in range(TILES):
                        for k in range(3):
                            last = mm(bank(6, 2)[:, t * P:t * P + slots * CAP], split[:, k, a, t::KT8],
                                      onehot[:, a, 0:slots, 0:CAP],
                                      start=(a == 0 and k == 0), stop=(a == TILES - 1 and k == 2))
                last.then_inc(S["xg"], 1)

            def product(kind, q0, b, x):
                for j in range(halves):
                    pe.wait_ge(S["lo"], q0 + j + 1)
                    lo_part = w_lo[:, 2 * MATS.index(kind) + j // 2, 2048 * (j % 2):2048 * (j % 2) + 2048]
                    for i in range(2):
                        k = 2 * j + i
                        for c in range(2):
                            cols = slice(1024 * i + 512 * c, 1024 * i + 512 * c + 512)
                            mm(bank(b + c), x[:, k, :], w_hi[j][:, cols], start=(k == 0), stop=False)
                            last = mm(bank(b + c), x[:, k, :], lo_part[:, cols], start=False, stop=(k == 7))
                    last.then_inc(S["used"], 1)

            def turned(b, src, done):
                for f in range(8):
                    last = mm(bank(b)[:, f * CAP:(f + 1) * CAP], src[:, f * P:(f + 1) * P], const("fold"), start=True, stop=True)
                last.then_inc(done, 1)

            def gate_turned(n):
                pe.wait_ge(S["gev"], n + 1)
                turned(4, g_sb, S["gT2"])

            def up_turned(n):
                pe.wait_ge(S["uout"], n + 1)
                turned(5, u_sb, S["uT2"])

            def slots_turned(i, b, e):
                for a in range(TILES):
                    mm(bank(b)[:, a * P:(a + 1) * P], onehot[:, a, i, :], ident_b[:, :], start=True, stop=True)
                for a in range(TILES):
                    for k in range(3):
                        last = mm(bank(b)[:, TOK:TOK + 1], onehot[:, a, i, :], gate3[:, a, k, bass.ds(e, 1)],
                                  start=(a == 0 and k == 0), stop=(a == TILES - 1 and k == 2))
                last.then_inc(S["pgt"], 1)

            def scatter(m, a, items=2):
                for k in range(2):
                    if a:
                        pe.wait_ge(S["accrd"], 6 * m + 2 * a + k)
                    for i in range(items):
                        last = mm(bank(6 + k), pgT[:, i, a * P:(a + 1) * P], y_sb[:, i, 512 * k:512 * k + 512],
                                  start=(i == 0), stop=(i == items - 1))
                    last.then_inc(S["acc"], 1)

            def item_a(m, n, first=False):
                gate_turned(n)
                if not first:
                    pe.wait_ge(S["yev"], n)
                    pe.wait_ge(S["pgtev"], n)
                    scatter(m - 1, 0)
                product("up", stream("up", n), 2, xparts[:, 0])
                if not first:
                    scatter(m - 1, 1)
                up_turned(n)
                product("gate", stream("gate", n + 1), 0, xparts[:, 1])
                if not first:
                    scatter(m - 1, 2)
                pe.wait_ge(S["hlo"], n + 1)
                slots_turned(0, 4, n)
                slots_turned(1, 5, n + 1)
                product("down", stream("down", n), 2, hparts)

            def item_b(m, n, last=False):
                pe.wait_ge(S["pgtev"], n + 1)
                gate_turned(n)
                if not last:
                    pe.wait_ge(S["accrd"], 6 * m + 1)
                    gather(m + 1, 0)
                pe.wait_ge(S["yev"], n)
                product("up", stream("up", n), 2, xparts[:, 1])
                if not last:
                    gather(m + 1, 1)
                up_turned(n)
                if not last:
                    pe.wait_ge(S["xlo"], m + 2)
                    product("gate", stream("gate", n + 1), 0, xparts[:, 0])
                pe.wait_ge(S["hlo"], n + 1)
                product("down", stream("down", n), 2, hparts)

            def down_biases(a, b):
                for k in range(2):
                    last = mm(bank(b + k), gT[:, a * P:(a + 1) * P], bd[:, 512 * k:512 * k + 512], start=True, stop=True)
                last.then_inc(S["bdm"], 1)

            gather(0, 0)
            gather(0, 1)
            pe.wait_ge(S["gT"], 1)
            down_biases(0, 2)
            down_biases(1, 4)
            pe.wait_ge(S["xlo"], 1)
            product("gate", 0, 0, xparts[:, 0])
            pe.wait_ge(S["bdd"], 1)
            down_biases(2, 2)
            pe.wait_ge(S["accrd"], 1)
            item_a(0, 0, first=True)
            item_b(0, 1)
            with pe.Fori(1, E // 2 - 1) as m:
                item_a(m, 2 * m)
                item_b(m, 2 * m + 1)
            item_a(E // 2 - 1, E - 2)
            item_b(E // 2 - 1, E - 1, last=True)
            pe.wait_ge(S["yev"], E)
            pe.wait_ge(S["accrd"], 3 * E - 5)
            for a in range(TILES):
                scatter(E // 2 - 1, a)
            pe.wait_ge(S["overx"], 1)
            n_over = pe.value_load(over[0:1, 0:1], min_val=0, max_val=MAX_OVER)
            with pe.If(n_over > 0):
                with pe.Fori(0, MAX_OVER) as i:
                    with pe.If(n_over > i):
                        n = i + E
                        m = i + E // 2
                        pe.wait_ge(S["accrd"], 6 * m + 1)
                        expert = pe.value_load(over[0:1, bass.ds(i + 1, 1)], min_val=0, max_val=E - 1)
                        gather(m, 0, slots=1)
                        gather(m, 1, slots=1)
                        pe.wait_ge(S["xlo"], m + 1)
                        product("gate", stream_over("gate", n), 0, xparts[:, 0])
                        gate_turned(n)
                        product("up", stream_over("up", n), 2, xparts[:, 0])
                        up_turned(n)
                        pe.wait_ge(S["hlo"], n + 1)
                        slots_turned(0, 4, expert)
                        product("down", stream_over("down", n), 2, hparts)
                        pe.wait_ge(S["yev"], n + 1)
                        pe.wait_ge(S["pgtev"], n + 1)
                        for a in range(TILES):
                            scatter(m, a, items=1)

        @block.scalar
        def _(act):
            f = nc.scalar.activation
            act.wait_ge(S["x_in"], 32)
            for t in range(3):
                f(xs[:, t, :], h[:, t, :], ACT.Square, accum_out=small[:, 40 + t:41 + t])
            act.wait_ge(S["mem_in"], 16)
            for t in range(2):
                last = f(xs_mem[:, t, :], mem[:, t, :], ACT.Square, accum_out=small[:, 43 + t:44 + t])
            last.then_inc(S["ss"], 1)
            act.wait_ge(S["ss"], 2)
            f(small[:, 46:51], small[:, 40:45], ACT.Sqrt).then_inc(S["rt5"], 1)
            def xp_sample(c):
                return xp[:, c, LP:WP].rearrange("p (s k) -> p s k", k=3 + LS)[:, :, 3:3 + LS]

            act.wait_ge(S["cwtr"], 1)
            f(cw[:, :], bank(2)[:, 0:374], ACT.Copy).then_inc(S["cwT"], 1)
            def silu(c):
                act.wait_ge(S["conv"], c + 1)
                f(qkv[:, c, 0:256], conv_acc[:, 0:256], ACT.Silu)
                f(qkv[:, c, 256:TOK].rearrange("p (s k) -> p s k", k=LS),
                  conv_acc[:, LP:WP].rearrange("p (s k) -> p s k", k=3 + LS)[:, :, 0:LS], ACT.Silu).then_inc(S["silu"], 1)

            for q in range(27):
                b = bank(q % 8)
                act.wait_ge(S["pj"], q + 1)
                if q < 2:
                    last = f(kvp[:, q, :], b, ACT.Copy)
                elif q < 14:
                    f(xp[:, q - 2, 3:LP], b[:, 0:256], ACT.Copy)
                    last = f(xp_sample(q - 2), b[:, 256:TOK].rearrange("p (s k) -> p s k", k=LS), ACT.Copy)
                elif q == 14:
                    last = f(small[:, 64:88], b[:, 0:24], ACT.Copy)
                elif q < 19:
                    last = f(dg[:, q - 15, :], b[:, 0:TOK], ACT.Silu)
                elif q < 21:
                    last = f(sbb[:, q - 19, :], b[:, 0:TOK], ACT.Copy)
                elif q < 23:
                    last = f(cT[:, q - 21, :], b[:, 0:TOK], ACT.Copy)
                elif q < 25:
                    last = f(hT[:, q - 23, :], b[:, 0:TOK], ACT.Copy)
                else:
                    last = f(mq[:, q - 25, :], b[:, 0:TOK], ACT.Copy)
                last.then_inc(S["pjev"], 1)
                if 4 <= q < 4 + NQKV:
                    silu(q - 4)
            for k in range(3):
                act.wait_ge(S["cotr"], k + 1)
                f(cor[:, 512 * k:512 * k + 512], bank(4 + k)[0:27, :], ACT.Copy).then_inc(S["cor"], 1)
            act.wait_ge(S["cotr"], 4)
            f(scor[:, :], bank(7)[0:18, 0:256], ACT.Copy).then_inc(S["cor"], 1)
            act.wait_ge(S["vec_in"], 96)
            f(small[:, 108:112], hb[:, 0:4], ACT.Exp)
            act.wait_ge(S["ab"], 1)
            f(small[:, 128:140], small[:, 112:124], ACT.Exp, scale=-1.0).then_inc(S["abx"], 1)
            act.wait_ge(S["ab"], 2)
            f(small[:, 128:140], small[:, 128:140], ACT.Ln).then_inc(S["abl"], 1)
            f(small[:, 144:156], small[:, 88:100], ACT.Sigmoid).then_inc(S["abg"], 1)
            act.wait_ge(S["co"], 1)
            for s in range(9):
                act.wait_ge(S["ktr"], s + 1)
                f(kT[:, :, s, :], bank(s % 8).rearrange("p (b m) -> p b m", b=2), ACT.Copy).then_inc(S["kT"], 1)
            act.wait_ge(S["silu"], NQKV)
            f(sq4, qkv[:, 0:4, :], ACT.Square).then_inc(S["sq"], 1)
            for t in range(TILES):
                act.wait_ge(S["soft"], t + 1)
                if t:
                    act.wait_ge(S["ptr"], t)
                for hh in range(4):
                    last = f(prob[:, hh, :], bank(2 * t + hh // 2)[:, (hh % 2) * 256:(hh % 2) * 256 + 256], ACT.Exp,
                             bias=small[:, 160 + hh:161 + hh], scale=0.125, accum_out=small[:, 164 + hh:165 + hh])
                last.then_inc(S["pexp"], 1)
                if t < 2:
                    act.wait_ge(S["nadd"], t + 1)
                    f(nr4, nr4, ACT.Sqrt).then_inc(S["nsqrt"], 1)
                act.wait_ge(S["ptr"], t + 1)
                if t:
                    act.wait_ge(S["pv"], t)
                f(probT, bank(6, 2).rearrange("p (c n) -> p c n", c=8), ACT.Copy).then_inc(S["pT"], 1)
                act.wait_ge(S["pv"], t + 1)
                f(mq[:, :, t * P:(t + 1) * P], bank(2 * t)[:, 0:256].rearrange("p (b n) -> p b n", b=2),
                  ACT.Copy).then_inc(S["ym"], 1)
                if t == 0:
                    act.wait_ge(S["nsum"], 1)
                    f(sq4, qkv[:, 4:8, :], ACT.Square).then_inc(S["sq"], 1)
            act.wait_ge(S["kv_out"], 32)
            act.wait_ge(S["corout"], 32)
            kept = [0]

            def keep(steps):
                for k in range(kept[0], min(steps // KT8, EARLY)):
                    act.wait_ge(S["early"], k + 1)
                    f(early[:, k, :], bank(3 - 2 * (k % 2))[:, 0:TOK], ACT.Copy).then_inc(S["earlyout"], 1)
                    kept[0] += 1

            steps = 0
            for t in range(TILES):
                act.wait_ge(S["gex"], 2 * t + 1)
                f(small[:, 180:188], small[:, 172:180], ACT.Exp).then_inc(S["gex"], 1)
                act.wait_ge(S["dexp"], 3 * t + 1)
                f(eB, bank(1).rearrange("p (h n) -> p h n", h=4), ACT.Exp)
                f(dTm, dTm, ACT.Exp)
                f(dec, dec, ACT.Exp, scale=-1.0).then_inc(S["dexp"], 2)
                act.wait_ge(S["dmul"], t + 1)
                for n in range(1, len(tile_levels[t])):
                    k = LEVEL_STEPS[t] + n
                    act.wait_ge(S["Yready"], k)
                    f(Ym, bank(7).rearrange("p (h n) -> p h n", h=4), ACT.Copy).then_inc(S["uready"], 1)
                    if n == 1:
                        steps += FILL[0]
                    keep(steps)
                    steps += FILL[1] + FILL[2]
                act.wait_ge(S["wkt"], t + 1)
                f(nwk, bank(4).rearrange("p (h n) -> p h n", h=4), ACT.Copy, scale=-1.0).then_inc(S["nwk"], 1)
                keep(steps)
                if t < 2:
                    for b in range(2):
                        act.wait_ge(S["u"], 2 * t + b + 1)
                        f(um[64 * b:64 * b + 64, :, :], bank(5)[64 * b:64 * b + 64, :].rearrange("p (h n) -> p h n", h=4),
                          ACT.Copy).then_inc(S["uev"], 1)
                    act.wait_ge(S["snew"], 2 * t + 2)
                else:
                    act.wait_ge(S["u"], 5)
                    f(uT, bank(5).rearrange("p (h n) -> p h n", h=4), ACT.Copy).then_inc(S["utr"], 1)
                    act.wait_ge(S["u"], 6)
                    f(um, bank(2).rearrange("p (h n) -> p h n", h=4), ACT.Copy).then_inc(S["uev"], 1)
                    act.wait_ge(S["oready"], 1)
                f(oS, bank(0).rearrange("p (h n) -> p h n", h=4), ACT.Copy)
                f(osq, bank(0).rearrange("p (h n) -> p h n", h=4), ACT.Square).then_inc(S["oev"], 1)
                act.wait_ge(S["onorm"], 2 * t + 1)
                f(osq, osq, ACT.Sqrt).then_inc(S["onorm"], 1)
            def hi(kind, n, q0, j, free=True):
                s = 2 * MATS.index(kind) + j // 2
                act.wait_ge(loaded[s], 16 * len(range(s, TRUNK_PIECES, 4)) * (s < 4) + 16 + 16 * n)
                if free:
                    act.wait_ge(S["used"], q0 + j - 3)
                f(w_hi[j][:, :], ring[:, s, 2048 * (j % 2):2048 * (j % 2) + 2048], ACT.Copy).then_inc(S["hi"], 1)

            act.wait_ge(S["yd"], 3)
            for k in range(24):
                if k >= EARLY:
                    act.wait_ge(S["gp"], k - EARLY + 1)
                if k >= 4:
                    act.wait_ge(S["mrg"], k - 3)
                src = bank(2 * (k % 4))[:, 0:TOK] if k >= EARLY else early[:, k, :]
                f(sig[:, k % 4, :], src, ACT.Sigmoid).then_inc(S["gsig"], 1)
            for t in range(TILES):
                act.wait_ge(S["hadd"], 4 + t)
                last = f(x2[:, t, :], h[:, t, :], ACT.Square, accum_out=small[:, 40 + t:41 + t])
            last.then_inc(S["ss2"], 1)
            act.wait_ge(S["rt2"], 1)
            f(small[:, 46:49], small[:, 40:43], ACT.Sqrt).then_inc(S["rt2"], 1)
            act.wait_ge(S["brt"], 1)
            for k, dst in enumerate((bg, bu)):
                last = f(dst[:, 0:256], bank(6)[:, 256 * k:256 * k + 256], ACT.Copy)
            last.then_inc(S["bT"], 1)
            act.wait_ge(S["x2"], 3)
            act.wait_ge(S["wo"], 6)
            f(split[:, 0, :, :], x2, ACT.Copy).then_inc(S["split"], 1)
            act.wait_ge(S["rest"], 1)
            f(split[:, 1, :, :], x2, ACT.Copy).then_inc(S["split"], 1)
            hi("gate", 0, 0, 0, free=False)
            act.wait_ge(S["lgx"], 1)
            f(rt[2], rt[1], ACT.Exp).then_inc(S["lgx"], 1)
            hi("gate", 0, 0, 1, free=False)
            act.wait_ge(S["gtr"], 1)
            act.wait_ge(S["x2T"], 3)
            f(gT, bank(1)[0:E, 0:TOK], ACT.Copy).then_inc(S["gT"], 1)
            act.wait_ge(S["rest"], 2)
            f(split[:, 2, :, :], x2, ACT.Copy).then_inc(S["split"], 1)
            hi("gate", 0, 0, 2, free=False)
            hi("gate", 0, 0, 3, free=False)
            def x_hi(m, items=2):
                act.wait_ge(S["xg"], 2 * m + 2)
                f(xparts[:, 0:items, :, 0:CAP],
                  bank(6, 2).rearrange("p (t i c) -> p i t c", t=KT8, i=2)[:, 0:items], ACT.Copy).then_inc(S["xhi"], 1)

            def g_out(n, q0):
                act.wait_ge(S["used"], q0 + halves)
                f(g_sb[:, :], bank(0, 2), ACT.Copy).then_inc(S["gev"], 1)

            def u_out(n, q0):
                act.wait_ge(S["used"], q0 + halves)
                f(u_sb[:, :], bank(2, 2), ACT.Copy).then_inc(S["uout"], 1)

            def y_out(n, q0, i):
                act.wait_ge(S["used"], q0 + halves)
                f(y_sb[:, i, :], bank(2, 2), ACT.Copy).then_inc(S["yev"], 1)

            def slots_out(n, i, b):
                act.wait_ge(S["pgt"], n + 1)
                f(gs[:, i:i + 1], bank(b)[:, TOK:TOK + 1], ACT.Copy).then_inc(S["gsc"], 1)
                act.wait_ge(S["gsc"], n + 1)
                f(pgT[:, i, :], bank(b)[:, 0:TOK], ACT.Copy, scale=gs[:, i:i + 1]).then_inc(S["pgtev"], 1)

            def sigmoid(n):
                act.wait_ge(S["hg"], n + 1)
                f(sg, hg, ACT.Sigmoid, scale=ALPHA).then_inc(S["sgm"], 1)

            def h_hi(n):
                act.wait_ge(S["hf"], n + 1)
                f(hparts[:, :, 0:CAP], hu.rearrange("p (f c) -> p f c", f=8), ACT.Copy).then_inc(S["hhi"], 1)

            def item(m, n, i, last=False):
                up, gate_, down = stream("up", n), stream("gate", n + 1) if not last else 0, stream("down", n)
                hi("up", n, up, 3)
                sigmoid(n)
                if not last:
                    for j in range(3):
                        hi("gate", n + 1, gate_, j)
                u_out(n, up)
                if i and not last:
                    x_hi(m + 1)
                if not last:
                    hi("gate", n + 1, gate_, 3)
                h_hi(n)
                for j in range(3):
                    hi("down", n, down, j)
                if not last:
                    g_out(n + 1, gate_)
                if i == 0:
                    slots_out(n, 0, 4)
                    slots_out(n + 1, 1, 5)
                hi("down", n, down, 3)
                if not last:
                    for j in range(3):
                        hi("up", n + 1, stream("up", n + 1), j)
                y_out(n, down, i)

            x_hi(0)
            for j in range(3):
                hi("up", 0, stream("up", 0), j)
            g_out(0, 0)
            item(0, 0, 0)
            item(0, 1, 1)
            with act.Fori(1, E // 2 - 1) as m:
                item(m, 2 * m, 0)
                item(m, 2 * m + 1, 1)
            item(E // 2 - 1, E - 2, 0)
            item(E // 2 - 1, E - 1, 1, last=True)
            act.wait_ge(S["overx"], 1)
            n_over = act.value_load(over[0:1, 0:1], min_val=0, max_val=MAX_OVER)
            with act.If(n_over > 0):
                with act.Fori(0, MAX_OVER) as i:
                    with act.If(n_over > i):
                        n = i + E
                        x_hi(i + E // 2, items=1)
                        for j in range(halves):
                            hi("gate", n, stream_over("gate", n), j)
                        g_out(n, stream_over("gate", n))
                        sigmoid(n)
                        for j in range(halves):
                            hi("up", n, stream_over("up", n), j)
                        u_out(n, stream_over("up", n))
                        h_hi(n)
                        slots_out(n, 0, 4)
                        for j in range(halves):
                            hi("down", n, stream_over("down", n), j)
                        y_out(n, stream_over("down", n), 0)
            act.wait_ge(S["fss"], 1)
            for t in range(TILES):
                last = f(bank(2 * t, 2), h[:, t, :], ACT.Square, accum_out=small[:, 40 + t:41 + t])
            last.then_inc(S["fss"], 1)
            act.wait_ge(S["frt"], 1)
            f(small[:, 46:49], small[:, 40:43], ACT.Sqrt).then_inc(S["frt"], 1)

        @block.vector
        def _(dve):
            v = nc.vector
            own = [0]

            def link(ins):
                own[0] += 1
                ins.then_inc(vlink, 1)
                dve.wait_ge(vlink, own[0])

            v.memset(xp[:, :, 0:3], 0.0)
            link(v.memset(sp[:, :, 0:2], 0.0))
            dve.wait_ge(S["ss"], 1)
            v.tensor_scalar(small[:, 40:45], small[:, 40:45], 1.0 / D, EPS, ALU.mult, ALU.add).then_inc(S["ss"], 1)
            dve.wait_ge(S["rt5"], 1)
            link(v.reciprocal(small[:, 52:57], small[:, 46:51]))
            for t in range(5):
                src, dst = (h[:, t, :], xs[:, t, :]) if t < 3 else (mem[:, t - 3, :], xs_mem[:, t - 3, :])
                v.tensor_scalar(dst, src, small[:, 52 + t:53 + t], None, ALU.mult).then_inc(S["xs"], 1)
            dve.wait_ge(S["vec_in"], 96)
            for t in range(5):
                dve.wait_ge(S["xtr"], t + 1)
                for k in range(2):
                    dst = xnT[:, 4 * k:4 * k + 4, t * P:(t + 1) * P] if t < 3 else mT[:, 4 * k:4 * k + 4, (t - 3) * P:(t - 2) * P]
                    c = 4 * k + (0 if t < 3 else 16)
                    last = v.tensor_tensor(dst, bank((2 * t + k) % 8).rearrange("p (t n) -> p t n", t=4),
                                           norms[:, c:c + 4].unsqueeze(2).to_broadcast([P, 4, P]), ALU.mult)
                last.then_inc(S["xT"], 1)
            dve.wait_ge(S["cwT"], 1)
            for c in range(NQKV):
                v.tensor_copy(xp[:, c, LP:WP].rearrange("p (s k) -> p s k", k=3 + LS)[:, :, 0:3],
                              cwv[:, c, 0:24].rearrange("p (s k) -> p s k", k=3))
            for c in range(2):
                last = v.tensor_copy(sp[:, c, SP2:WS].rearrange("p (s k) -> p s k", k=2 + LS)[:, :, 0:2],
                                     scwv[:, c, 0:16].rearrange("p (s k) -> p s k", k=2))
            link(last)
            for c in range(NQKV):
                n = WP - 3
                dve.wait_ge(S["pjev"], c + 3)
                if c:
                    dve.wait_ge(S["silu"], c)
                link(v.tensor_scalar(conv_acc[:, 0:n], xp[:, c, 0:n], cwv[:, c, 24:25], None, ALU.mult))
                for j in range(1, 4):
                    ins = v.scalar_tensor_tensor(out=conv_acc[:, 0:n], in0=xp[:, c, j:j + n], scalar=cwv[:, c, 24 + j:25 + j],
                                                 in1=conv_acc[:, 0:n], op0=ALU.mult, op1=ALU.add)
                    if j < 3:
                        link(ins)
                ins.then_inc(S["conv"], 1)
            v.tensor_copy(cov[:, :, 0:3], xp[:, :, LP - 3:LP])
            for c in range(NQKV):
                last = v.tensor_copy(cov[:, c, 3:27].rearrange("p (s k) -> p s k", k=3),
                                     xp[:, c, LP:WP].rearrange("p (s k) -> p s k", k=3 + LS)[:, :, LS:LS + 3])
            last.then_inc(S["co"], 1)
            dve.wait_ge(S["pjev"], 25)
            dve.wait_ge(S["silu"], NQKV)
            link(v.tensor_tensor(sp[:, :, 2:SP2], cT[:, :, 0:256], hT[:, :, 0:256], ALU.mult))
            for c in range(2):
                last = v.tensor_tensor(sp[:, c, SP2:WS].rearrange("p (s k) -> p s k", k=2 + LS)[:, :, 2:2 + LS],
                                       cT[:, c, 256:TOK].rearrange("p (s k) -> p s k", k=LS),
                                       hT[:, c, 256:TOK].rearrange("p (s k) -> p s k", k=LS), ALU.mult)
            link(last)
            for c in range(2):
                n = WS - 2
                link(v.tensor_scalar(conv_acc[:, 0:n], sp[:, c, 0:n], scwv[:, c, 16:17], None, ALU.mult))
                for j in range(1, 3):
                    link(v.scalar_tensor_tensor(out=conv_acc[:, 0:n], in0=sp[:, c, j:j + n], scalar=scwv[:, c, 16 + j:17 + j],
                                                in1=conv_acc[:, 0:n], op0=ALU.mult, op1=ALU.add))
                v.tensor_tensor(sbb[:, c, 0:256], sbb[:, c, 0:256], conv_acc[:, 0:256], ALU.mult)
                link(v.tensor_tensor(sbb[:, c, 256:TOK].rearrange("p (s k) -> p s k", k=LS),
                                     sbb[:, c, 256:TOK].rearrange("p (s k) -> p s k", k=LS),
                                     conv_acc[:, SP2:WS].rearrange("p (s k) -> p s k", k=2 + LS)[:, :, 0:LS], ALU.mult))
            v.tensor_copy(scov[:, :, 0:2], sp[:, :, SP2 - 2:SP2])
            for c in range(2):
                last = v.tensor_copy(scov[:, c, 2:18].rearrange("p (s k) -> p s k", k=2),
                                     sp[:, c, SP2:WS].rearrange("p (s k) -> p s k", k=2 + LS)[:, :, LS:LS + 2])
            last.then_inc(S["co"], 1)
            lgt = small[:, 64:88].rearrange("p (a k) -> p a k", a=3)
            az = small[:, 192:204].rearrange("p (a k) -> p a k", a=3)
            link(v.tensor_tensor(az, lgt[:, :, 0:4], hb[:, 4:8].unsqueeze(1).to_broadcast([P, 3, 4]), ALU.add))
            v.tensor_copy(small[:, 88:100].rearrange("p (a k) -> p a k", a=3), lgt[:, :, 4:8])
            link(v.tensor_scalar(small[:, 112:124], small[:, 192:204], -1.0, None, ALU.mult))
            v.tensor_tensor(small[:, 112:124], small[:, 112:124], small[:, 192:204], ALU.max).then_inc(S["ab"], 1)
            dve.wait_ge(S["abx"], 1)
            v.tensor_scalar(small[:, 128:140], small[:, 128:140], 1.0, None, ALU.add).then_inc(S["ab"], 1)
            dve.wait_ge(S["abl"], 1)
            link(v.scalar_tensor_tensor(out=small[:, 192:204], in0=small[:, 192:204], scalar=0.0, in1=small[:, 128:140],
                                        op0=ALU.max, op1=ALU.add))
            gv = small[:, 0:36].rearrange("p (a k) -> p a k", a=3)
            v.scalar_tensor_tensor(out=gv[:, :, 0:4], in0=az, scalar=-1.0,
                                   in1=small[:, 108:112].unsqueeze(1).to_broadcast([P, 3, 4]), op0=ALU.mult, op1=ALU.mult)
            dve.wait_ge(S["abg"], 1)
            v.tensor_copy(gv[:, :, 4:8], small[:, 144:156].rearrange("p (a k) -> p a k", a=3)).then_inc(S["gates"], 1)
            dve.wait_ge(S["corout"], 32)
            link(v.memset(qm[:, :], 0.0))
            for s in range(NSEQ):
                last = v.tensor_copy(qmv[:, s, :, s * LS:(s + 1) * LS], mq[:, :, 256 + s * LS:256 + (s + 1) * LS])
            last.then_inc(S["qm"], 1)
            for t in range(TILES):
                dve.wait_ge(S["sc"], t + 1)
                link(v.tensor_reduce(small[:, 160:164], bank(2 * t, 2).rearrange("p (h m) -> p h m", h=4), AX.X, ALU.max))
                v.tensor_scalar(small[:, 160:164], small[:, 160:164], -0.125, None, ALU.mult).then_inc(S["soft"], 1)
                if t < 2:
                    dve.wait_ge(S["nsum"], t + 1)
                    if t:
                        dve.wait_ge(S["norm"], t)
                    for g in range(2):
                        sums = bank(NORM_BANKS[t][2 * g], 2).rearrange("p (c n) -> p c n", c=2)
                        last = v.tensor_scalar(nr4[:, 2 * g:2 * g + 2, :], sums[:, :, 0:TOK], EPS, None, ALU.add)
                    last.then_inc(S["nadd"], 1)
                dve.wait_ge(S["pexp"], t + 1)
                link(v.reciprocal(small[:, 168:172], small[:, 164:168]))
                v.tensor_tensor(prob, prob, small[:, 168:172].unsqueeze(2).to_broadcast([P, 4, 256]), ALU.mult)\
                    .then_inc(S["pn"], 1)
                if t < 2:
                    dve.wait_ge(S["nsqrt"], t + 1)
                    link(v.reciprocal(nr4, nr4))
                    v.scalar_tensor_tensor(out=qkv[:, 4 * t:4 * t + 4, :], in0=qkv[:, 4 * t:4 * t + 4, :],
                                           scalar=(float(P) ** -0.5 if t == 0 else 1.0), in1=nr4, op0=ALU.mult,
                                           op1=ALU.mult).then_inc(S["norm"], 1)
            dve.wait_ge(S["gates"], 1)
            dve.wait_ge(S["ym"], 3)
            b3 = lambda x: x.unsqueeze(2).to_broadcast([P, HEADS, P])
            m3 = lambda x: x.unsqueeze(1).to_broadcast([P, HEADS, P])

            def decays(t):
                v.tensor_copy(gb, b3(small[:, 12 * t:12 * t + 4])).then_inc(S["gbr"], 1)
                dve.wait_ge(S["gcum"], t + 1)
                link(v.tensor_copy(small[:, 172:176], bank(0)[:, 0:4]))
                v.tensor_tensor(small[:, 176:180], bank(0)[:, 4:8], small[:, 172:176], ALU.subtract).then_inc(S["gex"], 1)

            for t in range(TILES):
                cols = slice(t * P, (t + 1) * P)
                bv4 = lambda k: bank(k).rearrange("p (h n) -> p h n", h=HEADS)
                beta = small[:, 12 * t + 4:12 * t + 8]
                if t == 0:
                    decays(0)
                dve.wait_ge(S["cumb"], t + 1)
                for hh in range(HEADS):
                    v.tensor_scalar(dTm[:, hh, :], bv4(1)[:, hh, :], small[:, 172 + hh:173 + hh], 0.0, ALU.subtract, ALU.min)
                    last = v.tensor_scalar(dec[:, hh, :], bv4(1)[:, hh, :], small[:, 172 + hh:173 + hh], 0.0, ALU.subtract, ALU.max)
                last.then_inc(S["dexp"], 1)
                dve.wait_ge(S["gex"], 2 * t + 2)
                link(v.tensor_tensor(small[:, 188:192], small[:, 180:184], beta, ALU.mult))
                dve.wait_ge(S["dexp"], 3 * t + 3)
                dve.wait_ge(S["kk"], t + 1)
                link(v.tensor_tensor(dTm, dTm, m3(upto[t]), ALU.mult))
                v.tensor_tensor(qkT, bv4(3), dTm, ALU.mult)
                link(v.tensor_tensor(dec, dec, b3(beta), ALU.mult))
                link(v.tensor_tensor(Am, bv4(2), dec, ALU.mult))
                link(v.tensor_tensor(Em, Am, m3(const("level1")), ALU.mult))
                v.tensor_tensor(Dm, m3(ident), Em, ALU.subtract).then_inc(S["lv"], 1)
                dve.wait_ge(S["lv"], LEVEL_STEPS[t] + 2 * t + 1)
                v.tensor_tensor(Em, Am, m3(const("level2")), ALU.mult).then_inc(S["dmul"], 1)
                dve.wait_ge(S["Fready"], t + 1)
                v.tensor_copy(Fm, bv4(6)).then_inc(S["lv"], 1)
                v.tensor_tensor(qd, qkv[:, 0:4, cols], eB, ALU.mult)
                dve.wait_ge(S["tok"], t + 1)
                v.tensor_tensor(bk, bv4(4), b3(small[:, 188:192]), ALU.mult)
                v.tensor_tensor(kd, bv4(4), b3(small[:, 184:188]), ALU.mult)
                v.tensor_tensor(bv, bv4(5), b3(beta), ALU.mult).then_inc(S["tokev"], 1)
                for n in range(1, len(tile_levels[t])):
                    k = LEVEL_STEPS[t] + n
                    last_level = n == len(tile_levels[t]) - 1
                    dve.wait_ge(S["Gready"], k)
                    v.tensor_tensor(Fm, Fm, bv4(6), ALU.subtract)
                    if not last_level:
                        v.tensor_tensor(Em, Am, m3(const(f"level{tile_levels[t][n + 1]}")), ALU.mult)
                    v.tensor_tensor(Dm, Dm, bv4(2), ALU.subtract).then_inc(S["lv"], 1)
                def output_norm():
                    dve.wait_ge(S["osum"], t + 1)
                    v.tensor_scalar(osq, bv4(1), 1.0 / P, EPS, ALU.mult, ALU.add).then_inc(S["onorm"], 1)
                    if t + 1 < TILES:
                        decays(t + 1)
                    dve.wait_ge(S["onorm"], 2 * t + 2)
                    link(v.reciprocal(osq, osq))
                    link(v.scalar_tensor_tensor(out=oS, in0=oS, scalar=norms[:, 24:25], in1=osq, op0=ALU.mult, op1=ALU.mult))
                    v.tensor_tensor(dg[:, :, cols], dg[:, :, cols], oS, ALU.mult).then_inc(S["yd"], 1)

                if t < 2:
                    for b in range(2):
                        k = 2 * t + b
                        dve.wait_ge(S["snew"], k + 1)
                        if k == 0:
                            v.tensor_copy(st[:, :, :], bv4(6)).then_inc(S["st_upd"], 1)
                        else:
                            for hh in range(HEADS):
                                last = v.scalar_tensor_tensor(out=st[:, hh, :], in0=st[:, hh, :],
                                                              scalar=eB[:, hh, 64 * b + 63:64 * b + 64],
                                                              in1=bv4(6 + b)[:, hh, :], op0=ALU.mult, op1=ALU.add)
                            last.then_inc(S["st_upd"], 1)
                    if t == 1:
                        dve.wait_ge(S["st_upd"], 4)
                        v.tensor_copy(small[:, 210:211], st[:, 0, 0:1]).then_inc(S["st_all"], 1)
                    output_norm()
                else:
                    def mask(hh):
                        v.tensor_tensor(umask[hh % 2], um[:, hh, :].unsqueeze(1).to_broadcast([P, NSEQ, P]),
                                        const("seq").unsqueeze(2).to_broadcast([P, NSEQ, P]), ALU.mult).then_inc(S["um"], 1)

                    dve.wait_ge(S["uev"], 5)
                    mask(0)
                    mask(1)
                    output_norm()
                    for hh in range(HEADS):
                        dve.wait_ge(S["snew"], 5 + hh)
                        for s in range(NSEQ):
                            c = s * LS + LS - 1
                            last = v.scalar_tensor_tensor(out=states[:, s, hh, :], in0=states[:, s, hh, :],
                                                          scalar=eB[:, hh, c:c + 1],
                                                          in1=bank((6, 2)[hh % 2] + s // 4)[:, (s % 4) * P:(s % 4 + 1) * P],
                                                          op0=ALU.mult, op1=ALU.add)
                        last.then_inc(S["st_upd"], 1)
                        if hh + 2 < HEADS:
                            mask(hh + 2)
                    dve.wait_ge(S["st_upd"], 8)
                    v.tensor_copy(small[:, 210:211], states[:, 0, 0, 0:1]).then_inc(S["st_all"], 1)
            for k in range(24):
                half, b, c = k // 12, k // 4 % 3, k % 4
                dst = mg[:, 4 * half + c, :]
                dve.wait_ge(S["gsig"], k + 1)
                dve.wait_ge(S["gz"], k + 1)
                z = bank(2 * (k % 4) + 1)[:, 0:TOK]
                if b == 0:
                    ins = v.tensor_tensor(dst, sig[:, k % 4, :], z, ALU.mult)
                else:
                    link(v.tensor_tensor(sig[:, k % 4, :], sig[:, k % 4, :], z, ALU.mult))
                    dve.wait_ge(S["mrg"], k)
                    ins = v.tensor_tensor(dst, dst, sig[:, k % 4, :], ALU.add)
                ins.then_inc(S["mrg"], 1)
            for k in range(2):
                for a in range(TILES):
                    n = 3 * k + a
                    dve.wait_ge(S["wo"], n + 1)
                    v.tensor_tensor(h[:, a, 512 * k:512 * k + 512], h[:, a, 512 * k:512 * k + 512], bank(n),
                                    ALU.add).then_inc(S["hadd"], 1)
            dve.wait_ge(S["ss2"], 1)
            v.tensor_scalar(small[:, 40:43], small[:, 40:43], 1.0 / D, EPS, ALU.mult, ALU.add).then_inc(S["rt2"], 1)
            dve.wait_ge(S["rt2"], 2)
            dve.wait_ge(S["rout_in"], 48)
            link(v.reciprocal(small[:, 52:55], small[:, 46:49]))
            for a in range(TILES):
                v.scalar_tensor_tensor(out=x2[:, a, :], in0=h[:, a, :], scalar=small[:, 52 + a:53 + a], in1=w2b,
                                       op0=ALU.mult, op1=ALU.mult).then_inc(S["x2"], 1)
            for a in range(TILES):
                dve.wait_ge(S["x2tr"], a + 1)
                v.tensor_copy(x2T[:, :, a * P:(a + 1) * P], bank(2 * a, 2).rearrange("p (t n) -> p t n", t=KT8))\
                    .then_inc(S["x2T"], 1)
            dve.wait_ge(S["split"], 1)
            v.tensor_tensor(x2, x2, split[:, 0, :, :], ALU.subtract).then_inc(S["rest"], 1)
            dve.wait_ge(S["out"], 64)
            dve.wait_ge(S["lgm"], 1)
            link(v.tensor_tensor(lg, bank(7)[:, 0:3 * E].rearrange("p (a e) -> p a e", a=3),
                                 br.unsqueeze(1).to_broadcast([P, 3, E]), ALU.add))
            top = small[:, 216:240].rearrange("p (a k) -> p a k", a=3)
            for a in range(TILES):
                last = v.max(top[:, a, :], lg[:, a, :])
            link(last)
            be = lambda x: x.to_broadcast([P, 3, E])
            mask, t1, t2, t3, t4_, t5 = rt
            v.memset(t5, 0.0)
            v.tensor_tensor(mask, lg, be(top[:, :, 3:4]), ALU.is_gt)
            link(v.tensor_tensor(t3, lg, be(top[:, :, 3:4]), ALU.is_equal))
            v.tensor_reduce(small[:, 240:243], mask, AX.X, ALU.add)
            for a in range(TILES):
                last = v.tensor_tensor_scan(t4_[:, a, :], t3[:, a, :], t5[:, a, :], 0.0, ALU.add, ALU.add)
            link(last)
            link(v.tensor_scalar(small[:, 244:247], small[:, 240:243], -1.0, 4.0, ALU.mult, ALU.add))
            link(v.tensor_tensor(t4_, t4_, be(small[:, 244:247].unsqueeze(2)), ALU.is_le))
            link(v.tensor_tensor(t4_, t4_, t3, ALU.mult))
            link(v.tensor_tensor(mask, mask, t4_, ALU.add))
            v.tensor_tensor(t1, lg, be(top[:, :, 0:1]), ALU.subtract).then_inc(S["lgx"], 1)
            dve.wait_ge(S["lgx"], 2)
            link(v.tensor_tensor(t2, t2, mask, ALU.mult))
            link(v.tensor_reduce(small[:, 248:251], t2, AX.X, ALU.add))
            link(v.reciprocal(small[:, 252:255], small[:, 248:251]))
            v.tensor_tensor(gate[:, :, :], t2, be(small[:, 252:255].unsqueeze(2)), ALU.mult).then_inc(S["sel"], 1)
            dve.wait_ge(S["sel"], 1)
            link(v.tensor_copy(gate3[:, :, 0, :], gate[:, :, :]))
            link(v.tensor_tensor(t2, gate[:, :, :], gate3[:, :, 0, :], ALU.subtract))
            link(v.tensor_copy(gate3[:, :, 1, :], t2))
            link(v.tensor_tensor(t2, t2, gate3[:, :, 1, :], ALU.subtract))
            v.tensor_copy(ident_b[:, :], ident)
            link(v.tensor_copy(gate3[:, :, 2, :], t2))
            dve.wait_ge(S["split"], 2)
            v.tensor_tensor(x2, x2, split[:, 1, :, :], ALU.subtract).then_inc(S["rest"], 1)
            dve.wait_ge(S["posm"], 1)
            link(v.tensor_scalar(t1, bank(0)[:, 0:3 * E].rearrange("p (a e) -> p a e", a=3), 1.0, None, ALU.add))
            link(v.tensor_tensor(t1, t1, mask, ALU.mult))
            cnt = t2[:, 0, :]
            v.tensor_copy(cnt, bank(0)[:, 3 * E:4 * E])
            link(v.tensor_scalar(pos[:, :, 0:E], t1, -1.0, None, ALU.add))
            def place(slots):
                items = slots.shape[2]
                v.tensor_tensor(onehot[:, :, 0:items, :],
                                const("slots2").unsqueeze(1).unsqueeze(1).to_broadcast([P, 3, items, 2 * CAP]),
                                slots.unsqueeze(3).to_broadcast([P, 3, items, 2 * CAP]), ALU.is_equal).then_inc(S["P"], 1)

            def lo(kind, q0, j):
                s = 2 * MATS.index(kind) + j // 2
                cols = slice(2048 * (j % 2), 2048 * (j % 2) + 2048)
                dve.wait_ge(S["hi"], q0 + j + 1)
                v.tensor_tensor(w_lo[:, s, cols], ring[:, s, cols], w_hi[j][:, :].bitcast(F32), ALU.subtract).then_inc(S["lo"], 1)

            def x_lo(m, items=2):
                dve.wait_ge(S["xhi"], m + 1)
                for i in range(items):
                    last = v.tensor_tensor(xparts[:, i, :, CAP:2 * CAP],
                                           bank(6, 2).rearrange("p (t i c) -> p i t c", t=KT8, i=2)[:, i],
                                           xparts[:, i, :, 0:CAP].bitcast(F32), ALU.subtract)
                last.then_inc(S["xlo"], 1)

            c8 = lambda x: x.rearrange("p (f c) -> p f c", f=8)
            biased = lambda b, e: b[:, bass.ds(e * 8, 8)].unsqueeze(2).to_broadcast([P, 8, CAP])

            def gate_in(n, e):
                dve.wait_ge(S["gT2"], n + 1)
                v.tensor_tensor(c8(hg), c8(bank(4)), biased(bg, e), ALU.add).then_inc(mlink, 1)
                dve.wait_ge(mlink, 4 * n + 1)
                v.tensor_scalar(hg, hg, LIMIT, None, ALU.min).then_inc(S["hg"], 1)

            def gate_mul(n):
                dve.wait_ge(S["sgm"], n + 1)
                v.tensor_tensor(hg, hg, sg, ALU.mult).then_inc(mlink, 1)

            def up_in(n, e):
                dve.wait_ge(S["uT2"], n + 1)
                v.tensor_tensor(c8(hu), c8(bank(5)), biased(bu, e), ALU.add).then_inc(mlink, 1)
                dve.wait_ge(mlink, 4 * n + 3)
                v.tensor_scalar(hu, hu, -LIMIT, LIMIT, ALU.max, ALU.min).then_inc(mlink, 1)
                dve.wait_ge(mlink, 4 * n + 4)
                v.scalar_tensor_tensor(out=hu, in0=hu, scalar=1.0, in1=hg, op0=ALU.add, op1=ALU.mult).then_inc(S["hf"], 1)

            def h_lo(n):
                dve.wait_ge(S["hhi"], n + 1)
                v.tensor_tensor(hparts[:, :, CAP:2 * CAP], c8(hu), hparts[:, :, 0:CAP].bitcast(F32),
                                ALU.subtract).then_inc(S["hlo"], 1)

            def add(m, a):
                for k in range(2):
                    dve.wait_ge(S["acc"], 6 * m + 2 * a + k + 1)
                    o = h[:, a, 512 * k:512 * k + 512]
                    v.tensor_tensor(o, o, bank(6 + k), ALU.add).then_inc(S["accrd"], 1)

            def item_a(m, n, first=False):
                up, gate_, down = stream("up", n), stream("gate", n + 1), stream("down", n)
                if not first:
                    dve.wait_ge(S["accrd"], 6 * m - 5)
                lo("up", up, 1)
                gate_in(n, n)
                lo("up", up, 2)
                if not first:
                    add(m - 1, 0)
                lo("up", up, 3)
                gate_mul(n)
                lo("gate", gate_, 0)
                lo("gate", gate_, 1)
                if not first:
                    add(m - 1, 1)
                lo("gate", gate_, 2)
                up_in(n, n)
                lo("gate", gate_, 3)
                h_lo(n)
                lo("down", down, 0)
                lo("down", down, 1)
                if not first:
                    add(m - 1, 2)
                lo("down", down, 2)
                lo("down", down, 3)
                lo("up", stream("up", n + 1), 0)

            def item_b(m, n, last=False):
                up, gate_, down = stream("up", n), stream("gate", n + 1) if not last else 0, stream("down", n)
                if not last:
                    dve.wait_ge(S["pgt"], n + 1)
                    place(pos[:, :, bass.ds(n + 1, 2)])
                lo("up", up, 1)
                gate_in(n, n)
                lo("up", up, 2)
                lo("up", up, 3)
                gate_mul(n)
                if not last:
                    for j in range(3):
                        lo("gate", gate_, j)
                    x_lo(m + 1)
                up_in(n, n)
                if not last:
                    lo("gate", gate_, 3)
                h_lo(n)
                for j in range(4):
                    lo("down", down, j)
                if not last:
                    lo("up", stream("up", n + 1), 0)

            def add_biases(a, b):
                dve.wait_ge(S["bdm"], a + 1)
                return v.tensor_tensor(h[:, a, :], h[:, a, :], bank(b, 2), ALU.add)

            dve.wait_ge(S["bT"], 1)
            place(pos[:, :, 0:2])
            lo("gate", 0, 0)
            lo("gate", 0, 1)
            lo("gate", 0, 2)
            x_lo(0)
            lo("gate", 0, 3)
            dve.wait_ge(S["split"], 3)
            nb = t2[:, 1, :]
            end = t2[:, 2, :]
            link(v.tensor_scalar(nb, cnt, float(CAP), None, ALU.is_gt))
            for r in range(2, 6):
                link(v.tensor_scalar(t3[:, 0, :], cnt, float(CAP * r), None, ALU.is_gt))
                link(v.tensor_tensor(nb, nb, t3[:, 0, :], ALU.add))
            link(v.tensor_tensor_scan(end, nb, t5[:, 0, :], 0.0, ALU.add, ALU.add))
            big = xn[:, 512:512 + MAX_OVER * E].rearrange("p (i e) -> p i e", i=MAX_OVER)
            lst = xn[:, 1400:1400 + 2 * MAX_OVER].rearrange("p (k i) -> p k i", k=2)
            link(v.tensor_tensor(big, const("rounds").unsqueeze(2).to_broadcast([P, MAX_OVER, E]),
                                 end.unsqueeze(1).to_broadcast([P, MAX_OVER, E]), ALU.is_ge))
            link(v.tensor_reduce(lst[:, 0, :], big, AX.X, ALU.add))
            link(v.tensor_tensor(big, big, nb.unsqueeze(1).to_broadcast([P, MAX_OVER, E]), ALU.mult))
            link(v.tensor_reduce(lst[:, 1, :], big, AX.X, ALU.add))
            link(v.tensor_tensor(lst[:, 1, :], const("rounds"), lst[:, 1, :], ALU.subtract))
            v.tensor_scalar(shift[:, :], lst[:, 1, :], 1.0, float(CAP), ALU.add, ALU.mult)
            v.tensor_scalar(over[0:1, 1:1 + MAX_OVER], lst[0:1, 0, :], float(E - 1), None, ALU.min)
            v.tensor_copy(over[0:1, 0:1], end[0:1, E - 1:E]).then_inc(S["overx"], 1)
            add_biases(0, 2).then_inc(S["bdd"], 1)
            add_biases(1, 4)
            lo("up", stream("up", 0), 0)
            add_biases(2, 2).then_inc(S["accrd"], 1)
            item_a(0, 0, first=True)
            item_b(0, 1)
            with dve.Fori(1, E // 2 - 1) as m:
                item_a(m, 2 * m)
                item_b(m, 2 * m + 1)
            item_a(E // 2 - 1, E - 2)
            item_b(E // 2 - 1, E - 1, last=True)
            for a in range(TILES):
                add(E // 2 - 1, a)
            n_over = dve.value_load(over[0:1, 0:1], min_val=0, max_val=MAX_OVER)
            with dve.If(n_over > 0):
                with dve.Fori(0, MAX_OVER) as i:
                    with dve.If(n_over > i):
                        n = i + E
                        expert = dve.value_load(over[0:1, bass.ds(i + 1, 1)], min_val=0, max_val=E - 1)
                        slot = small[:, 216:219]
                        v.tensor_scalar(slot, pos[:, :, bass.ds(expert, 1)].rearrange("p a o -> p (a o)"),
                                        shift[:, bass.ds(i, 1)], None, ALU.subtract).then_inc(olink, 1)
                        dve.wait_ge(olink, i + 1)
                        dve.wait_ge(S["pgt"], n)
                        place(slot.unsqueeze(2))
                        x_lo(i + E // 2, items=1)
                        for j in range(halves):
                            lo("gate", stream_over("gate", n), j)
                        gate_in(n, expert)
                        gate_mul(n)
                        for j in range(halves):
                            lo("up", stream_over("up", n), j)
                        up_in(n, expert)
                        h_lo(n)
                        for j in range(halves):
                            lo("down", stream_over("down", n), j)
                        for a in range(TILES):
                            add(i + E // 2, a)
            v.memset(small[:, 210:211], 0.0).then_inc(S["fss"], 1)
            dve.wait_ge(S["fss"], 2)
            v.tensor_scalar(small[:, 40:43], small[:, 40:43], 1.0 / D, EPS, ALU.mult, ALU.add).then_inc(S["frt"], 1)
            dve.wait_ge(S["frt"], 2)
            dve.wait_ge(S["fw_in"], 16)
            link(v.reciprocal(small[:, 52:55], small[:, 46:49]))
            for t in range(TILES):
                if t == 2:
                    dve.wait_ge(S["fout"], 32)
                v.scalar_tensor_tensor(out=outb[:, t % 2, :], in0=h[:, t, :], scalar=small[:, 52 + t:53 + t], in1=fw[:, :],
                                       op0=ALU.mult, op1=ALU.mult).then_inc(S["fo"], 1)


_INS = ['x_prompt', 'x_sample', 'mem_prompt', 'state_dn', 'state_dn_conv', 'state_sc_conv', 'cache_mem_k', 'cache_mem_v',
        'w_in', 'dn_conv_w', 'dn_A_log', 'dn_dt_bias', 'dn_norm_w', 'sc_conv_w', 'mem_norm_w', 'w_mem_kv', 'w_br', 'w_o',
        'norm1_w', 'norm2_w', 'w_router', 'b_router', 'w_gate', 'b_gate', 'w_up', 'b_up', 'w_down', 'b_down',
        'final_norm_w']
_OUTS = [(1, 256, 1024), (8, 16, 1024), (1, 1, 4, 128, 128), (1, 1, 3, 1536), (1, 1, 2, 256), (1, 1, 256, 4, 64),
         (1, 1, 256, 4, 64), (1, 8, 4, 128, 128), (1, 8, 3, 1536), (1, 8, 2, 256)]


def kernel(**inputs):
    import concourse.bacc as _bacc
    from concourse.bass_utils import run_bass_kernel_spmd as _run

    nc = _bacc.Bacc("TRN2", target_bir_lowering=False, num_devices=1)
    arrays, aps = {}, {}
    for name in _INS:
        a = np.ascontiguousarray(inputs[name])
        arrays[f"in_{name}_dram"] = a
        aps[name] = nc.dram_tensor(f"in_{name}_dram", a.shape, mybir.dt.from_np(a.dtype), kind="ExternalInput").ap()
    arrays["in_consts_dram"] = constant_table()
    aps["consts"] = nc.dram_tensor("in_consts_dram", (P, CONST_WIDTH), F32, kind="ExternalInput").ap()
    for i, shape in enumerate(_OUTS):
        aps[f"out_{i}"] = nc.dram_tensor(f"out_{i}_dram", shape, F32, kind="ExternalOutput").ap()
    build(nc, aps)
    r = _run(nc, [arrays], core_ids=[0])
    return tuple(r.results[0][f"out_{i}_dram"] for i in range(len(_OUTS)))
```
